# Optimizing a Trainium2 kernel written in Bass

```python
import math
import jax, jax.numpy as jnp
from jax import lax
import numpy as np

D_MODEL = 1024
BATCH = 1
SEQ = 256
DEPTH = 2

GRID_W = 64
HEAD_DIM = 64
ATTN_HEADS = 8
ATTN_KV_HEADS = 2
ATTN_WIDTH = ATTN_HEADS * HEAD_DIM
KV_WIDTH = ATTN_KV_HEADS * HEAD_DIM
HY_HEADS = 4
HY_WIDTH = HY_HEADS * HEAD_DIM
HY_ORDER = 2
FN_GROUPS = 4
FN_WIDTH = FN_GROUPS * HEAD_DIM
D_MIX = ATTN_WIDTH + HY_WIDTH + FN_WIDTH
HY_PROJ = (HY_ORDER + 1) * HY_WIDTH
IN_COLS = ATTN_WIDTH + 2 * KV_WIDTH + HY_PROJ + FN_WIDTH
Q_BLOCK = 128
ROPE_THETA = 10000.0
SHORT_CONV = 3
HY_BANDS = 8
HY_POS_FEATS = 1 + 2 * HY_BANDS
HY_FILTER_WIDTH = 64
HY_FILTERS = HY_ORDER * 2 * HY_WIDTH
HY_FAST_DECAY_PCT = 0.3
HY_SLOW_DECAY_PCT = 1.5
HY_DECAY_TARGET = 1e-2
PEER_KEYS = 128
PEER_EXPERTS = PEER_KEYS * PEER_KEYS
PEER_HEADS = 8
PEER_DK = 256
PEER_TOPK = 16
PEER_TOKEN_BLOCK = 128
EPS = 1e-6

kernel_name = 'hybrid_attn_hyena_fnet_peer_encoder'

def rmsnorm(x, g):
    xf = x.astype(jnp.float32)
    y = xf * lax.rsqrt(jnp.mean(xf * xf, axis=-1, keepdims=True) + EPS)
    return (y * g.astype(jnp.float32)).astype(x.dtype)

def axial_rope_tables(L):
    rows_n = L // GRID_W
    row = jnp.repeat(jnp.arange(rows_n), GRID_W).astype(jnp.float32)
    col = jnp.tile(jnp.arange(GRID_W), rows_n).astype(jnp.float32)
    n_freq = HEAD_DIM // 4
    inv = ROPE_THETA ** (-jnp.arange(n_freq, dtype=jnp.float32) / n_freq)
    ang = jnp.stack([row[:, None] * inv, col[:, None] * inv], axis=1)
    return jnp.cos(ang), jnp.sin(ang)

def apply_axial_rope(x, cos, sin):
    B, L, H, _ = x.shape
    xr = x.astype(jnp.float32).reshape(B, L, H, 2, 2, HEAD_DIM // 4)
    c = cos[None, :, None]
    s = sin[None, :, None]
    x1, x2 = xr[..., 0, :], xr[..., 1, :]
    out = jnp.stack([x1 * c - x2 * s, x2 * c + x1 * s], axis=-2)
    return out.reshape(B, L, H, HEAD_DIM).astype(x.dtype)

def attention_group(q, k, v, q_g, k_g, cos, sin):
    B, L, _ = q.shape
    rep = ATTN_HEADS // ATTN_KV_HEADS
    q = apply_axial_rope(rmsnorm(q.reshape(B, L, ATTN_HEADS, HEAD_DIM), q_g), cos, sin)
    k = apply_axial_rope(rmsnorm(k.reshape(B, L, ATTN_KV_HEADS, HEAD_DIM), k_g), cos, sin)
    v = v.reshape(B, L, ATTN_KV_HEADS, HEAD_DIM)
    n_blk = L // Q_BLOCK
    qb = q.reshape(B, n_blk, Q_BLOCK, ATTN_KV_HEADS, rep, HEAD_DIM).transpose(1, 0, 2, 3, 4, 5)
    scale = HEAD_DIM ** -0.5

    def block(qi):
        s = jnp.einsum('bqgrd,bkgd->bgrqk', qi, k).astype(jnp.float32) * scale
        p = jax.nn.softmax(s, axis=-1).astype(v.dtype)
        return jnp.einsum('bgrqk,bkgd->bqgrd', p, v)

    out = lax.map(block, qb)
    return out.transpose(1, 0, 2, 3, 4, 5).reshape(B, L, ATTN_WIDTH)

def short_conv(u, w, b):
    L = u.shape[1]
    pad = SHORT_CONV // 2
    up = jnp.pad(u, ((0, 0), (pad, pad), (0, 0)))
    y = b
    for j in range(SHORT_CONV):
        y = y + up[:, j:j + L] * w[j]
    return y

def hyena_filter_spectra(L, w1, b1, f1, w2, b2, f2, w3):
    t = jnp.linspace(0.0, 1.0, L, dtype=jnp.float32)[:, None]
    bands = jnp.arange(1, HY_BANDS + 1, dtype=jnp.float32)
    ang = 2.0 * math.pi * t * bands
    z = jnp.concatenate([t, jnp.sin(ang), jnp.cos(ang)], axis=-1)
    h = jnp.sin(f1 * (z @ w1.astype(jnp.float32) + b1))
    h = jnp.sin(f2 * (h @ w2.astype(jnp.float32) + b2))
    h = (h @ w3.astype(jnp.float32)).reshape(L, HY_ORDER, 2, HY_WIDTH)
    rates = jnp.linspace(-math.log(HY_DECAY_TARGET) / HY_SLOW_DECAY_PCT,
                         -math.log(HY_DECAY_TARGET) / HY_FAST_DECAY_PCT, HY_WIDTH, dtype=jnp.float32)
    h = h * jnp.exp(-t[:, :, None, None] * rates)
    h = h * lax.rsqrt(jnp.sum(h * h, axis=(0, 2), keepdims=True) + EPS)
    fwd, bwd = h[:, :, 0], h[:, :, 1]
    k_full = jnp.concatenate([fwd, jnp.zeros_like(fwd[:1]), bwd[1:][::-1]], axis=0)
    return jnp.fft.rfft(k_full, n=2 * L, axis=0)

def long_conv(u, kf, bias):
    L = u.shape[1]
    uf = jnp.fft.rfft(u, n=2 * L, axis=1)
    y = jnp.fft.irfft(uf * kf[None], n=2 * L, axis=1)[:, :L]
    return y + u * bias

def hyena_group(proj, conv_w, conv_b, kf, bias):
    u = short_conv(proj, conv_w, conv_b).astype(jnp.float32)
    v, x1, x2 = jnp.split(u, HY_ORDER + 1, axis=-1)
    z = v
    for n, gate in enumerate((x1, x2)):
        z = gate * long_conv(z, kf[:, n], bias[n].astype(jnp.float32))
    return z

def fourier_group(u, w, b):
    B, L, _ = u.shape
    ug = u.astype(jnp.float32).reshape(B, L, FN_GROUPS, HEAD_DIM)
    f = jnp.fft.fft2(ug, axes=(1, 3), norm='ortho').real
    y = jnp.einsum('blgd,gde->blge', f, w.astype(jnp.float32)).reshape(B, L, FN_WIDTH)
    return y + b.astype(jnp.float32)

def peer(x, w_query, sub_keys, u_tab, v_tab):
    B, L, D = x.shape
    T = B * L
    xt = x.reshape(T, D)
    q = (xt @ w_query).reshape(T, PEER_HEADS, 2, PEER_DK // 2)
    s = jnp.einsum('thpd,phkd->thpk', q, sub_keys).astype(jnp.float32)
    s_top, i_top = lax.top_k(s, PEER_TOPK)
    cand = (s_top[:, :, 0, :, None] + s_top[:, :, 1, None, :]).reshape(T, PEER_HEADS, PEER_TOPK * PEER_TOPK)
    cand_idx = (i_top[:, :, 0, :, None] * PEER_KEYS + i_top[:, :, 1, None, :]).reshape(T, PEER_HEADS, PEER_TOPK * PEER_TOPK)
    best, pos = lax.top_k(cand, PEER_TOPK)
    idx = jnp.take_along_axis(cand_idx, pos, axis=-1)
    g = jax.nn.softmax(best, axis=-1)
    n_blk = T // PEER_TOKEN_BLOCK

    def block(args):
        xb, ib, gb = args
        ue = jnp.take(u_tab, ib, axis=0)
        a = jax.nn.gelu(jnp.einsum('thkd,td->thk', ue, xb).astype(jnp.float32), approximate=False)
        ve = jnp.take(v_tab, ib, axis=0)
        return jnp.einsum('thk,thkd->td', (gb * a).astype(ve.dtype), ve)

    out = lax.map(block, (xt.reshape(n_blk, PEER_TOKEN_BLOCK, D),
                          idx.reshape(n_blk, PEER_TOKEN_BLOCK, PEER_HEADS, PEER_TOPK),
                          g.reshape(n_blk, PEER_TOKEN_BLOCK, PEER_HEADS, PEER_TOPK)))
    return out.reshape(B, L, D).astype(x.dtype)

def setup_inputs(seed: int = 0) -> dict:
    key = jax.random.key(seed)
    ks = jax.random.split(key, 32)

    def nrm(k, shape, scale):
        return jax.random.normal(k, shape, jnp.float32) * scale

    def gain(k, shape):
        return 1.0 + 0.02 * jax.random.normal(k, shape, jnp.float32)

    return {
        'x': nrm(ks[0], (BATCH, SEQ, D_MODEL), 1.0),
        'norm1_g': gain(ks[1], (DEPTH, D_MODEL)),
        'w_in': nrm(ks[2], (DEPTH, D_MODEL, IN_COLS), D_MODEL ** -0.5),
        'q_norm_g': gain(ks[3], (DEPTH, HEAD_DIM)),
        'k_norm_g': gain(ks[4], (DEPTH, HEAD_DIM)),
        'hy_conv_w': nrm(ks[5], (DEPTH, SHORT_CONV, HY_PROJ), SHORT_CONV ** -0.5),
        'hy_conv_b': nrm(ks[6], (DEPTH, HY_PROJ), 0.02),
        'hy_w1': nrm(ks[7], (DEPTH, HY_POS_FEATS, HY_FILTER_WIDTH), HY_POS_FEATS ** -0.5),
        'hy_b1': nrm(ks[8], (DEPTH, HY_FILTER_WIDTH), 0.02),
        'hy_freq1': gain(ks[9], (DEPTH, HY_FILTER_WIDTH)),
        'hy_w2': nrm(ks[10], (DEPTH, HY_FILTER_WIDTH, HY_FILTER_WIDTH), HY_FILTER_WIDTH ** -0.5),
        'hy_b2': nrm(ks[11], (DEPTH, HY_FILTER_WIDTH), 0.02),
        'hy_freq2': gain(ks[12], (DEPTH, HY_FILTER_WIDTH)),
        'hy_w3': nrm(ks[13], (DEPTH, HY_FILTER_WIDTH, HY_FILTERS), HY_FILTER_WIDTH ** -0.5),
        'hy_bias': nrm(ks[14], (DEPTH, HY_ORDER, HY_WIDTH), 0.1),
        'fn_w': nrm(ks[15], (DEPTH, FN_GROUPS, HEAD_DIM, HEAD_DIM), HEAD_DIM ** -0.5),
        'fn_b': nrm(ks[16], (DEPTH, FN_WIDTH), 0.02),
        'mix_norm_g': gain(ks[17], (DEPTH, D_MIX)),
        'w_out': nrm(ks[18], (DEPTH, D_MIX, D_MODEL), D_MIX ** -0.5),
        'norm2_g': gain(ks[19], (DEPTH, D_MODEL)),
        'peer_w_query': nrm(ks[20], (DEPTH, D_MODEL, PEER_HEADS * PEER_DK), D_MODEL ** -0.5),
        'peer_sub_keys': nrm(ks[21], (DEPTH, 2, PEER_HEADS, PEER_KEYS, PEER_DK // 2), (PEER_DK // 2) ** -0.5),
        'peer_u': nrm(ks[22], (DEPTH, PEER_EXPERTS, D_MODEL), D_MODEL ** -0.5),
        'peer_v': nrm(ks[23], (DEPTH, PEER_EXPERTS, D_MODEL), PEER_HEADS ** -0.5),
        'final_g': gain(ks[24], (D_MODEL,)),
    }

def reference(x, norm1_g, w_in, q_norm_g, k_norm_g, hy_conv_w, hy_conv_b, hy_w1, hy_b1, hy_freq1,
              hy_w2, hy_b2, hy_freq2, hy_w3, hy_bias, fn_w, fn_b, mix_norm_g, w_out, norm2_g,
              peer_w_query, peer_sub_keys, peer_u, peer_v, final_g):
    L = x.shape[1]
    cos, sin = axial_rope_tables(L)
    o_k = ATTN_WIDTH
    o_v = o_k + KV_WIDTH
    o_h = o_v + KV_WIDTH
    o_f = o_h + HY_PROJ
    for l in range(DEPTH):
        h = rmsnorm(x, norm1_g[l])
        p = h @ w_in[l]
        a = attention_group(p[..., :o_k], p[..., o_k:o_v], p[..., o_v:o_h],
                            q_norm_g[l], k_norm_g[l], cos, sin)
        kf = hyena_filter_spectra(L, hy_w1[l], hy_b1[l], hy_freq1[l], hy_w2[l], hy_b2[l],
                                  hy_freq2[l], hy_w3[l])
        y = hyena_group(p[..., o_h:o_f], hy_conv_w[l], hy_conv_b[l], kf, hy_bias[l])
        f = fourier_group(p[..., o_f:], fn_w[l], fn_b[l])
        g = mix_norm_g[l]
        mixed = jnp.concatenate([
            rmsnorm(a, g[:ATTN_WIDTH]),
            rmsnorm(y.astype(x.dtype), g[ATTN_WIDTH:ATTN_WIDTH + HY_WIDTH]),
            rmsnorm(f.astype(x.dtype), g[ATTN_WIDTH + HY_WIDTH:]),
        ], axis=-1)
        x = x + mixed @ w_out[l]
        x = x + peer(rmsnorm(x, norm2_g[l]), peer_w_query[l], peer_sub_keys[l], peer_u[l], peer_v[l])
    return rmsnorm(x, final_g)


_drawn_inputs = setup_inputs


def setup_inputs(seed=0):
    import zlib

    import numpy as np

    out = dict(_drawn_inputs(seed))
    spreads = {}
    factors = {'hy_freq2': 2.676, 'final_g': 2.815}
    for name, (base, spread) in spreads.items():
        noise = np.random.default_rng([zlib.crc32(name.encode()), seed]).standard_normal(out[name].shape)
        drawn = base * np.exp(spread * noise) if base else spread * noise
        out[name] = __import__('jax').numpy.asarray(drawn.astype(out[name].dtype))
    for name, factor in factors.items():
        out[name] = (out[name] * factor).astype(out[name].dtype)
    return out
```

```python
from contextlib import ExitStack

import concourse.bass as bass
from concourse import mybir

ALU = mybir.AluOpType
ACT = mybir.ActivationFunctionType
AX = mybir.AxisListType
F32 = mybir.dt.float32
F32R = mybir.dt.float32r
U32 = mybir.dt.uint32

P = 128
DEPTH = 2
SEQ = 256
D = 1024
TB = SEQ // P
DT = D // P
HEAD = 64
HEADS, KV_HEADS = 8, 2
A_W, KV_W, HY_W, FN_W = 512, 128, 256, 256
QKV = A_W + 2 * KV_W
CT = (3 * HY_W + FN_W) // P
IN_COLS = QKV + CT * P
PH, KEYS, TOPK = 8, 128, 16
HP = 2 * PH
PICKS = PH * TOPK
EPS = 1e-6
NEG = -3.0e38

INV_2PI = 0.15915494309189535
ROUND = 12582912.0
TWO_PI = (6.28125, 0.0019350051879882812, 3.019916050561733e-07)
SIN_MAX = 3.1415925

PV = {"g1": 0, "g2": 8, "gm": 16, "cw": 24, "cb": 42, "hb": 48, "fb": 52, "b1": 54, "f1": 55, "b2": 56, "f2": 57}
PV_N = 58
PM = {"w1": 0, "w2": 64, "w3": 128, "fw": 1152}
PM_N = 1408
KC = {"ident": 0, "iota": 128, "ones": 256, "cos": 384, "sin": 512, "neg_half": 640, "not_first": 641, "iota16": 642}
KC_N = 658
CF = {"z": 0, "decay": 256, "sin0": 768, "cosn": 1280, "bc": 1536, "bs": 1664}
CF_N = 1792
CD = {"cos": 0, "sin": 512, "icos": 1024, "isin": 1536, "fc": 2048, "fs": 2560}
CD_N = 3072

W_IN = 0
W_OUT = 0
W_Q, W_Q_SLOTS, W_Q_N = 8192, 3, 2048
H_T = 14336
CONV = 14336
SPEC = 16384
SUBKEYS = 16384
FILTER_C = 18944
FILTER_M = 20736
P_QKV = 18944
P_T = 20480
FN_U = 22028
FN_P = 20480
QUERY_T = 18944
MIXED = 22544
GAIN_QK = 22544
SINE = 23568
DFT = 24592
SCR = 27664
CAND = 24576
EQ = 26624
SCORES = 28672
GUARD = 96


class Signal:

    def __init__(self, sem, per_layer):
        self.sem, self.per_layer = sem, per_layer


def at(signal, layer, count):
    return signal.sem, layer * signal.per_layer + count


DVE_STEPS = 73


def hybrid_encoder(nc, x_in, w_in, w_out, w_query, sub_keys, tab_u, tab_v, pvec, pmat, gain_qk, kconst, cfilter,
                   cdft, final_g, out):
    with ExitStack() as ctx:
        def sb(name, shape, dt=F32):
            return ctx.enter_context(nc.sbuf_tensor(name, shape, dt))

        def sig(name, per_layer):
            return Signal(ctx.enter_context(nc.semaphore(name)), per_layer)

        work = sb("work", [P, P, SEQ])
        x = sb("x", [P, TB, D])
        x_hi = sb("x_hi", [P, DT, SEQ], F32R)
        x_lo = sb("x_lo", [P, DT, SEQ], F32R)
        raw = sb("raw", [P, 4, D])
        tab_hi = sb("tab_hi", [P, 2, D], F32R)
        tab_lo = sb("tab_lo", [P, 2, D], F32R)
        w_hi = sb("w_hi", [P, 2, SEQ], F32R)
        w_lo = sb("w_lo", [P, 2, SEQ], F32R)
        picks = sb("picks", [P, 3, SEQ])
        onehot = sb("onehot", [P, 2, 2, 4, P])
        kc = sb("kc", [P, KC_N])
        pv = sb("pv", [P, PV_N])
        chosen = sb("chosen", [P, 3, TB, PICKS])
        small = sb("small", [P, 128])
        ps = ctx.enter_context(nc.psum_tensor("ps", [P, 8, 512], F32))

        workf = work[:, :, :].rearrange("p j t -> p (j t)")
        rawf = raw[:, :, :].rearrange("p s d -> p (s d)")
        onef = onehot[:, :, :, :, :].rearrange("p s a t c -> p (s a t c)")

        def area(start, n):
            return workf[:, start:start + n]

        ident = kc[:, KC["ident"]:KC["ident"] + P]
        iota = kc[:, KC["iota"]:KC["iota"] + P]
        ones = kc[:, KC["ones"]:KC["ones"] + P]
        cos_r = kc[:, KC["cos"]:KC["cos"] + TB * HEAD].rearrange("p (b d) -> p b d", b=TB)
        sin_r = kc[:, KC["sin"]:KC["sin"] + TB * HEAD].rearrange("p (b d) -> p b d", b=TB)
        neg_half = kc[:, KC["neg_half"]:KC["neg_half"] + 1]
        iota16 = kc[:, KC["iota16"]:KC["iota16"] + TOPK]

        def par(name, i=0, rows=P):
            return pv[0:rows, PV[name] + i:PV[name] + i + 1]

        ss = small[:, 0:2]
        rinv = small[:, 2:4]
        ss20 = small[:, 4:24]
        r20 = small[:, 24:44]
        mx = small[:, 44:52]
        nmx = small[:, 52:60]
        rs = small[:, 60:68]
        rrs = small[:, 68:76]
        ms6 = small[:, 76:82]
        r6 = small[:, 82:88]
        ssg = small[:, 88:104]
        ms = small[:, 104:106]
        ms20 = small[:, 106:126]

        fc = area(FILTER_C, CF_N)
        fm = area(FILTER_M, PM_N)
        arg = workf[0:64, SINE:SINE + 256]
        turns = workf[0:64, SINE + 256:SINE + 512]
        f_h1 = workf[0:64, SINE + 512:SINE + 768]
        f_h2 = workf[0:64, SINE + 768:SINE + 1024]
        filt = area(SCR, 2048).rearrange("p (b o e c) -> p b o e c", b=TB, o=2, e=2)
        filt_sq = onef[:, 0:2048].rearrange("p (b o e c) -> p b o e c", b=TB, o=2, e=2)
        f_sum = area(SCR + 2048, 1024).rearrange("p (b o c) -> p b o c", b=TB, o=2)
        f_dif = area(SCR + 3072, 1024).rearrange("p (b o c) -> p b o c", b=TB, o=2)
        f_rn = area(SCR + 4096, 512)
        decay = fc[:, CF["decay"]:CF["decay"] + 512].rearrange("p (b c) -> p b c", b=TB)
        sin0 = fc[:, CF["sin0"]:CF["sin0"] + 512].rearrange("p (b f) -> p b f", b=TB)
        cosn = fc[:, CF["cosn"]:CF["cosn"] + 256].rearrange("p (b f) -> p b f", b=TB)
        spec = area(SPEC, 2560).rearrange("p (k o c) -> p k o c", k=5, o=2)
        dft = area(DFT, CD_N)

        def mat(name):
            return dft[:, CD[name]:CD[name] + 512].rearrange("p (b f) -> p b f", b=TB)

        xn = rawf[:, 0:2048].rearrange("p (b d) -> p b d", b=TB)
        h_t = area(H_T, 2048).rearrange("p (k t) -> p k t", k=DT)
        win = area(W_IN, DT * IN_COLS).rearrange("p (k n) -> p k n", k=DT)
        p_qkv = area(P_QKV, TB * QKV).rearrange("p (b n) -> p b n", b=TB)
        p_t = area(P_T, 6 * 258).rearrange("p (k t) -> p k t", k=6)
        fn_u = area(FN_U, 512).rearrange("p (k t) -> p k t", k=2)
        fn_m = rawf[:, 3584:4096].rearrange("p (m q c) -> p m q c", m=2, q=2)
        conv = area(CONV, 1536).rearrange("p (k t) -> p k t", k=6)
        tap1 = rawf[:, 0:1536].rearrange("p (k t) -> p k t", k=6)
        tap2 = rawf[:, 1536:3072].rearrange("p (k t) -> p k t", k=6)
        z_t = rawf[:, 3072:3584].rearrange("p (b c) -> p b c", b=TB)
        prod = rawf[:, 0:2048].rearrange("p (m k c) -> p m k c", m=4, k=2)
        y_spec = rawf[:, 2048:3072].rearrange("p (m k c) -> p m k c", m=2, k=2)
        qn = area(SCR, 1280)
        rope = area(SCR + 1280, 1280)
        k_twice = area(SCR, 512).rearrange("p (b g e d) -> p b g e d", b=TB, g=2, e=2)
        rot = onef[:, 0:1280]
        gqk = area(GAIN_QK, 640)
        q_t = area(SCR + 3568, 1024).rearrange("p (k t) -> p k t", k=4)
        k_t = area(SCR + 4592, 512).rearrange("p (k t) -> p k t", k=2)
        probs = area(SCR, 2048).rearrange("p (s k) -> p s k", s=HEADS)
        probs_t = onef[:, 0:2048].rearrange("p (b s q) -> p b s q", b=TB, s=HEADS)
        fn_p = area(FN_P, 1024).rearrange("p (b q m c) -> p b q m c", b=TB, q=2, m=2)
        mixed = area(MIXED, 2048).rearrange("p (k t) -> p k t", k=8)
        mixed_sq = area(SCR, 2048).rearrange("p (k t) -> p k t", k=8)
        wout = area(W_OUT, DT * D).rearrange("p (k n) -> p k n", k=DT)
        h2_t = area(SCR, 2048).rearrange("p (k t) -> p k t", k=DT)
        query_t = area(QUERY_T, HP * SEQ).rearrange("p (k t) -> p k t", k=HP)
        subk = area(SUBKEYS, HP * KEYS).rearrange("p (k n) -> p k n", k=HP)
        scores = area(SCORES, TB * HP * KEYS).rearrange("p (b k n) -> p b k n", b=TB, k=HP)
        cand = area(CAND, PH * TOPK * TOPK).rearrange("p (h a b) -> p h a b", h=PH, a=TOPK)
        eq = area(EQ, PICKS * TOPK).rearrange("p (n r) -> p n r", r=TOPK)
        v_top = onef[:, 0:512].rearrange("p (b k n) -> p b k n", b=TB, k=HP)
        i_top = onef[:, 512:1024].bitcast(U32).rearrange("p (b k n) -> p b k n", b=TB, k=HP)
        i_topf = onef[:, 1024:1536].rearrange("p (b k n) -> p b k n", b=TB, k=HP)
        best = onef[:, 1536:1792].rearrange("p (b h n) -> p b h n", b=TB, h=PH)
        pos = onef[:, 1792:2048].bitcast(U32).rearrange("p (b n) -> p b n", b=TB)
        place_u = onef[:, 0:256].bitcast(U32).rearrange("p (s n) -> p s n", s=2)
        place_f = onef[:, 256:512].rearrange("p (s n) -> p s n", s=2)

        const_in = sig("const_in", 0)
        x_landed = sig("x_landed", 0)
        params_in = sig("params_in", 64)
        dft_in = sig("dft_in", 16)
        gqk_in = sig("gqk_in", 16)
        w_in_in = [sig(f"w_in_in{k}", 16) for k in range(DT)]
        w_out_in = sig("w_out_in", 16)
        w_q_in = [sig(f"w_q_in{s}", 16 * len(range(s, DT, W_Q_SLOTS))) for s in range(W_Q_SLOTS)]
        subk_in = sig("subk_in", 16)
        raw_in = [sig(f"raw_in{s}", 16 * 64) for s in range(4)]
        dve_step = sig("dve_step", DVE_STEPS)
        pool_step = sig("pool_step", 1)
        mlp_ready = sig("mlp_ready", 2)
        sine_arg = sig("sine_arg", 2)
        sine_done = sig("sine_done", 2)
        taps_ready = sig("taps_ready", TB)
        filt_done = sig("filt_done", TB)
        filt_sq_done = sig("filt_sq_done", 1)
        sumdif_done = sig("sumdif_done", 1)
        f_norm_ready = sig("f_norm_ready", 1)
        f_root_done = sig("f_root_done", 1)
        spec_ready = sig("spec_ready", 5)
        spec_done = sig("spec_done", 5)
        sq_sum = sig("sq_sum", 4)
        mean_sq = sig("mean_sq", 4)
        inv_root = sig("inv_root", 4)
        xn_done = sig("xn_done", 2 * TB)
        xT_ready = sig("xT_ready", 8)
        hT_act = sig("hT_act", 8)
        hT_dve = sig("hT_dve", 8)
        fn_m_ready = sig("fn_m_ready", 1)
        fn_m_done = sig("fn_m_done", 1)
        proj_ready = sig("proj_ready", 8)
        pT_done = sig("pT_done", 4)
        qkv_done = sig("qkv_done", 4)
        pad_done = sig("pad_done", 1)
        conv_taps = sig("conv_taps", 1)
        conv_done = sig("conv_done", 1)
        zT_ready = sig("zT_ready", 2)
        zT_done = sig("zT_done", 2)
        u_spec_ready = sig("u_spec_ready", 2)
        y_spec_done = sig("y_spec_done", 2)
        y_ready = sig("y_ready", 2)
        hyena_done = sig("hyena_done", 2)
        fn1_ready = sig("fn1_ready", 2)
        fn1_done = sig("fn1_done", 2)
        fn2_ready = sig("fn2_ready", 1)
        fn2_done = sig("fn2_done", 1)
        rope_done = sig("rope_done", 1)
        qkT_ready = sig("qkT_ready", 3)
        qkT_done = sig("qkT_done", 3)
        att_ready = sig("att_ready", TB)
        max_done = sig("max_done", TB)
        exp_done = sig("exp_done", TB)
        probs_done = sig("probs_done", TB)
        pTr_ready = sig("pTr_ready", TB)
        pTr_act = sig("pTr_act", TB)
        pTr_dve = sig("pTr_dve", TB)
        attn_ready = sig("attn_ready", TB)
        attn_done = sig("attn_done", TB)
        mixed_sq_done = sig("mixed_sq_done", 1)
        mixed_done = sig("mixed_done", 1)
        group_ready = sig("group_ready", 1)
        out_ready = sig("out_ready", 6)
        out_added = sig("out_added", 6)
        x_split = sig("x_split", 1)
        w_q_used = sig("w_q_used", DT - 1)
        query_ready = sig("query_ready", 8)
        query_act = sig("query_act", 4)
        query_dve = sig("query_dve", 4)
        scores_ready = sig("scores_ready", 8)
        scores_act = sig("scores_act", 4)
        scores_dve = sig("scores_dve", 4)
        best_done = sig("best_done", 1)
        gate_exp = sig("gate_exp", 1)
        topk_done = sig("topk_done", 1)
        picksT_ready = sig("picksT_ready", 1)
        picksT_done = sig("picksT_done", 1)
        hi_done = sig("hi_done", 256)
        lo_done = sig("lo_done", 256)
        tile_used = sig("tile_used", 256)
        gelu_done = sig("gelu_done", 64)
        hot_i = sig("hot_i", 64)
        hot_j = sig("hot_j", 64)
        hot_g = sig("hot_g", 64)
        gates_ready = sig("gates_ready", 64)
        weighted = sig("weighted", 64)
        whi_done = sig("whi_done", 128)
        wlo_done = sig("wlo_done", 128)
        layer_done = sig("layer_done", 1)
        fin = sig("fin", 0)
        fg_in = sig("fg_in", 0)
        out_written = sig("out_written", 0)

        block = ctx.enter_context(nc.Block())

        def settled(eng):
            eng.drain()

        @block.sync
        def _(sp):
            sp.dma_start(kc[:, :], kconst[:, :]).then_inc(const_in.sem, 16)
            sp.dma_start(x[:, :, :], x_in.rearrange("(b p) d -> p b d", p=P)).then_inc(x_landed.sem, 16)
            with sp.Fori(0, DEPTH) as l:
                sp.wait_ge(layer_done.sem, l + 1)
                sp.dma_start(pv[:, :], pvec[l, :, :]).then_inc(params_in.sem, 16)
                sp.dma_start(fc, cfilter[:, :]).then_inc(params_in.sem, 16)
                sp.dma_start(fm[:, 0:704], pmat[l, :, 0:704]).then_inc(params_in.sem, 16)
                sp.dma_start(fm[:, 704:1408], pmat[l, :, 704:1408]).then_inc(params_in.sem, 16)
                sp.dma_start(dft, cdft[:, :]).then_inc(dft_in.sem, 16)
                for k in range(DT):
                    sp.dma_start(win[:, k, :], w_in[l, k * P:(k + 1) * P, :]).then_inc(w_in_in[k].sem, 16)
                sp.dma_start(gqk, gain_qk[l, :, :]).then_inc(gqk_in.sem, 16)
                sp.wait_ge(*at(proj_ready, l, 8))
                sp.dma_start(wout, w_out[l, :, :].rearrange("(k p) n -> p k n", p=P)).then_inc(w_out_in.sem, 16)
                for k in range(W_Q_SLOTS):
                    sp.dma_start(area(W_Q + k * W_Q_N, W_Q_N), w_query[l, k * P:(k + 1) * P, :]).then_inc(w_q_in[k].sem, 16)
                sp.wait_ge(*at(hyena_done, l, 2))
                sp.dma_start(subk, sub_keys[l, :, :]).then_inc(subk_in.sem, 16)
                for s in range(4):
                    sp.wait_ge(*at(xT_ready, l, 8))
                    sp.dma_start(raw[:, s, :], tab_u[l, s, :, :]).then_inc(raw_in[s].sem, 16)
                for k in range(W_Q_SLOTS, DT):
                    sp.wait_ge(*at(w_q_used, l, k - W_Q_SLOTS + 1))
                    sp.dma_start(area(W_Q + (k % W_Q_SLOTS) * W_Q_N, W_Q_N),
                                 w_query[l, k * P:(k + 1) * P, :]).then_inc(w_q_in[k % W_Q_SLOTS].sem, 16)

                def stream(table, i, first):
                    for s in range(4):
                        sp.wait_ge(*at(hi_done, l, i * 4 + first + s - 3))
                        sp.wait_ge(*at(lo_done, l, i * 4 + first + s - 3))
                        sp.dma_start(raw[:, s, :], table[l, i * 4 + s, :, :]).then_inc(raw_in[s].sem, 16)

                with sp.Fori(1, 32) as i:
                    stream(tab_u, i, 0)
                with sp.Fori(0, 32) as i:
                    stream(tab_v, i, 128)
            sp.wait_ge(layer_done.sem, DEPTH + 1)
            sp.dma_start(area(0, D), final_g[:, :]).then_inc(fg_in.sem, 16)
            sp.wait_ge(fin.sem, 1)
            sp.dma_start(out.rearrange("(b p) d -> p b d", p=P), xn).then_inc(out_written.sem, 16)
            sp.wait_ge(out_written.sem, 16)

        @block.tensor
        def _(pe):
            mm, tr = nc.tensor.matmul, nc.tensor.transpose
            pe.wait_ge(const_in.sem, 16)
            with pe.Fori(0, DEPTH) as l:
                pe.wait_ge(*at(params_in, l, 64))
                pe.wait_ge(layer_done.sem, l + 1)
                mm(ps[0:64, 0, 0:256], fm[0:17, PM["w1"]:PM["w1"] + 64], fc[0:17, CF["z"]:CF["z"] + 256],
                   start=True, stop=True).then_inc(mlp_ready.sem, 1)
                pe.wait_ge(*at(sine_done, l, 1))
                mm(ps[:, 1, 0:256], fm[0:64, PM["w2"]:PM["w2"] + P], f_h1,
                   start=True, stop=True).then_inc(mlp_ready.sem, 1)
                pe.wait_ge(*at(sine_done, l, 2))
                for b in range(TB):
                    for n in range(2):
                        last = mm(ps[:, 2 + 2 * b + n, :], f_h2[:, b * P:(b + 1) * P],
                                  fm[0:64, PM["w3"] + n * 512:PM["w3"] + (n + 1) * 512], start=True, stop=True)
                    last.then_inc(taps_ready.sem, 1)
                pe.wait_ge(*at(filt_sq_done, l, 1))
                for b in range(TB):
                    for e in range(2):
                        last = mm(ps[:, 6, :], ones, filt_sq[:, b, :, e, :], start=(b + e == 0), stop=(b + e == 2))
                last.then_inc(f_norm_ready.sem, 1)
                pe.wait_ge(*at(sumdif_done, l, 1))
                pe.wait_ge(*at(dft_in, l, 16))
                for n, (m, c, src) in enumerate(((mat("cos"), 0, f_sum), (mat("cos"), P, f_sum), (sin0, 0, f_dif),
                                                 (sin0, P, f_dif), (cosn, 0, f_sum))):
                    for b in range(TB):
                        last = mm(ps[:, n, :], m[:, b, c:c + P], src[:, b, :, :], start=(b == 0), stop=(b == 1))
                    last.then_inc(spec_ready.sem, 1)
                pe.wait_ge(*at(spec_done, l, 1))
                for n, name in enumerate(("bc", "bs")):
                    last = mm(ps[:, 0, n * 256:(n + 1) * 256], fc[:, CF[name]:CF[name] + P],
                              fm[:, PM["fw"]:PM["fw"] + 256], start=True, stop=True)
                last.then_inc(fn_m_ready.sem, 1)
                pe.wait_ge(*at(spec_done, l, 5))

                def transpose_x(banks, done):
                    pe.wait_ge(*at(xn_done, l, done))
                    for k in range(DT):
                        for b in range(TB):
                            last = tr(ps[:, banks[k // 2], (k % 2) * 256 + b * P:(k % 2) * 256 + (b + 1) * P],
                                      xn[:, b, k * P:(k + 1) * P], ident)
                        if k % 2:
                            last.then_inc(xT_ready.sem, 1)

                transpose_x((4, 5, 6, 7), 2)
                pe.wait_ge(*at(hT_act, l, 4))
                pe.wait_ge(*at(hT_dve, l, 4))
                pe.wait_ge(*at(fn_m_done, l, 1))
                for k in range(DT):
                    pe.wait_ge(*at(w_in_in[k], l, 16))
                    for c in range(CT):
                        col = QKV + c * P
                        last = mm(ps[:, c // 2, (c % 2) * 256:(c % 2) * 256 + 256], win[:, k, col:col + P],
                                  h_t[:, k, :], start=(k == 0 and c % 2 == 0), stop=(k == DT - 1),
                                  skip_group_check=True)
                        if k == DT - 1 and c % 2:
                            last.then_inc(proj_ready.sem, 1)
                    for b in range(TB):
                        for n in range(2):
                            last = mm(ps[:, 4 + 2 * b + n, 0:384], h_t[:, k, b * P:(b + 1) * P],
                                      win[:, k, n * 384:(n + 1) * 384], start=(k == 0), stop=(k == DT - 1))
                            if k == DT - 1:
                                last.then_inc(proj_ready.sem, 1)

                def hyena_forward(o, bank):
                    if o == 0:
                        pe.wait_ge(*at(conv_done, l, 1))
                        pe.wait_ge(*at(pT_done, l, 4))
                    else:
                        pe.wait_ge(*at(hyena_done, l, 1))
                        pe.wait_ge(*at(fn2_done, l, 1))
                    for b in range(TB):
                        for c in range(2):
                            last = tr(ps[:, bank, b * 256 + c * P:b * 256 + (c + 1) * P],
                                      conv[:, c, b * P:(b + 1) * P], ident)
                    last.then_inc(zT_ready.sem, 1)
                    pe.wait_ge(*at(zT_done, l, o + 1))
                    if o:
                        pe.wait_ge(*at(y_spec_done, l, 1))
                    for n, name in enumerate(("cos", "sin")):
                        for f in range(2):
                            for b in range(TB):
                                last = mm(ps[:, 1 + n, f * 256:(f + 1) * 256], mat(name)[:, b, f * P:(f + 1) * P],
                                          z_t[:, b, :], start=(b == 0), stop=(b == 1))
                    last.then_inc(u_spec_ready.sem, 1)

                def hyena_inverse(o):
                    pe.wait_ge(*at(y_spec_done, l, o + 1))
                    if o:
                        pe.wait_ge(*at(hyena_done, l, 1))
                    for c in range(2):
                        for n, name in enumerate(("icos", "isin")):
                            for f in range(2):
                                last = mm(ps[:, 0, c * 256:(c + 1) * 256], y_spec[:, n, f, c * P:(c + 1) * P],
                                          mat(name)[:, f, :], start=(n + f == 0), stop=(n + f == 2))
                    last.then_inc(y_ready.sem, 1)

                hyena_forward(0, 0)
                pe.wait_ge(*at(qkv_done, l, 4))
                for b in range(TB):
                    for q in range(2):
                        last = mm(ps[:, (3, 7)[b], q * 256:(q + 1) * 256], fn_u[:, q, b * P:(b + 1) * P],
                                  fn_m[:, :, q, :], start=True, stop=True)
                    last.then_inc(fn1_ready.sem, 1)
                pe.wait_ge(*at(fn1_done, l, 2))
                for q in range(2):
                    for b in range(TB):
                        for n, name in enumerate(("fc", "fs")):
                            last = mm(ps[:, 3, q * 256:(q + 1) * 256], fn_p[:, b, q, n, :], mat(name)[:, b, :],
                                      start=(b + n == 0), stop=(b + n == 2))
                last.then_inc(fn2_ready.sem, 1)
                pe.wait_ge(*at(rope_done, l, 1))
                rope4 = rope.rearrange("p (b h d) -> p b h d", b=TB, h=10)
                for g in range(3):
                    for k in range(2):
                        for b in range(TB):
                            if g < 2:
                                src = rope4[:, b, 4 * g + 2 * k:4 * g + 2 * k + 2, :].rearrange("p h d -> p (h d)")
                            else:
                                src = k_twice[:, b, k, :, :].rearrange("p e d -> p (e d)")
                            last = tr(ps[:, 4 + g, k * 256 + b * P:k * 256 + (b + 1) * P], src, ident)
                    last.then_inc(qkT_ready.sem, 1)
                hyena_inverse(0)

                def attention_scores(b):
                    if b == 0:
                        pe.wait_ge(*at(qkT_done, l, 3))
                    else:
                        pe.wait_ge(*at(pTr_act, l, b))
                        pe.wait_ge(*at(pTr_dve, l, b))
                    for s in range(HEADS):
                        h, base = 2 * (s % 4) + s // 4, 64 * (s // 4)
                        last = mm(ps[:, 4 + s // 2, (s % 2) * 256:(s % 2) * 256 + 256],
                                  q_t[base:base + 64, h // 2, b * P:(b + 1) * P], k_t[base:base + 64, h // 4, :],
                                  start=True, stop=True)
                    last.then_inc(att_ready.sem, 1)

                def attention_transposes(b):
                    pe.wait_ge(*at(probs_done, l, b + 1))
                    for kb in range(TB):
                        for s in range(HEADS):
                            n = kb * HEADS + s
                            last = tr(ps[:, 4 + n // 4, (n % 4) * P:(n % 4 + 1) * P],
                                      probs[:, s, kb * P:(kb + 1) * P], ident)
                    last.then_inc(pTr_ready.sem, 1)

                def attention_values(b):
                    pe.wait_ge(*at(pTr_act, l, b + 1))
                    pe.wait_ge(*at(pTr_dve, l, b + 1))
                    if b == 0:
                        pe.wait_ge(*at(zT_done, l, 2))
                    else:
                        pe.wait_ge(*at(attn_done, l, b))
                    for s in range(HEADS):
                        h, base = 2 * (s % 4) + s // 4, 64 * (s // 4)
                        v_col = A_W + KV_W + (h // 4) * HEAD
                        for kb in range(TB):
                            last = mm(ps[base:base + 64, 3, (h // 2) * P:(h // 2 + 1) * P],
                                      p_qkv[:, kb, v_col:v_col + HEAD], probs_t[:, kb, s, :],
                                      start=(kb == 0), stop=(kb == 1))
                    last.then_inc(attn_ready.sem, 1)

                attention_scores(0)
                hyena_forward(1, 3)
                attention_transposes(0)
                hyena_inverse(1)
                attention_values(0)
                attention_scores(1)
                attention_transposes(1)
                attention_values(1)
                groups = ((0, 4), (4, 6), (6, 8))
                pe.wait_ge(*at(mixed_sq_done, l, 1))
                for g, (c0, c1) in enumerate(groups):
                    for b in range(TB):
                        for c in range(c0, c1):
                            last = mm(ps[:, 1, 2 * g + b:2 * g + b + 1], mixed_sq[:, c, b * P:(b + 1) * P],
                                      ones[:, 0:1], start=(c == c0), stop=(c == c1 - 1))
                last.then_inc(group_ready.sem, 1)
                pe.wait_ge(*at(mixed_done, l, 1))
                pe.wait_ge(*at(w_out_in, l, 16))
                for b in range(TB):
                    for g, (c0, c1) in enumerate(groups):
                        if b:
                            pe.wait_ge(*at(out_added, l, g + 1))
                        for n in range(2):
                            for c in range(c0, c1):
                                last = mm(ps[:, 2 + 2 * g + n, :], mixed[:, c, b * P:(b + 1) * P],
                                          wout[:, c, n * 512:(n + 1) * 512], start=(c == c0), stop=(c == c1 - 1))
                        last.then_inc(out_ready.sem, 1)
                transpose_x((0, 1, 2, 3), 4)
                pe.wait_ge(*at(hT_act, l, 8))
                pe.wait_ge(*at(hT_dve, l, 8))
                for k in range(DT):
                    s = k % W_Q_SLOTS
                    pe.wait_ge(*at(w_q_in[s], l, 16 * (k // W_Q_SLOTS + 1)))
                    for c in range(HP):
                        last = mm(ps[:, c // 2, (c % 2) * 256:(c % 2) * 256 + 256],
                                  area(W_Q + s * W_Q_N + c * P, P), h2_t[:, k, :],
                                  start=(k == 0 and c % 2 == 0), stop=(k == DT - 1), skip_group_check=True)
                        if k == DT - 1 and c % 2:
                            last.then_inc(query_ready.sem, 1)
                        if c == HP - 1 and k < DT - 1:
                            last.then_inc(w_q_used.sem, 1)
                pe.wait_ge(*at(subk_in, l, 16))
                pe.wait_ge(*at(query_act, l, 4))
                pe.wait_ge(*at(query_dve, l, 4))
                for b in range(TB):
                    for c in range(HP):
                        last = mm(ps[:, 4 * b + c // 4, (c % 4) * P:(c % 4 + 1) * P],
                                  query_t[:, c, b * P:(b + 1) * P], subk[:, c, :], start=True, stop=True)
                        if c % 4 == 3:
                            last.then_inc(scores_ready.sem, 1)
                pe.wait_ge(*at(scores_act, l, 4))
                pe.wait_ge(*at(scores_dve, l, 4))
                pe.wait_ge(*at(x_split, l, 1))

                def u_product(i, first):
                    for s in range(4):
                        j = i * 4 + s
                        pe.wait_ge(*at(hi_done, l, j + 1))
                        pe.wait_ge(*at(lo_done, l, j + 1))
                        if s % 2 == 0 and not first:
                            pe.wait_ge(*at(gelu_done, l, i * 2 + s // 2 - 1))
                        bank = ps[:, s // 2, (s % 2) * 256:(s % 2) * 256 + 256]
                        for k in range(DT):
                            cols = slice(k * P, (k + 1) * P)
                            mm(bank, tab_hi[:, s % 2, cols], x_lo[:, k, :], start=(k == 0), stop=False)
                            mm(bank, tab_hi[:, s % 2, cols], x_hi[:, k, :], start=False, stop=False)
                            last = mm(bank, tab_lo[:, s % 2, cols], x_hi[:, k, :], start=False, stop=(k == DT - 1))
                        last.then_inc(tile_used.sem, 1)

                u_product(0, True)
                with pe.Fori(1, 32) as i:
                    u_product(i, False)
                pe.wait_ge(*at(topk_done, l, 1))
                for n in range(3):
                    for b in range(TB):
                        last = tr(ps[:, 4 + n // 2, (n % 2) * 256 + b * P:(n % 2) * 256 + (b + 1) * P],
                                  chosen[:, n, b, :], ident)
                last.then_inc(picksT_ready.sem, 1)
                pe.wait_ge(*at(gelu_done, l, 64))

                def gates(i, first):
                    for s in range(2):
                        n = i * 2 + s
                        pe.wait_ge(*at(hot_g, l, n + 1))
                        pe.wait_ge(*at(hot_j, l, n + 1))
                        if not first:
                            pe.wait_ge(*at(weighted, l, n - 1))
                        for t in range(4):
                            last = mm(ps[:, s, t * P:(t + 1) * P], onehot[:, s, 0, t, :], onehot[:, s, 1, t, :],
                                      start=True, stop=True)
                        last.then_inc(gates_ready.sem, 1)

                gates(0, True)
                with pe.Fori(1, 32) as i:
                    gates(i, False)
                pe.wait_ge(*at(picksT_done, l, 1))

                def v_product(i, first, final):
                    for s in range(4):
                        j = i * 4 + s
                        pe.wait_ge(*at(hi_done, l, j + 129))
                        pe.wait_ge(*at(lo_done, l, j + 129))
                        pe.wait_ge(*at(whi_done, l, j + 1))
                        pe.wait_ge(*at(wlo_done, l, j + 1))
                        for b in range(TB):
                            tok = slice(b * P, (b + 1) * P)
                            for w, v, edge in ((w_hi, tab_lo, 0), (w_hi, tab_hi, 1), (w_lo, tab_hi, 2)):
                                for n in range(2):
                                    last = mm(ps[:, 4 + 2 * b + n, :], w[:, s % 2, tok],
                                              v[:, s % 2, n * 512:(n + 1) * 512],
                                              start=(first and s == 0 and edge == 0),
                                              stop=(final and s == 3 and edge == 2), skip_group_check=True)
                        last.then_inc(tile_used.sem, 1)

                v_product(0, True, False)
                with pe.Fori(1, 31) as i:
                    v_product(i, False, False)
                v_product(31, False, True)

        @block.scalar
        def _(act):
            fn = nc.scalar.activation
            act.wait_ge(const_in.sem, 16)
            act.wait_ge(x_landed.sem, 16)
            with act.Fori(0, DEPTH) as l:
                act.wait_ge(layer_done.sem, l + 1)
                for n, dst in enumerate((f_h1, f_h2)):
                    act.wait_ge(*at(sine_arg, l, n + 1))
                    fn(dst, arg, ACT.Sin).then_inc(sine_done.sem, 1)
                act.wait_ge(*at(filt_done, l, 2))
                fn(filt_sq, filt, ACT.Square).then_inc(filt_sq_done.sem, 1)
                for b in range(TB):
                    fn(x_lo[:, b * 4:(b + 1) * 4, :], x[:, b, :].rearrange("p (k t) -> p k t", k=4), ACT.Square,
                       accum_out=ss[:, b:b + 1]).then_inc(sq_sum.sem, 1)
                act.wait_ge(*at(f_norm_ready, l, 1))
                fn(f_rn, ps[:, 6, :], ACT.Sqrt, bias=EPS).then_inc(f_root_done.sem, 1)

                def evac_h(dst, gain, base, ready):
                    for k in range(4):
                        act.wait_ge(*at(xT_ready, l, ready + k // 2 + 1))
                        fn(dst[:, k, :], ps[:, base + k // 2, (k % 2) * 256:(k % 2) * 256 + 256], ACT.Copy,
                           scale=par(gain, k)).then_inc(hT_act.sem, 1)

                evac_h(h_t, "g1", 4, 0)
                act.wait_ge(*at(spec_done, l, 5))
                act.wait_ge(*at(fn_m_done, l, 1))
                for g in range(3):
                    act.wait_ge(*at(proj_ready, l, g + 1))
                    fn(p_t[:, 2 * g:2 * g + 2, 1:257], ps[:, g, :].rearrange("p (k t) -> p k t", k=2),
                       ACT.Copy).then_inc(pT_done.sem, 1)
                act.wait_ge(*at(proj_ready, l, 4))
                fn(fn_u, ps[:, 3, :].rearrange("p (k t) -> p k t", k=2), ACT.Copy).then_inc(pT_done.sem, 1)
                act.wait_ge(*at(pad_done, l, 1))
                act.wait_ge(*at(pT_done, l, 3))
                act.wait_ge(*at(xT_ready, l, 4))
                act.wait_ge(*at(proj_ready, l, 8))
                for c in range(6):
                    fn(conv[:, c, :], p_t[:, c, 0:256], ACT.Identity, scale=par("cw", c), bias=par("cb", c))
                    fn(tap1[:, c, :], p_t[:, c, 1:257], ACT.Copy, scale=par("cw", 6 + c))
                    last = fn(tap2[:, c, :], p_t[:, c, 2:258], ACT.Copy, scale=par("cw", 12 + c))
                last.then_inc(conv_taps.sem, 1)

                def evac_z(o, bank):
                    act.wait_ge(*at(zT_ready, l, o + 1))
                    fn(z_t, ps[:, bank, :].rearrange("p (b c) -> p b c", b=TB), ACT.Copy).then_inc(zT_done.sem, 1)

                evac_z(0, 0)
                for b in range(TB):
                    act.wait_ge(*at(fn1_ready, l, b + 1))
                    fn(fn_p[:, b, :, :, :], ps[:, (3, 7)[b], :].rearrange("p (q m c) -> p q m c", q=2, m=2),
                       ACT.Copy).then_inc(fn1_done.sem, 1)
                act.wait_ge(*at(fn2_ready, l, 1))
                for q in range(2):
                    last = fn(mixed[:, 6 + q, :], ps[:, 3, q * 256:(q + 1) * 256], ACT.Identity, bias=par("fb", q))
                last.then_inc(fn2_done.sem, 1)
                for g in range(3):
                    dst = (q_t[:, 0:2, :], q_t[:, 2:4, :], k_t)[g]
                    act.wait_ge(*at(qkT_ready, l, g + 1))
                    fn(dst, ps[:, 4 + g, :].rearrange("p (k t) -> p k t", k=2), ACT.Copy).then_inc(qkT_done.sem, 1)

                def exponentials(b):
                    act.wait_ge(*at(max_done, l, b + 1))
                    for s in range(HEADS):
                        last = fn(probs[:, s, :], ps[:, 4 + s // 2, (s % 2) * 256:(s % 2) * 256 + 256], ACT.Exp,
                                  bias=nmx[:, s:s + 1], scale=HEAD ** -0.5, accum_out=rs[:, s:s + 1])
                    last.then_inc(exp_done.sem, 1)

                def evac_probs(b):
                    act.wait_ge(*at(pTr_ready, l, b + 1))
                    fn(probs_t[:, 0, :, :], ps[:, 4:6, :].rearrange("p k (s q) -> p (k s) q", q=P),
                       ACT.Copy).then_inc(pTr_act.sem, 1)

                def evac_attn(b):
                    act.wait_ge(*at(attn_ready, l, b + 1))
                    fn(mixed[:, 0:4, b * P:(b + 1) * P], ps[:, 3, :].rearrange("p (k q) -> p k q", k=4),
                       ACT.Copy).then_inc(attn_done.sem, 1)

                exponentials(0)
                evac_z(1, 3)
                evac_probs(0)
                evac_attn(0)
                exponentials(1)
                evac_probs(1)
                evac_attn(1)
                act.wait_ge(*at(attn_done, l, 2))
                act.wait_ge(*at(fn2_done, l, 1))
                act.wait_ge(*at(hyena_done, l, 2))
                act.wait_ge(*at(pTr_ready, l, 2))
                fn(mixed_sq, mixed, ACT.Square).then_inc(mixed_sq_done.sem, 1)
                for b in range(TB):
                    act.wait_ge(*at(out_added, l, 3 * b + 3))
                    fn(x_lo[:, b * 4:(b + 1) * 4, :], x[:, b, :].rearrange("p (k t) -> p k t", k=4), ACT.Square,
                       accum_out=ss[:, b:b + 1]).then_inc(sq_sum.sem, 1)
                act.wait_ge(*at(group_ready, l, 1))
                evac_h(h2_t, "g2", 0, 4)
                for g in range(4):
                    act.wait_ge(*at(query_ready, l, g + 1))
                    fn(query_t[:, 2 * g:2 * g + 2, :], ps[:, g, :].rearrange("p (k t) -> p k t", k=2),
                       ACT.Copy).then_inc(query_act.sem, 1)
                for g in range(4):
                    act.wait_ge(*at(scores_ready, l, 4 + g + 1))
                    fn(scores[:, 1, 4 * g:4 * g + 4, :], ps[:, 4 + g, :].rearrange("p (k n) -> p k n", k=4),
                       ACT.Copy).then_inc(scores_act.sem, 1)

                def upper(s, j, slot_free, layer_base):
                    act.wait_ge(*at(raw_in[s], l, slot_free))
                    fn(tab_hi[:, s % 2, :], raw[:, s, :], ACT.Copy).then_inc(hi_done.sem, 1)

                def u_upper(i, s, early):
                    if not (early and s < 2):
                        act.wait_ge(*at(tile_used, l, i * 4 + s - 1))
                    act.wait_ge(*at(raw_in[s], l, i * 16 + 16))
                    fn(tab_hi[:, s % 2, :], raw[:, s, :], ACT.Copy).then_inc(hi_done.sem, 1)

                def gelu(n, bank):
                    act.wait_ge(*at(tile_used, l, 2 * n + 2))
                    fn(work[:, bass.ds(2 * n, 2), :], ps[:, bank, :].rearrange("p (k t) -> p k t", k=2),
                       ACT.Gelu).then_inc(gelu_done.sem, 1)

                def u_quad(i, early):
                    u_upper(i, 0, early)
                    u_upper(i, 1, early)
                    if not early:
                        gelu(i * 2 - 1, 1)
                    u_upper(i, 2, early)
                    u_upper(i, 3, early)
                    gelu(i * 2, 0)

                u_quad(0, True)
                with act.Fori(1, GUARD // 4) as i:
                    u_quad(i, False)
                act.wait_ge(*at(best_done, l, 1))
                fn(best.rearrange("p b h n -> p (b h n)"), best.rearrange("p b h n -> p (b h n)"), ACT.Exp).then_inc(gate_exp.sem, 1)
                act.wait_ge(*at(topk_done, l, 1))
                with act.Fori(GUARD // 4, 32) as i:
                    u_quad(i, False)
                gelu(63, 1)

                def v_quad(i):
                    for s in range(4):
                        act.wait_ge(*at(tile_used, l, i * 4 + s + 127))
                        act.wait_ge(*at(raw_in[s], l, i * 16 + 528))
                        fn(tab_hi[:, s % 2, :], raw[:, s, :], ACT.Copy).then_inc(hi_done.sem, 1)
                        act.wait_ge(*at(weighted, l, 64))
                        fn(w_hi[:, s % 2, :], work[:, i * 4 + s, :], ACT.Copy).then_inc(whi_done.sem, 1)

                with act.Fori(0, 32) as i:
                    v_quad(i)
            act.wait_ge(layer_done.sem, DEPTH + 1)
            for b in range(TB):
                fn(x_lo[:, b * 4:(b + 1) * 4, :], x[:, b, :].rearrange("p (k t) -> p k t", k=4), ACT.Square,
                   accum_out=ss[:, b:b + 1]).then_inc(sq_sum.sem, 1)

        @block.gpsimd
        def _(pool):
            pool.wait_ge(const_in.sem, 16)
            with pool.Fori(0, DEPTH) as l:
                def inverse_root(n, dst, src, width):
                    pool.wait_ge(*at(mean_sq, l, n))
                    nc.gpsimd.tensor_tensor(dst, src, neg_half.broadcast_to([P, width]), ALU.pow)\
                        .then_inc(inv_root.sem, 1)

                inverse_root(1, rinv, ms, 2)
                pool.wait_ge(*at(conv_taps, l, 1))
                nc.gpsimd.tensor_tensor(conv, conv, tap1, ALU.add).then_inc(pool_step.sem, 1)
                pool.wait_ge(*at(pool_step, l, 1))
                nc.gpsimd.tensor_tensor(conv, conv, tap2, ALU.add).then_inc(conv_done.sem, 1)
                inverse_root(2, r20, ms20, 20)
                inverse_root(3, r6, ms6, 6)
                inverse_root(4, rinv, ms, 2)

                def u_lower(i, early):
                    for s in range(4):
                        if not (early and s < 2):
                            pool.wait_ge(*at(tile_used, l, i * 4 + s - 1))
                        pool.wait_ge(*at(hi_done, l, i * 4 + s + 1))
                        nc.gpsimd.tensor_tensor(tab_lo[:, s % 2, :], raw[:, s, :], tab_hi[:, s % 2, :].bitcast(F32),
                                                ALU.subtract).then_inc(lo_done.sem, 1)

                u_lower(0, True)
                with pool.Fori(1, 32) as i:
                    u_lower(i, False)

                def scale_hot(i):
                    for s in range(2):
                        n = i * 2 + s
                        pool.wait_ge(*at(hot_i, l, n + 1))
                        nc.gpsimd.tensor_tensor(
                            onehot[:, s, 0, :, :], onehot[:, s, 0, :, :],
                            picks[:, 2, bass.ds(n * 4, 4)].rearrange("p (t a) -> p t a", a=1).broadcast_to([P, 4, P]),
                            ALU.mult).then_inc(hot_g.sem, 1)

                with pool.Fori(0, 32) as i:
                    scale_hot(i)
            pool.wait_ge(mean_sq.sem, DEPTH * 4 + 1)
            nc.gpsimd.tensor_tensor(rinv, ms, neg_half.broadcast_to([P, 2]), ALU.pow).then_inc(inv_root.sem, 1)

        @block.vector
        def _(dve):
            v = nc.vector
            dve.wait_ge(const_in.sem, 16)
            dve.wait_ge(x_landed.sem, 16)
            v.memset(small[:, 127:128], 0.0).then_inc(layer_done.sem, 1)
            with dve.Fori(0, DEPTH) as l:
                count = [0]

                def link(ins):
                    count[0] += 1
                    ins.then_inc(dve_step.sem, 1)
                    dve.wait_ge(*at(dve_step, l, count[0]))

                def norm_scale(n):
                    dve.wait_ge(*at(sq_sum, l, 2 * n + 2))
                    if n:
                        dve.wait_ge(*at(inv_root, l, 3))
                    v.tensor_scalar(ms, ss, 1.0 / D, EPS, ALU.mult, ALU.add).then_inc(mean_sq.sem, 1)
                    dve.wait_ge(*at(inv_root, l, (1, 4)[n]))
                    for b in range(TB):
                        v.tensor_scalar(xn[:, b, :], x[:, b, :], rinv[:, b:b + 1], None, ALU.mult)\
                            .then_inc(xn_done.sem, 1)

                dve.wait_ge(*at(params_in, l, 64))
                for n in range(2):
                    dve.wait_ge(*at(mlp_ready, l, n + 1))
                    link(v.tensor_scalar(arg, ps[0:64, n, 0:256], par(("b1", "b2")[n], rows=64),
                                         par(("f1", "f2")[n], rows=64), ALU.add, ALU.mult))
                    link(v.tensor_scalar(turns, arg, INV_2PI, ROUND, ALU.mult, ALU.add))
                    link(v.tensor_scalar(turns, turns, ROUND, None, ALU.subtract))
                    for part in TWO_PI:
                        link(v.scalar_tensor_tensor(arg, turns, -part, arg, ALU.mult, ALU.add))
                    v.tensor_scalar(arg, arg, SIN_MAX, -SIN_MAX, ALU.min, ALU.max).then_inc(sine_arg.sem, 1)
                    dve.wait_ge(*at(sine_arg, l, n + 1))
                    dve.wait_ge(*at(sine_done, l, n + 1))
                for b in range(TB):
                    dve.wait_ge(*at(taps_ready, l, b + 1))
                    v.tensor_tensor(filt[:, b, :, :, :].rearrange("p o e c -> p (o e) c"),
                                    ps[:, 2 + 2 * b:4 + 2 * b, :].rearrange("p k (e c) -> p (k e) c", c=256),
                                    decay[:, b:b + 1, :].broadcast_to([P, 4, 256]), ALU.mult)\
                        .then_inc(filt_done.sem, 1)
                dve.wait_ge(*at(filt_done, l, 2))
                for b in range(TB):
                    mask = kc[:, KC["not_first"]:KC["not_first"] + 1] if b == 0 else 1.0
                    link(v.scalar_tensor_tensor(f_sum[:, b, :, :], filt[:, b, :, 1, :], mask, filt[:, b, :, 0, :],
                                                ALU.mult, ALU.add))
                    last = v.tensor_tensor(f_dif[:, b, :, :], filt[:, b, :, 1, :], filt[:, b, :, 0, :], ALU.subtract)
                    if b == 0:
                        link(last)
                last.then_inc(sumdif_done.sem, 1)
                norm_scale(0)
                dve.wait_ge(*at(f_root_done, l, 1))
                link(v.reciprocal(f_rn, f_rn))
                for n in range(5):
                    dve.wait_ge(*at(spec_ready, l, n + 1))
                    v.tensor_tensor(spec[:, n, :, :].rearrange("p o c -> p (o c)"), ps[:, n, :], f_rn, ALU.mult)\
                        .then_inc(spec_done.sem, 1)
                dve.wait_ge(*at(fn_m_ready, l, 1))
                v.tensor_copy(fn_m.rearrange("p m q c -> p (m q c)"), ps[:, 0, :]).then_inc(fn_m_done.sem, 1)
                v.memset(p_t[:, :, 0:1], 0.0)
                v.memset(p_t[:, :, 257:258], 0.0).then_inc(pad_done.sem, 1)

                def evac_h(dst, gain, base, ready):
                    for k in range(4, 8):
                        dve.wait_ge(*at(xT_ready, l, ready + k // 2 + 1))
                        v.tensor_scalar(dst[:, k, :], ps[:, base + k // 2, (k % 2) * 256:(k % 2) * 256 + 256],
                                        par(gain, k), None, ALU.mult).then_inc(hT_dve.sem, 1)

                evac_h(h_t, "g1", 4, 0)
                for n in range(4):
                    dve.wait_ge(*at(proj_ready, l, 5 + n))
                    v.tensor_copy(p_qkv[:, n // 2, (n % 2) * 384:(n % 2) * 384 + 384], ps[:, 4 + n, 0:384])\
                        .then_inc(qkv_done.sem, 1)
                dve.wait_ge(*at(qkv_done, l, 4))
                dve.wait_ge(*at(gqk_in, l, 16))
                qk = p_qkv[:, :, 0:640]
                rope3 = rope.rearrange("p (b n) -> p b n", b=TB)
                qn3 = qn.rearrange("p (b n) -> p b n", b=TB)
                link(v.tensor_tensor(rope3, qk, qk, ALU.mult))
                link(v.tensor_reduce(ss20, rope.rearrange("p (n d) -> p n d", d=HEAD), AX.X, ALU.add))
                v.tensor_scalar(ms20, ss20, 1.0 / HEAD, EPS, ALU.mult, ALU.add).then_inc(mean_sq.sem, 1)
                dve.wait_ge(*at(inv_root, l, 2))
                for b in range(TB):
                    link(v.tensor_tensor(qn3[:, b, :].rearrange("p (h d) -> p h d", d=HEAD),
                                         p_qkv[:, b, 0:640].rearrange("p (h d) -> p h d", d=HEAD),
                                         r20[:, b * 10:(b + 1) * 10].rearrange("p (h a) -> p h a", a=1)
                                         .broadcast_to([P, 10, HEAD]), ALU.mult))
                link(v.tensor_tensor(qn3, qn3, gqk.rearrange("p (a n) -> p a n", a=1).broadcast_to([P, TB, 640]),
                                     ALU.mult))
                rot5 = rot.rearrange("p (b h a e d) -> p b h a e d", b=TB, h=10, a=2, e=2)
                qn5 = qn.rearrange("p (b h a e d) -> p b h a e d", b=TB, h=10, a=2, e=2)
                for b in range(TB):
                    link(v.tensor_tensor(rope3[:, b, :].rearrange("p (h d) -> p h d", d=HEAD),
                                         qn3[:, b, :].rearrange("p (h d) -> p h d", d=HEAD),
                                         cos_r[:, b:b + 1, :].broadcast_to([P, 10, HEAD]), ALU.mult))
                    sins = sin_r[:, b:b + 1, :].rearrange("p o (a e d) -> p o a e d", a=2, e=2)
                    for e in range(2):
                        link(v.tensor_tensor(rot5[:, b, :, :, e, :], qn5[:, b, :, :, 1 - e, :],
                                             sins[:, :, :, e, :].broadcast_to([P, 10, 2, 16]), ALU.mult))
                link(v.tensor_tensor(rope, rope, rot, ALU.add))
                for b in range(TB):
                    last = v.tensor_copy(k_twice[:, b, :, :, :],
                                         rope3[:, b, 512:640].rearrange("p (g a d) -> p g a d", g=2, a=1)
                                         .broadcast_to([P, 2, 2, HEAD]))
                last.then_inc(rope_done.sem, 1)

                def hyena_multiply(o):
                    dve.wait_ge(*at(u_spec_ready, l, o + 1))
                    re = ps[:, 1, :].rearrange("p (k c) -> p k c", k=2)
                    im = ps[:, 2, :].rearrange("p (k c) -> p k c", k=2)
                    link(v.tensor_tensor(prod[:, 0, :, :], re, spec[:, 0:2, o, :], ALU.mult))
                    link(v.tensor_tensor(prod[:, 1, :, :], im, spec[:, 2:4, o, :], ALU.mult))
                    link(v.tensor_tensor(prod[:, 2, :, :], re, spec[:, 2:4, o, :], ALU.mult))
                    link(v.tensor_tensor(prod[:, 3, 0, :], im[:, 0, :], spec[:, 4, o, :], ALU.mult))
                    link(v.tensor_tensor(prod[:, 3, 1, :], im[:, 1, :], spec[:, 1, o, :], ALU.mult))
                    link(v.tensor_tensor(y_spec[:, 0, :, :], prod[:, 0, :, :], prod[:, 1, :, :], ALU.subtract))
                    v.tensor_tensor(y_spec[:, 1, :, :], prod[:, 2, :, :], prod[:, 3, :, :], ALU.add)\
                        .then_inc(y_spec_done.sem, 1)

                def hyena_gate(o):
                    dve.wait_ge(*at(y_ready, l, o + 1))
                    dve.wait_ge(*at(y_spec_done, l, o + 1))
                    for c in range(2):
                        link(v.scalar_tensor_tensor(prod[:, 0, c, :], conv[:, c, :], par("hb", 2 * o + c),
                                                    ps[:, 0, c * 256:(c + 1) * 256], ALU.mult, ALU.add))
                    dst = conv[:, 0:2, :] if o == 0 else mixed[:, 4:6, :]
                    v.tensor_tensor(dst, prod[:, 0, :, :], conv[:, 2 + 2 * o:4 + 2 * o, :], ALU.mult)\
                        .then_inc(hyena_done.sem, 1)

                def softmax_max(b):
                    dve.wait_ge(*at(att_ready, l, b + 1))
                    link(v.tensor_reduce(mx, ps[:, 4:8, :].rearrange("p k (s n) -> p (k s) n", n=256), AX.X,
                                         ALU.max))
                    v.tensor_scalar(nmx, mx, -HEAD ** -0.5, None, ALU.mult).then_inc(max_done.sem, 1)

                def softmax_scale(b):
                    dve.wait_ge(*at(exp_done, l, b + 1))
                    link(v.reciprocal(rrs, rs))
                    v.tensor_tensor(probs, probs, rrs.rearrange("p (s a) -> p s a", a=1)
                                    .broadcast_to([P, HEADS, 256]), ALU.mult).then_inc(probs_done.sem, 1)

                def evac_probs(b):
                    dve.wait_ge(*at(pTr_ready, l, b + 1))
                    v.tensor_copy(probs_t[:, 1, :, :], ps[:, 6:8, :].rearrange("p k (s q) -> p (k s) q", q=P))\
                        .then_inc(pTr_dve.sem, 1)

                hyena_multiply(0)
                hyena_gate(0)
                softmax_max(0)
                softmax_scale(0)
                hyena_multiply(1)
                evac_probs(0)
                hyena_gate(1)
                softmax_max(1)
                softmax_scale(1)
                dve.wait_ge(*at(attn_ready, l, 1))
                evac_probs(1)
                dve.wait_ge(*at(mixed_sq_done, l, 1))
                v.tensor_tensor(mixed, mixed, pv[:, PV["gm"]:PV["gm"] + 8].rearrange("p (k a) -> p k a", a=1)
                                .broadcast_to([P, 8, SEQ]), ALU.mult).then_inc(mixed_done.sem, 1)
                dve.wait_ge(*at(group_ready, l, 1))
                link(v.tensor_scalar(ms6[:, 0:2], ps[:, 1, 0:2], 1.0 / A_W, EPS, ALU.mult, ALU.add))
                v.tensor_scalar(ms6[:, 2:6], ps[:, 1, 2:6], 1.0 / HY_W, EPS, ALU.mult, ALU.add)\
                    .then_inc(mean_sq.sem, 1)
                dve.wait_ge(*at(inv_root, l, 3))
                for b in range(TB):
                    for g in range(3):
                        dve.wait_ge(*at(out_ready, l, 3 * b + g + 1))
                        v.scalar_tensor_tensor(x[:, b, :], ps[:, 2 + 2 * g:4 + 2 * g, :].rearrange("p k n -> p (k n)"),
                                               r6[:, 2 * g + b:2 * g + b + 1], x[:, b, :], ALU.mult, ALU.add)\
                            .then_inc(out_added.sem, 1)
                        dve.wait_ge(*at(out_added, l, 3 * b + g + 1))
                norm_scale(1)
                evac_h(h2_t, "g2", 0, 4)
                dve.wait_ge(*at(hT_act, l, 8))
                dve.wait_ge(*at(hT_dve, l, 8))
                link(v.tensor_copy(x_hi[:, :, :], h2_t))
                v.tensor_tensor(x_lo[:, :, :], h2_t, x_hi[:, :, :].bitcast(F32), ALU.subtract).then_inc(x_split.sem, 1)
                for g in range(4):
                    dve.wait_ge(*at(query_ready, l, 4 + g + 1))
                    v.tensor_copy(query_t[:, 8 + 2 * g:10 + 2 * g, :],
                                  ps[:, 4 + g, :].rearrange("p (k t) -> p k t", k=2)).then_inc(query_dve.sem, 1)
                for g in range(4):
                    dve.wait_ge(*at(scores_ready, l, g + 1))
                    if g == 3:
                        dve.wait_ge(*at(scores_act, l, 4))
                    v.tensor_copy(scores[:, 0, 4 * g:4 * g + 4, :], ps[:, g, :].rearrange("p (k n) -> p k n", k=4))\
                        .then_inc(scores_dve.sem, 1)
                settled(dve)

                def top16(values, indices, row, rows):
                    steps = (lambda r: v.max(values(r)[:, 0:8], row(r)),
                             lambda r: v.max_index(indices(r)[:, 0:8], values(r)[:, 0:8], row(r)),
                             lambda r: v.match_replace(row(r), values(r)[:, 0:8], row(r), NEG),
                             lambda r: v.max(values(r)[:, 8:16], row(r)),
                             lambda r: v.max_index(indices(r)[:, 8:16], values(r)[:, 8:16], row(r)))
                    for step in steps:
                        for r in range(rows):
                            last = step(r)
                        settled(dve)

                for b in range(TB):
                    top16(lambda r: v_top[:, b, r, :], lambda r: i_top[:, b, r, :], lambda r: scores[:, b, r, :], HP)
                link(v.tensor_copy(i_topf, i_top))
                for b in range(TB):
                    side = v_top[:, b, :, :].rearrange("p (h s) n -> p h s n", s=2)
                    v.tensor_tensor(
                        cand, side[:, :, 0, :].rearrange("p h (n a) -> p h n a", a=1).broadcast_to([P, PH, 16, 16]),
                        side[:, :, 1:2, :].broadcast_to([P, PH, 16, 16]), ALU.add)
                    settled(dve)
                    top16(lambda r: best[:, b, r, :], lambda r: pos[:, b, r * 16:(r + 1) * 16],
                          lambda r: cand[:, r, :, :].rearrange("p a b -> p (a b)"), PH)
                bests = best.rearrange("p b h n -> p (b h) n")
                link(v.tensor_copy(ssg.rearrange("p (n a) -> p n a", a=1), bests[:, :, 0:1]))
                v.tensor_tensor(bests, bests, ssg.rearrange("p (n a) -> p n a", a=1).broadcast_to([P, 16, 16]),
                                ALU.subtract).then_inc(best_done.sem, 1)
                for b in range(TB):
                    link(v.tensor_single_scalar(place_u[:, 0, :], pos[:, b, :], 4, op=ALU.logical_shift_right))
                    link(v.tensor_single_scalar(place_u[:, 1, :], pos[:, b, :], 15, op=ALU.bitwise_and))
                    link(v.tensor_copy(place_f, place_u))
                    for s in range(2):
                        link(v.tensor_tensor(
                            eq, place_f[:, s, :].rearrange("p (n a) -> p n a", a=1).broadcast_to([P, PICKS, TOPK]),
                            iota16.rearrange("p (a n) -> p a n", a=1).broadcast_to([P, PICKS, TOPK]), ALU.is_equal))
                        side = i_topf[:, b, :, :].rearrange("p (h s) n -> p h s n", s=2)[:, :, s:s + 1, :]
                        eq4 = eq.rearrange("p (h k) r -> p h k r", h=PH)
                        link(v.tensor_tensor(eq4, eq4, side.broadcast_to([P, PH, TOPK, TOPK]), ALU.mult))
                        link(v.tensor_reduce(chosen[:, s, b, :], eq, AX.X, ALU.add))
                dve.wait_ge(*at(gate_exp, l, 1))
                link(v.tensor_reduce(ssg, bests, AX.X, ALU.add))
                link(v.reciprocal(ssg, ssg))
                v.tensor_tensor(chosen[:, 2, :, :].rearrange("p b (h n) -> p (b h) n", n=16), bests,
                                ssg.rearrange("p (n a) -> p n a", a=1).broadcast_to([P, 16, 16]), ALU.mult)\
                    .then_inc(topk_done.sem, 1)
                dve.wait_ge(*at(picksT_ready, l, 1))
                link(v.tensor_copy(picks[:, 0:2, :], ps[:, 4, :].rearrange("p (n t) -> p n t", n=2)))
                v.tensor_copy(picks[:, 2, :], ps[:, 5, 0:256]).then_inc(picksT_done.sem, 1)
                dve.wait_ge(*at(picksT_done, l, 1))
                dve.wait_ge(*at(gelu_done, l, 64))

                def hot(i, s, side, signal, early):
                    n = i * 2 + s
                    if not early:
                        dve.wait_ge(*at(gates_ready, l, n - 1))
                    v.tensor_tensor(onehot[:, s, side, :, :],
                                    iota.rearrange("p (a c) -> p a c", a=1).broadcast_to([P, 4, P]),
                                    picks[:, side, bass.ds(n * 4, 4)].rearrange("p (t a) -> p t a", a=1)
                                    .broadcast_to([P, 4, P]), ALU.is_equal).then_inc(signal.sem, 1)

                def weigh(n, s):
                    dve.wait_ge(*at(gates_ready, l, n + 1))
                    cell = work[:, :, bass.ds(n * 4, 4)]
                    v.tensor_tensor(cell, ps[:, s, :].rearrange("p (t j) -> p j t", t=4), cell, ALU.mult)\
                        .then_inc(weighted.sem, 1)

                def gate_body(i, first):
                    hot(i, 0, 0, hot_i, first)
                    hot(i, 0, 1, hot_j, first)
                    if not first:
                        weigh(i * 2 - 1, 1)
                    hot(i, 1, 0, hot_i, first)
                    hot(i, 1, 1, hot_j, first)
                    weigh(i * 2, 0)

                gate_body(0, True)
                with dve.Fori(1, 32) as i:
                    gate_body(i, False)
                weigh(63, 1)
                settled(dve)

                with dve.Fori(0, 32) as i:
                    for s in range(4):
                        dve.wait_ge(*at(hi_done, l, i * 4 + s + 129))
                        dve.wait_ge(*at(tile_used, l, i * 4 + s + 127))
                        v.tensor_tensor(tab_lo[:, s % 2, :], raw[:, s, :], tab_hi[:, s % 2, :].bitcast(F32),
                                        ALU.subtract).then_inc(lo_done.sem, 1)
                        dve.wait_ge(*at(whi_done, l, i * 4 + s + 1))
                        v.tensor_tensor(w_lo[:, s % 2, :], work[:, i * 4 + s, :], w_hi[:, s % 2, :].bitcast(F32),
                                        ALU.subtract).then_inc(wlo_done.sem, 1)
                dve.wait_ge(*at(tile_used, l, 256))
                v.tensor_tensor(x[:, :, :].rearrange("p b d -> p (b d)"), ps[:, 4:8, :].rearrange("p k n -> p (k n)"),
                                x[:, :, :].rearrange("p b d -> p (b d)"), ALU.add).then_inc(layer_done.sem, 1)
                assert count[0] == dve_step.per_layer, f"dve_step counts {count[0]} per layer"
                dve.wait_ge(*at(layer_done, l, 2))
            dve.wait_ge(sq_sum.sem, DEPTH * 4 + 2)
            v.tensor_scalar(ms, ss, 1.0 / D, EPS, ALU.mult, ALU.add).then_inc(mean_sq.sem, 1)
            dve.wait_ge(inv_root.sem, DEPTH * 4 + 1)
            dve.wait_ge(fg_in.sem, 16)
            for b in range(TB):
                last = v.scalar_tensor_tensor(xn[:, b, :], x[:, b, :], rinv[:, b:b + 1], area(0, D), ALU.mult,
                                              ALU.mult)
            last.then_inc(fin.sem, 1)


def constants():
    import numpy as np
    f32 = np.float32
    kc = np.zeros((P, KC_N), f32)
    kc[:, KC["ident"]:KC["ident"] + P] = np.eye(P)
    kc[:, KC["iota"]:KC["iota"] + P] = np.arange(P)
    kc[:, KC["ones"]:KC["ones"] + P] = 1.0
    row = np.repeat(np.arange(SEQ // 64), 64).astype(f32)
    col = np.tile(np.arange(64), SEQ // 64).astype(f32)
    inv = (f32(10000.0) ** (-np.arange(16, dtype=f32) / f32(16))).astype(f32)
    ang = np.stack([row[:, None] * inv, col[:, None] * inv], axis=1)
    cos = np.stack([np.cos(ang), np.cos(ang)], axis=2).reshape(TB, P, 64)
    sin = np.stack([-np.sin(ang), np.sin(ang)], axis=2).reshape(TB, P, 64)
    kc[:, KC["cos"]:KC["cos"] + 128] = cos.transpose(1, 0, 2).reshape(P, 128)
    kc[:, KC["sin"]:KC["sin"] + 128] = sin.transpose(1, 0, 2).reshape(P, 128)
    kc[:, KC["neg_half"]] = -0.5
    kc[:, KC["not_first"]] = 1.0
    kc[0, KC["not_first"]] = 0.0
    kc[:, KC["iota16"]:KC["iota16"] + 16] = np.arange(16)

    def tiles(m):
        return m.reshape(TB, P, -1).transpose(1, 0, 2).reshape(P, -1)

    cf = np.zeros((P, CF_N), f32)
    t = np.linspace(0.0, 1.0, SEQ, dtype=f32)[:, None]
    bands = np.arange(1, 9, dtype=f32)
    a = (f32(2.0 * np.pi) * t * bands).astype(f32)
    z = np.concatenate([t, np.sin(a), np.cos(a)], axis=-1)
    cf[0:17, CF["z"]:CF["z"] + 256] = z.T
    rates = np.linspace(-np.log(1e-2) / 1.5, -np.log(1e-2) / 0.3, HY_W, dtype=f32)
    cf[:, CF["decay"]:CF["decay"] + 512] = tiles(np.exp(-t * rates))
    n = np.arange(SEQ)
    w = 2 * np.pi * ((n[:, None] * n[None, :]) % 512) / 512
    nyq = (-1.0) ** n
    c, s = np.cos(w), np.sin(w)
    cf[:, CF["sin0"]:CF["sin0"] + 512] = tiles(s)
    cn = c[:, 0:P].copy()
    cn[:, 0] = nyq
    cf[:, CF["cosn"]:CF["cosn"] + 256] = tiles(cn)
    k = np.arange(64)
    wk = 2 * np.pi * ((k[:, None] * k[None, :]) % 64) / 64
    for g in range(2):
        cf[g * 64:(g + 1) * 64, CF["bc"] + g * 64:CF["bc"] + (g + 1) * 64] = np.cos(wk) / 128.0
        cf[g * 64:(g + 1) * 64, CF["bs"] + g * 64:CF["bs"] + (g + 1) * 64] = -np.sin(wk) / 128.0
    cd = np.zeros((P, CD_N), f32)
    sp = -s.copy()
    sp[:, 0] = nyq
    ic = c * (2.0 / 512)
    ic[0, :] = 1.0 / 512
    isn = -s * (2.0 / 512)
    isn[0, :] = nyq / 512
    wl = 2 * np.pi * ((n[:, None] * n[None, :]) % SEQ) / SEQ
    for name, m in (("cos", c), ("sin", sp), ("icos", ic), ("isin", isn), ("fc", np.cos(wl)), ("fs", np.sin(wl))):
        cd[:, CD[name]:CD[name] + 512] = tiles(m)
    return kc, cf, cd


def layouts(i):
    import numpy as np
    f32 = np.float32
    a = {k: np.asarray(v) for k, v in i.items()}
    pvec = np.zeros((DEPTH, P, PV_N), f32)

    def cols(v, k):
        return v.reshape(DEPTH, k, P).transpose(0, 2, 1)

    pvec[:, :, 0:8] = cols(a["norm1_g"], 8)
    pvec[:, :, 8:16] = cols(a["norm2_g"], 8)
    pvec[:, :, 16:24] = cols(a["mix_norm_g"], 8)
    pvec[:, :, 24:42] = cols(a["hy_conv_w"], 18)
    pvec[:, :, 42:48] = cols(a["hy_conv_b"], 6)
    pvec[:, :, 48:52] = cols(a["hy_bias"], 4)
    pvec[:, :, 52:54] = cols(a["fn_b"], 2)
    for n, name in enumerate(("hy_b1", "hy_freq1", "hy_b2", "hy_freq2")):
        pvec[:, 0:64, 54 + n] = a[name]
    pmat = np.zeros((DEPTH, P, PM_N), f32)
    pmat[:, 0:17, 0:64] = a["hy_w1"]
    pmat[:, 0:64, 64:128] = a["hy_w2"]
    pmat[:, 0:64, 128:1152] = a["hy_w3"]
    for g in range(4):
        q, h = g // 2, g % 2
        pmat[:, h * 64:(h + 1) * 64, 1152 + q * P + h * 64:1152 + q * P + (h + 1) * 64] = a["fn_w"][:, g]
    gqk = np.concatenate([np.tile(a["q_norm_g"], (1, 8)), np.tile(a["k_norm_g"], (1, 2))], axis=1)
    gqk = np.ascontiguousarray(np.broadcast_to(gqk[:, None, :], (DEPTH, P, 640)))
    subk = np.ascontiguousarray(a["peer_sub_keys"].transpose(0, 4, 2, 1, 3).reshape(DEPTH, P, HP * KEYS))
    tu = np.ascontiguousarray(a["peer_u"].reshape(DEPTH, P, P, DT, P).transpose(0, 2, 4, 3, 1).reshape(DEPTH, P, P, D))
    tv = np.ascontiguousarray(a["peer_v"].reshape(DEPTH, P, P, D).transpose(0, 2, 1, 3))
    kc, cf, cd = constants()
    return {
        "x_in": a["x"].reshape(SEQ, D), "w_in": a["w_in"], "w_out": a["w_out"], "w_query": a["peer_w_query"],
        "sub_keys": subk, "tab_u": tu, "tab_v": tv, "pvec": pvec, "pmat": pmat, "gain_qk": gqk, "kconst": kc,
        "cfilter": cf, "cdft": cd,
        "final_g": np.ascontiguousarray(np.broadcast_to(a["final_g"][None, :], (P, D))),
    }


def kernel(**inputs):
    import concourse.bacc as bacc
    from concourse.bass_utils import run_bass_kernel_spmd

    nc = bacc.Bacc("TRN2", target_bir_lowering=False, num_devices=1)
    arrays = layouts(inputs)
    args = [nc.dram_tensor(name, v.shape, mybir.dt.from_np(v.dtype), kind="ExternalInput").ap()
            for name, v in arrays.items()]
    out = nc.dram_tensor("out", (SEQ, D), F32, kind="ExternalOutput").ap()
    hybrid_encoder(nc, *args, out)
    r = run_bass_kernel_spmd(nc, [arrays], core_ids=[0])
    return r.results[0]["out"].reshape(1, SEQ, D)
```

```python
from contextlib import ExitStack

import concourse.bass as bass
from concourse import mybir

ALU = mybir.AluOpType
ACT = mybir.ActivationFunctionType
AX = mybir.AxisListType
F32 = mybir.dt.float32
F32R = mybir.dt.float32r
U32 = mybir.dt.uint32

P = 128
DEPTH = 2
SEQ = 256
D = 1024
TB = SEQ // P
DT = D // P
HEAD = 64
HEADS, KV_HEADS = 8, 2
A_W, KV_W, HY_W, FN_W = 512, 128, 256, 256
QKV = A_W + 2 * KV_W
CT = (3 * HY_W + FN_W) // P
IN_COLS = QKV + CT * P
PH, KEYS, TOPK = 8, 128, 16
HP = 2 * PH
PICKS = PH * TOPK
EPS = 1e-6
NEG = -3.0e38

INV_2PI = 0.15915494309189535
ROUND = 12582912.0
TWO_PI = (6.28125, 0.0019350051879882812, 3.019916050561733e-07)
SIN_MAX = 3.1415925

PV = {"g1": 0, "g2": 8, "gm": 16, "cw": 24, "cb": 42, "hb": 48, "fb": 52, "b1": 54, "f1": 55, "b2": 56, "f2": 57}
PV_N = 58
PM = {"w1": 0, "w2": 64, "w3": 128, "fw": 1152}
PM_N = 1408
KC = {"ident": 0, "iota": 128, "ones": 256, "cos": 384, "sin": 512, "neg_half": 640, "not_first": 641, "iota16": 642}
KC_N = 658
CF = {"z": 0, "decay": 256, "sin0": 768, "cosn": 1280, "bc": 1536, "bs": 1664}
CF_N = 1792
CD = {"cos": 0, "sin": 512, "icos": 1024, "isin": 1536, "fc": 2048, "fs": 2560}
CD_N = 3072

FILTER_C, FILTER_M = 0, 1792
DFT, GAIN_QK = 3200, 6272
LOADED_AHEAD = 6912
SINE, FILT, FILT_SQ, F_SUM, F_DIF, F_RN = 6912, 7936, 9984, 12032, 13056, 14080
PROBS, PROBS_T, MIXED_SQ = 6912, 9984, 0
TAPS = 9984
SPEC = 14592
ROPE_TAB = 17152
XN = 19712
P_QKV, P_T, FN_U = 21760, 23296, 24844
CONV, Z_T, ROPE, QN = 25356, 26892, 27404, 28684
Q_T, K_T, FN_P = 29964, 30988, 31500
QUERY_T = 0
SUBKEYS = SPEC
CAND, EQ, SCORES = 24576, 26624, 28672
GUARD = 96

A0, B0, O0, Q0, U0, V0, TILES = 0, 8, 16, 24, 40, 168, 296
OUT_ORDER = (6, 7, 4, 5, 0, 1, 2, 3)
EARLY = 40
LO_POOL = 2 * (O0 + 8) + 2 * EARLY
LO_DVE = 2 * TILES - LO_POOL
DVE_STEPS = 50


class Signal:

    def __init__(self, sem, per_layer):
        self.sem, self.per_layer = sem, per_layer


def at(signal, layer, count):
    return signal.sem, layer * signal.per_layer + count


def hybrid_encoder(nc, x_in, w_proj, sub_keys, tab_u, tab_v, pvec, pmat, gain_qk, kconst, cfilter,
                   cdft, final_g, out):
    with ExitStack() as ctx:
        def sb(name, shape, dt=F32):
            return ctx.enter_context(nc.sbuf_tensor(name, shape, dt))

        def sig(name, per_layer):
            return Signal(ctx.enter_context(nc.semaphore(name)), per_layer)

        work = sb("work", [P, P, SEQ])
        x = sb("x", [P, TB, D])
        x_hi = sb("x_hi", [P, DT, SEQ], F32R)
        x_lo = sb("x_lo", [P, DT, SEQ], F32R)
        raw = sb("raw", [P, 4, D])
        tab_hi = sb("tab_hi", [P, 2, D], F32R)
        tab_lo = sb("tab_lo", [P, 2, D], F32R)
        w_hi = sb("w_hi", [P, 2, SEQ], F32R)
        w_lo = sb("w_lo", [P, 2, SEQ], F32R)
        picks = sb("picks", [P, 3, SEQ])
        onehot = sb("onehot", [P, 2, 2, 4, P])
        kc = sb("kc", [P, KC_N])
        pv = sb("pv", [P, PV_N])
        chosen = sb("chosen", [P, 3, TB, PICKS])
        small = sb("small", [P, 128])
        ps = ctx.enter_context(nc.psum_tensor("ps", [P, 8, 512], F32))

        workf = work[:, :, :].rearrange("p j t -> p (j t)")
        onef = onehot[:, :, :, :, :].rearrange("p s a t c -> p (s a t c)")
        picksf = picks[:, :, :].rearrange("p n t -> p (n t)")
        chosenf = chosen[:, :, :, :].rearrange("p n b t -> p (n b t)")

        def area(start, n):
            return workf[:, start:start + n]

        ident = kc[:, KC["ident"]:KC["ident"] + P]
        iota = kc[:, KC["iota"]:KC["iota"] + P]
        ones = kc[:, KC["ones"]:KC["ones"] + P]
        cos_r = kc[:, KC["cos"]:KC["cos"] + TB * HEAD].rearrange("p (b d) -> p b d", b=TB)
        sin_r = kc[:, KC["sin"]:KC["sin"] + TB * HEAD].rearrange("p (b d) -> p b d", b=TB)
        neg_half = kc[:, KC["neg_half"]:KC["neg_half"] + 1]
        iota16 = kc[:, KC["iota16"]:KC["iota16"] + TOPK]

        def par(name, i=0, rows=P):
            return pv[0:rows, PV[name] + i:PV[name] + i + 1]

        ss = small[:, 0:2]
        rinv = small[:, 2:4]
        ss20 = small[:, 4:24]
        r20 = small[:, 24:44]
        mx = small[:, 44:52]
        nmx = small[:, 52:60]
        rs = small[:, 60:68]
        rrs = small[:, 68:76]
        ms6 = small[:, 76:82]
        r6 = small[:, 82:88]
        ssg = small[:, 88:104]
        ms = small[:, 104:106]
        ms20 = small[:, 106:126]

        fc = area(FILTER_C, CF_N)
        fm = area(FILTER_M, PM_N)
        arg = workf[0:64, SINE:SINE + 256]
        turns = workf[0:64, SINE + 256:SINE + 512]
        f_h1 = workf[0:64, SINE + 512:SINE + 768]
        f_h2 = workf[0:64, SINE + 768:SINE + 1024]
        filt = area(FILT, 2048).rearrange("p (b o e c) -> p b o e c", b=TB, o=2, e=2)
        filt_sq = area(FILT_SQ, 2048).rearrange("p (b o e c) -> p b o e c", b=TB, o=2, e=2)
        f_sum = area(F_SUM, 1024).rearrange("p (b o c) -> p b o c", b=TB, o=2)
        f_dif = area(F_DIF, 1024).rearrange("p (b o c) -> p b o c", b=TB, o=2)
        f_rn = area(F_RN, 512)
        decay = fc[:, CF["decay"]:CF["decay"] + 512].rearrange("p (b c) -> p b c", b=TB)
        sin0 = fc[:, CF["sin0"]:CF["sin0"] + 512].rearrange("p (b f) -> p b f", b=TB)
        cosn = fc[:, CF["cosn"]:CF["cosn"] + 256].rearrange("p (b f) -> p b f", b=TB)
        spec = area(SPEC, 2560).rearrange("p (k o c) -> p k o c", k=5, o=2)
        dft = area(DFT, CD_N)

        def mat(name):
            return dft[:, CD[name]:CD[name] + 512].rearrange("p (b f) -> p b f", b=TB)

        xn = area(XN, 2048).rearrange("p (b d) -> p b d", b=TB)
        p_qkv = area(P_QKV, TB * QKV).rearrange("p (b n) -> p b n", b=TB)
        p_t = area(P_T, 6 * 258).rearrange("p (k t) -> p k t", k=6)
        fn_u = area(FN_U, 512).rearrange("p (k t) -> p k t", k=2)
        fn_m = chosenf[:, 0:512].rearrange("p (m q c) -> p m q c", m=2, q=2)
        conv = area(CONV, 1536).rearrange("p (k t) -> p k t", k=6)
        tap1 = area(TAPS, 1536).rearrange("p (k t) -> p k t", k=6)
        tap2 = area(TAPS + 1536, 1536).rearrange("p (k t) -> p k t", k=6)
        z_t = area(Z_T, 512).rearrange("p (b c) -> p b c", b=TB)
        prod = onef[:, 0:2048].rearrange("p (m k c) -> p m k c", m=4, k=2)
        y_spec = area(QN, 1024).rearrange("p (m k c) -> p m k c", m=2, k=2)
        qn = area(QN, 1280)
        rope = area(ROPE, 1280)
        rot = onef[:, 0:1280]
        gqk = area(GAIN_QK, 640)
        cos_g = area(ROPE_TAB, 1280).rearrange("p (b n) -> p b n", b=TB)
        sin_g = area(ROPE_TAB + 1280, 1280).rearrange("p (b n) -> p b n", b=TB)
        k_twice = picksf[:, 0:512].rearrange("p (b g e d) -> p b g e d", b=TB, g=2, e=2)
        q_t = area(Q_T, 1024).rearrange("p (k t) -> p k t", k=4)
        k_t = area(K_T, 512).rearrange("p (k t) -> p k t", k=2)
        probs = area(PROBS, 2048).rearrange("p (u s k) -> p u s k", u=2, s=4)
        probs_t = area(PROBS_T, 4096).rearrange("p (u b s q) -> p u b s q", u=4, b=TB, s=4)
        fn_p = area(FN_P, 1024).rearrange("p (b q m c) -> p b q m c", b=TB, q=2, m=2)
        mixed_sq = area(MIXED_SQ, 2048).rearrange("p (k t) -> p k t", k=8)
        query_t = area(QUERY_T, HP * SEQ).rearrange("p (k t) -> p k t", k=HP)
        subk = area(SUBKEYS, HP * KEYS).rearrange("p (k n) -> p k n", k=HP)
        scores = area(SCORES, TB * HP * KEYS).rearrange("p (b k n) -> p b k n", b=TB, k=HP)
        cand = area(CAND, PH * TOPK * TOPK).rearrange("p (h a b) -> p h a b", h=PH, a=TOPK)
        eq = area(EQ, PICKS * TOPK).rearrange("p (n r) -> p n r", r=TOPK)
        v_top = onef[:, 0:512].rearrange("p (b k n) -> p b k n", b=TB, k=HP)
        i_top = onef[:, 512:1024].bitcast(U32).rearrange("p (b k n) -> p b k n", b=TB, k=HP)
        i_topf = onef[:, 1024:1536].rearrange("p (b k n) -> p b k n", b=TB, k=HP)
        best = onef[:, 1536:1792].rearrange("p (b h n) -> p b h n", b=TB, h=PH)
        pos = onef[:, 1792:2048].bitcast(U32).rearrange("p (b n) -> p b n", b=TB)
        dist_abs, hot_rows = (h[:, :, :].rearrange("p (s a) t -> p s (a t)", s=4)
                              .rearrange("p s (t c) -> p s t c", t=4) for h in (x_hi, x_lo))
        minus_j = chosenf[:, 0:SEQ]
        place_u = onef[:, 0:256].bitcast(U32).rearrange("p (s n) -> p s n", s=2)
        place_f = onef[:, 256:512].rearrange("p (s n) -> p s n", s=2)

        const_in = sig("const_in", 0)
        x_landed = sig("x_landed", 0)
        params_in = sig("params_in", 64)
        dft_in = sig("dft_in", 16)
        gqk_in = sig("gqk_in", 16)
        subk_in = sig("subk_in", 16)
        raw_in = [sig(f"raw_in{s}", 16 * TILES // 4) for s in range(4)]
        hi_done = sig("hi_done", 2 * TILES)
        lo_pool = sig("lo_pool", LO_POOL)
        lo_dve = sig("lo_dve", LO_DVE)
        half_used = sig("half_used", 2 * TILES)
        dve_step = sig("dve_step", DVE_STEPS)
        pool_step = sig("pool_step", 1)
        mlp_ready = sig("mlp_ready", 2)
        sine_arg = sig("sine_arg", 2)
        sine_done = sig("sine_done", 2)
        taps_ready = sig("taps_ready", TB)
        filt_done = sig("filt_done", TB)
        filt_sq_done = sig("filt_sq_done", 1)
        sumdif_done = sig("sumdif_done", 1)
        f_norm_ready = sig("f_norm_ready", 1)
        f_root_done = sig("f_root_done", 1)
        spec_ready = sig("spec_ready", 5)
        spec_done = sig("spec_done", 5)
        rope_tab_done = sig("rope_tab_done", 1)
        sq_sum = sig("sq_sum", 4)
        mean_sq = sig("mean_sq", 4)
        inv_root = sig("inv_root", 4)
        xn_done = sig("xn_done", 2 * TB)
        xT_ready = sig("xT_ready", 8)
        h_hi = sig("h_hi", 16)
        h_lo = sig("h_lo", 16)
        fn_m_ready = sig("fn_m_ready", 1)
        fn_m_done = sig("fn_m_done", 1)
        chan_done = sig("chan_done", 4)
        qkv_done = sig("qkv_done", 4)
        qk_sq = sig("qk_sq", 4)
        pad_done = sig("pad_done", 1)
        conv_taps = sig("conv_taps", 1)
        conv_done = sig("conv_done", 1)
        zT_ready = sig("zT_ready", 2)
        zT_done = sig("zT_done", 2)
        u_spec_ready = sig("u_spec_ready", 2)
        y_spec_done = sig("y_spec_done", 2)
        y_ready = sig("y_ready", 2)
        hyena_done = sig("hyena_done", 2)
        fn1_ready = sig("fn1_ready", 2)
        fn1_done = sig("fn1_done", 2)
        fn2_ready = sig("fn2_ready", 1)
        fn2_done = sig("fn2_done", 1)
        qn_done = sig("qn_done", 1)
        rot_done = sig("rot_done", 1)
        rope_done = sig("rope_done", 1)
        qkT_ready = sig("qkT_ready", 3)
        qkT_done = sig("qkT_done", 3)
        att_ready = sig("att_ready", 4)
        max_done = sig("max_done", 4)
        exp_done = sig("exp_done", 4)
        probs_done = sig("probs_done", 4)
        pT_ready = sig("pT_ready", 4)
        pT_act = sig("pT_act", 4)
        pT_dve = sig("pT_dve", 4)
        attn_ready = sig("attn_ready", 4)
        attn_sq = sig("attn_sq", TB)
        mix_hi = sig("mix_hi", 4)
        mix_lo = sig("mix_lo", 4)
        hyena_sq = sig("hyena_sq", 1)
        group_ready = sig("group_ready", 1)
        out_added = sig("out_added", 6)
        query_ready = sig("query_ready", 8)
        query_act = sig("query_act", 4)
        query_dve = sig("query_dve", 4)
        scores_ready = sig("scores_ready", 8)
        scores_act = sig("scores_act", 4)
        scores_dve = sig("scores_dve", 4)
        best_done = sig("best_done", 1)
        gate_exp = sig("gate_exp", 1)
        topk_done = sig("topk_done", 1)
        picksT_ready = sig("picksT_ready", 1)
        picksT_done = sig("picksT_done", 2)
        gelu_done = sig("gelu_done", 64)
        hot_i = sig("hot_i", 64)
        hot_scaled = sig("hot_scaled", 64)
        abs_done = sig("abs_done", 48)
        hot_j_act = sig("hot_j_act", 48)
        hot_j_dve = sig("hot_j_dve", 16)
        minus_done = sig("minus_done", 1)
        gates_ready = sig("gates_ready", 64)
        weighted = sig("weighted", 64)
        whi_done = sig("whi_done", 128)
        wlo_done = sig("wlo_done", 128)
        layer_done = sig("layer_done", 1)
        fin = sig("fin", 0)
        fg_in = sig("fg_in", 0)
        out_written = sig("out_written", 0)

        block = ctx.enter_context(nc.Block())

        def settled(eng):
            eng.drain()

        def half(buf, n, h, width=512):
            return buf[:, n % buf.shape[1], h * width:(h + 1) * width]

        def lo_count(n, h):
            if n < Q0:
                return lo_pool, 2 * n + h + 1
            return lo_dve, 2 * (n - Q0) + h + 1

        LO_U = 2 * (U0 - Q0 - EARLY)
        LO_V = 2 * (V0 - Q0 - EARLY)
        LO_E = 2 * Q0

        @block.sync
        def _(sp):
            def load_params(layer):
                sp.dma_start(pv[:, :], pvec[layer, :, :]).then_inc(params_in.sem, 16)
                sp.dma_start(fc, cfilter[:, :]).then_inc(params_in.sem, 16)
                sp.dma_start(fm[:, 0:704], pmat[layer, :, 0:704]).then_inc(params_in.sem, 16)
                sp.dma_start(fm[:, 704:1408], pmat[layer, :, 704:1408]).then_inc(params_in.sem, 16)
                sp.dma_start(dft, cdft[:, :]).then_inc(dft_in.sem, 16)
                sp.dma_start(gqk, gain_qk[layer, :, :]).then_inc(gqk_in.sem, 16)

            def load_channels(layer, k):
                sp.dma_start(raw[:, k % 4, :], w_proj[layer, k * P:(k + 1) * P, 0:D])\
                  .then_inc(raw_in[k % 4].sem, 16)

            sp.dma_start(x[:, :, :], x_in.rearrange("(b p) d -> p b d", p=P)).then_inc(x_landed.sem, 16)
            sp.dma_start(kc[:, :], kconst[:, :]).then_inc(const_in.sem, 16)
            load_params(0)
            for k in range(4):
                load_channels(0, k)
            with sp.Fori(0, DEPTH) as l:
                following = (l + 1) % DEPTH

                def slot_free(n):
                    signal, count = lo_count(n - 4, 1)
                    sp.wait_ge(*at(signal, l, count))

                for k in range(4, DT):
                    slot_free(A0 + k)
                    load_channels(l, k)
                for k in range(DT):
                    slot_free(B0 + k)
                    sp.dma_start(raw[:, k % 4, 0:QKV], w_proj[l, k * P:(k + 1) * P, D:D + QKV]).then_inc(raw_in[k % 4].sem, 16)
                for n, c in enumerate(OUT_ORDER):
                    slot_free(O0 + n)
                    sp.dma_start(raw[:, n % 4, :], w_proj[l, c * P:(c + 1) * P, IN_COLS:IN_COLS + D]).then_inc(raw_in[n % 4].sem, 16)
                for n in range(16):
                    slot_free(Q0 + n)
                    if n == 4:
                        sp.wait_ge(*at(hyena_done, l, 2))
                        sp.dma_start(subk, sub_keys[l, :, :]).then_inc(subk_in.sem, 16)
                    k, c = n // 2, n % 2
                    sp.dma_start(raw[:, n % 4, :], w_proj[l, k * P:(k + 1) * P, IN_COLS + (c + 1) * D:IN_COLS + (c + 2) * D])\
                      .then_inc(raw_in[n % 4].sem, 16)
                for n in range(4):
                    slot_free(U0 + n)
                    sp.dma_start(raw[:, n, :], tab_u[l, n, :, :]).then_inc(raw_in[n].sem, 16)

                def stream(i, table, signal, offset):
                    for s in range(4):
                        j = i * 4 + s
                        sp.wait_ge(*at(signal, l, j * 2 + offset - 6))
                        sp.dma_start(raw[:, s, :], table[l, j, :, :]).then_inc(raw_in[s].sem, 16)

                with sp.Fori(1, EARLY // 4 + 1) as i:
                    stream(i, tab_u, lo_pool, LO_E)
                with sp.Fori(EARLY // 4 + 1, 32) as i:
                    stream(i, tab_u, lo_dve, LO_U)
                with sp.Fori(0, 12) as i:
                    stream(i, tab_v, lo_dve, LO_V)
                sp.wait_ge(*at(whi_done, l, LOADED_AHEAD // SEQ + 1))
                sp.wait_ge(*at(wlo_done, l, LOADED_AHEAD // SEQ + 1))
                load_params(following)
                with sp.Fori(12, 32) as i:
                    stream(i, tab_v, lo_dve, LO_V)
                for k in range(4):
                    sp.wait_ge(*at(lo_dve, l, LO_DVE + 2 * (k - 3)))
                    load_channels(following, k)
            sp.wait_ge(layer_done.sem, DEPTH + 1)
            sp.dma_start(area(8192, D), final_g[:, :]).then_inc(fg_in.sem, 16)
            sp.wait_ge(fin.sem, 1)
            sp.dma_start(out.rearrange("(b p) d -> p b d", p=P), xn).then_inc(out_written.sem, 16)
            sp.wait_ge(out_written.sem, 16)
            sp.wait_ge(params_in.sem, (DEPTH + 1) * 64)
            sp.wait_ge(dft_in.sem, (DEPTH + 1) * 16)
            sp.wait_ge(gqk_in.sem, (DEPTH + 1) * 16)
            for s in range(4):
                sp.wait_ge(raw_in[s].sem, DEPTH * raw_in[s].per_layer + 16)

        @block.tensor
        def _(pe):
            mm, tr = nc.tensor.matmul, nc.tensor.transpose
            pe.wait_ge(const_in.sem, 16)
            with pe.Fori(0, DEPTH) as l:
                def in_halves(n, h):
                    pe.wait_ge(*at(hi_done, l, 2 * n + h + 1))
                    signal, count = lo_count(n, h)
                    pe.wait_ge(*at(signal, l, count))

                pe.wait_ge(layer_done.sem, l + 1)
                pe.wait_ge(*at(params_in, l, 64))
                mm(ps[0:64, 0, 0:256], fm[0:17, PM["w1"]:PM["w1"] + 64], fc[0:17, CF["z"]:CF["z"] + 256],
                   start=True, stop=True).then_inc(mlp_ready.sem, 1)

                def transpose_x(done):
                    pe.wait_ge(*at(xn_done, l, done))
                    for k in range(DT):
                        for b in range(TB):
                            last = tr(ps[:, 4 + k // 2, (k % 2) * 256 + b * P:(k % 2) * 256 + (b + 1) * P],
                                      xn[:, b, k * P:(k + 1) * P], ident)
                        if k % 2:
                            last.then_inc(xT_ready.sem, 1)

                def channels(k):
                    for h in range(2):
                        in_halves(A0 + k, h)
                        for c in range(4 * h, 4 * h + 4):
                            bank = ps[:, c // 2, (c % 2) * 256:(c % 2) * 256 + 256]
                            col = slice((c % 4) * P, (c % 4 + 1) * P)
                            hi, lo = half(tab_hi, A0 + k, h)[:, col], half(tab_lo, A0 + k, h)[:, col]
                            mm(bank, hi, x_lo[:, k, :], start=(k == 0 and c % 2 == 0), stop=False,
                               skip_group_check=True)
                            mm(bank, hi, x_hi[:, k, :], start=False, stop=False, skip_group_check=True)
                            last = mm(bank, lo, x_hi[:, k, :], start=False, stop=(k == DT - 1), skip_group_check=True)
                        last.then_inc(half_used.sem, 1)

                transpose_x(2)
                pe.wait_ge(*at(h_hi, l, 8))
                pe.wait_ge(*at(h_lo, l, 8))
                pe.wait_ge(*at(sine_arg, l, 1))
                channels(0)
                pe.wait_ge(*at(sine_done, l, 1))
                mm(ps[:, 4, 0:256], fm[0:64, PM["w2"]:PM["w2"] + P], f_h1,
                   start=True, stop=True).then_inc(mlp_ready.sem, 1)
                channels(1)
                channels(2)
                pe.wait_ge(*at(sine_done, l, 2))
                for b in range(TB):
                    for n in range(2):
                        last = mm(ps[:, (6, 4)[b] + n, :], f_h2[:, b * P:(b + 1) * P],
                                  fm[0:64, PM["w3"] + n * 512:PM["w3"] + (n + 1) * 512], start=True, stop=True)
                    last.then_inc(taps_ready.sem, 1)
                channels(3)
                channels(4)
                pe.wait_ge(*at(filt_sq_done, l, 1))
                for b in range(TB):
                    for e in range(2):
                        last = mm(ps[:, 6, :], ones, filt_sq[:, b, :, e, :], start=(b + e == 0), stop=(b + e == 2))
                last.then_inc(f_norm_ready.sem, 1)
                channels(5)
                pe.wait_ge(*at(sumdif_done, l, 1))
                pe.wait_ge(*at(dft_in, l, 16))
                for n, (m, c, src, bank) in enumerate((
                        (mat("cos"), 0, f_sum, 4), (mat("cos"), P, f_sum, 5), (sin0, 0, f_dif, 7),
                        (sin0, P, f_dif, 6), (cosn, 0, f_sum, 4))):
                    if n == 3:
                        pe.wait_ge(*at(f_root_done, l, 1))
                    if n == 4:
                        channels(6)
                        channels(7)
                        pe.wait_ge(*at(spec_done, l, 1))
                    for b in range(TB):
                        last = mm(ps[:, bank, :], m[:, b, c:c + P], src[:, b, :, :], start=(b == 0), stop=(b == 1))
                    last.then_inc(spec_ready.sem, 1)
                pe.wait_ge(*at(spec_done, l, 2))
                for n, name in enumerate(("bc", "bs")):
                    last = mm(ps[:, 5, n * 256:(n + 1) * 256], fc[:, CF[name]:CF[name] + P],
                              fm[:, PM["fw"]:PM["fw"] + 256], start=True, stop=True)
                last.then_inc(fn_m_ready.sem, 1)
                pe.wait_ge(*at(spec_done, l, 5))
                pe.wait_ge(*at(fn_m_done, l, 1))
                for k in range(DT):
                    for h in range(2):
                        in_halves(B0 + k, h)
                        hi, lo = half(tab_hi, B0 + k, h, 384), half(tab_lo, B0 + k, h, 384)
                        for b in range(TB):
                            tok = slice(b * P, (b + 1) * P)
                            bank = ps[:, 4 + 2 * b + h, 0:384]
                            mm(bank, x_hi[:, k, tok], lo, start=(k == 0), stop=False)
                            mm(bank, x_hi[:, k, tok], hi, start=False, stop=False)
                            last = mm(bank, x_lo[:, k, tok], hi, start=False, stop=(k == DT - 1))
                        last.then_inc(half_used.sem, 1)

                def hyena_forward(o):
                    if o == 0:
                        pe.wait_ge(*at(conv_done, l, 1))
                        pe.wait_ge(*at(chan_done, l, 4))
                    else:
                        pe.wait_ge(*at(hyena_done, l, 1))
                    for b in range(TB):
                        for c in range(2):
                            last = tr(ps[:, 0, b * 256 + c * P:b * 256 + (c + 1) * P],
                                      conv[:, c, b * P:(b + 1) * P], ident)
                    last.then_inc(zT_ready.sem, 1)
                    pe.wait_ge(*at(zT_done, l, o + 1))
                    for n, name in enumerate(("cos", "sin")):
                        for f in range(2):
                            for b in range(TB):
                                last = mm(ps[:, 1 + n, f * 256:(f + 1) * 256], mat(name)[:, b, f * P:(f + 1) * P],
                                          z_t[:, b, :], start=(b == 0), stop=(b == 1))
                    last.then_inc(u_spec_ready.sem, 1)

                def hyena_inverse(o):
                    pe.wait_ge(*at(y_spec_done, l, o + 1))
                    for c in range(2):
                        for n, name in enumerate(("icos", "isin")):
                            for f in range(2):
                                last = mm(ps[:, 0, c * 256:(c + 1) * 256], y_spec[:, n, f, c * P:(c + 1) * P],
                                          mat(name)[:, f, :], start=(n + f == 0), stop=(n + f == 2))
                    last.then_inc(y_ready.sem, 1)

                hyena_forward(0)
                for b in range(TB):
                    for q in range(2):
                        last = mm(ps[:, (3, 0)[b], q * 256:(q + 1) * 256], fn_u[:, q, b * P:(b + 1) * P],
                                  fn_m[:, :, q, :], start=True, stop=True)
                    last.then_inc(fn1_ready.sem, 1)
                pe.wait_ge(*at(fn1_done, l, 2))
                for q in range(2):
                    for b in range(TB):
                        for n, name in enumerate(("fc", "fs")):
                            last = mm(ps[:, 3, q * 256:(q + 1) * 256], fn_p[:, b, q, n, :], mat(name)[:, b, :],
                                      start=(b + n == 0), stop=(b + n == 2))
                last.then_inc(fn2_ready.sem, 1)
                pe.wait_ge(*at(qkv_done, l, 4))
                pe.wait_ge(*at(qk_sq, l, 4))
                pe.wait_ge(*at(rope_done, l, 1))
                rope4 = rope.rearrange("p (b h d) -> p b h d", b=TB, h=10)
                for g in range(3):
                    for k in range(2):
                        for b in range(TB):
                            if g < 2:
                                src = rope4[:, b, 4 * g + 2 * k:4 * g + 2 * k + 2, :].rearrange("p h d -> p (h d)")
                            else:
                                src = k_twice[:, b, k, :, :].rearrange("p e d -> p (e d)")
                            last = tr(ps[:, 4 + g, k * 256 + b * P:k * 256 + (b + 1) * P], src, ident)
                    last.then_inc(qkT_ready.sem, 1)

                def attention_scores(u):
                    if u < 2:
                        pe.wait_ge(*at(qkT_done, l, 3))
                    else:
                        pe.wait_ge(*at(pT_act, l, u - 1))
                        pe.wait_ge(*at(pT_dve, l, u - 1))
                    b, base = u // 2, 64 * (u % 2)
                    for s in range(4):
                        last = mm(ps[:, 4 + 2 * (u % 2) + s // 2, (s % 2) * 256:(s % 2) * 256 + 256],
                                  q_t[base:base + 64, s, b * P:(b + 1) * P], k_t[base:base + 64, s // 2, :],
                                  start=True, stop=True)
                    last.then_inc(att_ready.sem, 1)

                def attention_transposes(u):
                    pe.wait_ge(*at(probs_done, l, u + 1))
                    for kb in range(TB):
                        for s in range(4):
                            last = tr(ps[:, 4 + 2 * (u % 2) + kb, s * P:(s + 1) * P],
                                      probs[:, u % 2, s, kb * P:(kb + 1) * P], ident)
                    last.then_inc(pT_ready.sem, 1)

                def attention_values(u):
                    pe.wait_ge(*at(pT_act, l, u + 1))
                    pe.wait_ge(*at(pT_dve, l, u + 1))
                    b, base = u // 2, 64 * (u % 2)
                    if u == 0:
                        pe.wait_ge(*at(fn2_done, l, 1))
                    if u == 2:
                        pe.wait_ge(*at(mix_lo, l, 2))
                        pe.wait_ge(*at(attn_sq, l, 1))
                    for s in range(4):
                        v_col = A_W + KV_W + (s // 2) * HEAD
                        for kb in range(TB):
                            last = mm(ps[base:base + 64, 3, s * P:(s + 1) * P],
                                      p_qkv[:, kb, v_col:v_col + HEAD], probs_t[:, u, kb, s, :],
                                      start=(kb == 0), stop=(kb == 1))
                    last.then_inc(attn_ready.sem, 1)

                attention_scores(0)
                hyena_inverse(0)
                attention_scores(1)
                attention_transposes(0)
                hyena_forward(1)
                attention_values(0)
                attention_scores(2)
                attention_transposes(1)
                attention_values(1)
                attention_scores(3)
                hyena_inverse(1)
                attention_transposes(2)
                attention_values(2)
                attention_transposes(3)
                attention_values(3)
                groups = ((0, 4), (4, 6), (6, 8))
                pe.wait_ge(*at(attn_sq, l, 2))
                pe.wait_ge(*at(hyena_sq, l, 1))
                for g, (c0, c1) in enumerate(groups):
                    for b in range(TB):
                        for c in range(c0, c1):
                            last = mm(ps[:, 7, 2 * g + b:2 * g + b + 1], mixed_sq[:, c, b * P:(b + 1) * P],
                                      ones[:, 0:1], start=(c == c0), stop=(c == c1 - 1))
                last.then_inc(group_ready.sem, 1)
                pe.wait_ge(*at(mix_hi, l, 4))
                pe.wait_ge(*at(mix_lo, l, 4))
                for n, c in enumerate(OUT_ORDER):
                    if n == 2:
                        pe.wait_ge(*at(mean_sq, l, 3))
                    if n == 4:
                        pe.wait_ge(*at(out_added, l, 2))
                    first, final = n in (0, 2, 4), n in (1, 3, 7)
                    for h in range(2):
                        in_halves(O0 + n, h)
                        hi, lo = half(tab_hi, O0 + n, h), half(tab_lo, O0 + n, h)
                        for b in range(TB):
                            tok = slice(b * P, (b + 1) * P)
                            bank = ps[:, (4 if n in (2, 3) else 0) + 2 * b + h, :]
                            mm(bank, x_hi[:, c, tok], lo, start=first, stop=False)
                            mm(bank, x_hi[:, c, tok], hi, start=False, stop=False)
                            last = mm(bank, x_lo[:, c, tok], hi, start=False, stop=final)
                        last.then_inc(half_used.sem, 1)
                transpose_x(4)
                pe.wait_ge(*at(h_hi, l, 16))
                pe.wait_ge(*at(h_lo, l, 16))
                for n in range(16):
                    k, part = n // 2, n % 2
                    for h in range(2):
                        in_halves(Q0 + n, h)
                        for c in range(4):
                            tile = part * 8 + h * 4 + c
                            bank = ps[:, tile // 2, (tile % 2) * 256:(tile % 2) * 256 + 256]
                            col = slice(c * P, (c + 1) * P)
                            hi, lo = half(tab_hi, Q0 + n, h)[:, col], half(tab_lo, Q0 + n, h)[:, col]
                            mm(bank, hi, x_lo[:, k, :], start=(k == 0 and c % 2 == 0), stop=False,
                               skip_group_check=True)
                            mm(bank, hi, x_hi[:, k, :], start=False, stop=False, skip_group_check=True)
                            last = mm(bank, lo, x_hi[:, k, :], start=False, stop=(k == DT - 1), skip_group_check=True)
                        last.then_inc(half_used.sem, 1)
                pe.wait_ge(*at(subk_in, l, 16))
                pe.wait_ge(*at(query_act, l, 4))
                pe.wait_ge(*at(query_dve, l, 4))
                for b in range(TB):
                    for c in range(HP):
                        last = mm(ps[:, 4 * b + c // 4, (c % 4) * P:(c % 4 + 1) * P],
                                  query_t[:, c, b * P:(b + 1) * P], subk[:, c, :], start=True, stop=True)
                        if c % 4 == 3:
                            last.then_inc(scores_ready.sem, 1)
                pe.wait_ge(*at(scores_dve, l, 2))

                def u_product(i, first, signal, offset):
                    for s in range(4):
                        j = i * 4 + s
                        if s % 2 == 0 and not first:
                            pe.wait_ge(*at(gelu_done, l, i * 2 + s // 2 - 1))
                        bank = ps[:, s // 2, (s % 2) * 256:(s % 2) * 256 + 256]
                        for h in range(2):
                            pe.wait_ge(*at(hi_done, l, j * 2 + 2 * U0 + h + 1))
                            pe.wait_ge(*at(signal, l, j * 2 + offset + h + 1))
                            for k in range(4):
                                col = slice(k * P, (k + 1) * P)
                                hi, lo = half(tab_hi, s, h)[:, col], half(tab_lo, s, h)[:, col]
                                mm(bank, hi, x_lo[:, 4 * h + k, :], start=(h + k == 0), stop=False)
                                mm(bank, hi, x_hi[:, 4 * h + k, :], start=False, stop=False)
                                last = mm(bank, lo, x_hi[:, 4 * h + k, :], start=False, stop=(h + k == 4))
                            last.then_inc(half_used.sem, 1)

                u_product(0, True, lo_pool, LO_E)
                with pe.Fori(1, EARLY // 4) as i:
                    u_product(i, False, lo_pool, LO_E)
                with pe.Fori(EARLY // 4, 32) as i:
                    u_product(i, False, lo_dve, LO_U)
                pe.wait_ge(*at(topk_done, l, 1))
                for n in range(3):
                    for b in range(TB):
                        last = tr(ps[:, 4 + n // 2, (n % 2) * 256 + b * P:(n % 2) * 256 + (b + 1) * P],
                                  chosen[:, n, b, :], ident)
                last.then_inc(picksT_ready.sem, 1)
                def gates(i, first):
                    for s in range(4):
                        n = i * 4 + s
                        pe.wait_ge(*at(hot_scaled, l, n + 1))
                        if s < 3:
                            pe.wait_ge(*at(hot_j_act, l, i * 3 + s + 1))
                        else:
                            pe.wait_ge(*at(hot_j_dve, l, i + 1))
                        if s >= 2 or not first:
                            pe.wait_ge(*at(weighted, l, n - 1))
                        for t in range(4):
                            last = mm(ps[:, 2 + s % 2, t * P:(t + 1) * P], onehot[:, s % 2, 0, t, :],
                                      onehot[:, s % 2, 1, t, :], start=True, stop=True)
                        last.then_inc(gates_ready.sem, 1)

                gates(0, True)
                with pe.Fori(1, 16) as i:
                    gates(i, False)
                pe.wait_ge(*at(picksT_done, l, 2))

                def v_product(i, first, final):
                    for s in range(4):
                        j = i * 4 + s
                        pe.wait_ge(*at(whi_done, l, j + 1))
                        pe.wait_ge(*at(wlo_done, l, j + 1))
                        for h in range(2):
                            pe.wait_ge(*at(hi_done, l, j * 2 + 2 * V0 + h + 1))
                            pe.wait_ge(*at(lo_dve, l, j * 2 + LO_V + h + 1))
                            hi, lo = half(tab_hi, s, h), half(tab_lo, s, h)
                            for b in range(TB):
                                tok = slice(b * P, (b + 1) * P)
                                bank = ps[:, 4 + 2 * b + h, :]
                                mm(bank, w_hi[:, s % 2, tok], lo, start=(first and s == 0), stop=False,
                                   skip_group_check=True)
                                mm(bank, w_hi[:, s % 2, tok], hi, start=False, stop=False, skip_group_check=True)
                                last = mm(bank, w_lo[:, s % 2, tok], hi, start=False, stop=(final and s == 3),
                                          skip_group_check=True)
                            last.then_inc(half_used.sem, 1)

                v_product(0, True, False)
                with pe.Fori(1, 31) as i:
                    v_product(i, False, False)
                v_product(31, False, True)

        @block.scalar
        def _(act):
            fn = nc.scalar.activation
            act.wait_ge(x_landed.sem, 16)
            with act.Fori(0, DEPTH) as l:
                def upper(n, h, width=512):
                    if n >= 2:
                        act.wait_ge(*at(half_used, l, 2 * n + h - 3))
                    if h == 0:
                        act.wait_ge(*at(raw_in[n % 4], l, 16 * (n // 4 + 1)))
                    fn(half(tab_hi, n, h, width), half(raw, n, h, width), ACT.Copy).then_inc(hi_done.sem, 1)

                def square_sums():
                    for b in range(TB):
                        fn(x_lo[:, b * 4:(b + 1) * 4, :], x[:, b, :].rearrange("p (k t) -> p k t", k=4), ACT.Square,
                           accum_out=ss[:, b:b + 1]).then_inc(sq_sum.sem, 1)

                def transposed_upper(gain, ready):
                    for k in range(DT):
                        if k % 2 == 0:
                            act.wait_ge(*at(xT_ready, l, ready + k // 2 + 1))
                        fn(x_hi[:, k, :], ps[:, 4 + k // 2, (k % 2) * 256:(k % 2) * 256 + 256], ACT.Copy,
                           scale=par(gain, k)).then_inc(h_hi.sem, 1)

                act.wait_ge(layer_done.sem, l + 1)
                square_sums()
                upper(0, 0)
                upper(0, 1)
                upper(1, 0)
                upper(1, 1)
                act.wait_ge(*at(params_in, l, 64))
                transposed_upper("g1", 0)
                act.wait_ge(*at(sine_arg, l, 1))
                fn(f_h1, arg, ACT.Sin).then_inc(sine_done.sem, 1)
                upper(2, 0)
                upper(2, 1)
                act.wait_ge(*at(sine_arg, l, 2))
                fn(f_h2, arg, ACT.Sin).then_inc(sine_done.sem, 1)
                for n in (3, 4):
                    upper(n, 0)
                    upper(n, 1)
                act.wait_ge(*at(filt_done, l, 2))
                fn(filt_sq, filt, ACT.Square).then_inc(filt_sq_done.sem, 1)
                upper(5, 0)
                upper(5, 1)
                upper(6, 0)
                upper(6, 1)
                act.wait_ge(*at(f_norm_ready, l, 1))
                fn(f_rn, ps[:, 6, :], ACT.Sqrt, bias=EPS).then_inc(f_root_done.sem, 1)
                upper(7, 0)
                upper(7, 1)
                for n in (8, 9):
                    upper(n, 0, 384)
                    upper(n, 1, 384)
                act.wait_ge(*at(half_used, l, 2 * (A0 + DT)))
                for g in range(3):
                    fn(p_t[:, 2 * g:2 * g + 2, 1:257], ps[:, g, :].rearrange("p (k t) -> p k t", k=2),
                       ACT.Copy).then_inc(chan_done.sem, 1)
                fn(fn_u, ps[:, 3, :].rearrange("p (k t) -> p k t", k=2), ACT.Copy).then_inc(chan_done.sem, 1)
                act.wait_ge(*at(pad_done, l, 1))
                act.wait_ge(*at(chan_done, l, 3))
                act.wait_ge(*at(spec_ready, l, 5))
                for c in range(6):
                    fn(conv[:, c, :], p_t[:, c, 0:256], ACT.Identity, scale=par("cw", c), bias=par("cb", c))
                    fn(tap1[:, c, :], p_t[:, c, 1:257], ACT.Copy, scale=par("cw", 6 + c))
                    last = fn(tap2[:, c, :], p_t[:, c, 2:258], ACT.Copy, scale=par("cw", 12 + c))
                    if c == 5:
                        last.then_inc(conv_taps.sem, 1)
                    upper(10 + c, 0, 384)
                    upper(10 + c, 1, 384)
                for n, cols in enumerate((384, 256, 384, 256)):
                    start = (n // 2) * 640 + (n % 2) * 384
                    act.wait_ge(*at(qkv_done, l, n + 1))
                    fn(rope[:, start:start + cols], p_qkv[:, n // 2, (n % 2) * 384:(n % 2) * 384 + cols],
                       ACT.Square).then_inc(qk_sq.sem, 1)

                def z_transposed(o):
                    act.wait_ge(*at(zT_ready, l, o + 1))
                    fn(z_t, ps[:, 0, :].rearrange("p (b c) -> p b c", b=TB), ACT.Copy).then_inc(zT_done.sem, 1)

                def exponentials(u):
                    act.wait_ge(*at(max_done, l, u + 1))
                    g = u % 2
                    for s in range(4):
                        last = fn(probs[:, g, s, :],
                                  ps[:, 4 + 2 * g + s // 2, (s % 2) * 256:(s % 2) * 256 + 256], ACT.Exp,
                                  bias=nmx[:, 4 * g + s:4 * g + s + 1], scale=HEAD ** -0.5,
                                  accum_out=rs[:, 4 * g + s:4 * g + s + 1])
                    last.then_inc(exp_done.sem, 1)

                def probs_transposed(u):
                    act.wait_ge(*at(pT_ready, l, u + 1))
                    fn(probs_t[:, u, 0, :, :], ps[:, 4 + 2 * (u % 2), :].rearrange("p (s q) -> p s q", q=P),
                       ACT.Copy).then_inc(pT_act.sem, 1)

                def attention_out(b):
                    act.wait_ge(*at(attn_ready, l, 2 * b + 2))
                    fn(mixed_sq[:, 0:4, b * P:(b + 1) * P], ps[:, 3, :].rearrange("p (k q) -> p k q", k=4),
                       ACT.Square).then_inc(attn_sq.sem, 1)
                    for k in range(4):
                        last = fn(x_hi[:, k, b * P:(b + 1) * P], ps[:, 3, k * P:(k + 1) * P], ACT.Copy,
                                  scale=par("gm", k))
                    last.then_inc(mix_hi.sem, 1)

                for h in range(2):
                    upper(O0, h)
                z_transposed(0)
                for b in range(TB):
                    act.wait_ge(*at(fn1_ready, l, b + 1))
                    fn(fn_p[:, b, :, :, :], ps[:, (3, 0)[b], :].rearrange("p (q m c) -> p q m c", q=2, m=2),
                       ACT.Copy).then_inc(fn1_done.sem, 1)
                act.wait_ge(*at(fn2_ready, l, 1))
                for q in range(2):
                    last = fn(fn_u[:, q, :], ps[:, 3, q * 256:(q + 1) * 256], ACT.Identity, bias=par("fb", q))
                last.then_inc(fn2_done.sem, 1)
                for g in range(3):
                    dst = (q_t[:, 0:2, :], q_t[:, 2:4, :], k_t)[g]
                    act.wait_ge(*at(qkT_ready, l, g + 1))
                    fn(dst, ps[:, 4 + g, :].rearrange("p (k t) -> p k t", k=2), ACT.Copy).then_inc(qkT_done.sem, 1)
                act.wait_ge(*at(fn2_done, l, 1))
                for q in range(2):
                    last = fn(x_hi[:, 6 + q, :], fn_u[:, q, :], ACT.Copy, scale=par("gm", 6 + q))
                last.then_inc(mix_hi.sem, 1)
                exponentials(0)
                fn(mixed_sq[:, 6:8, :], fn_u, ACT.Square)
                exponentials(1)
                probs_transposed(0)
                z_transposed(1)
                probs_transposed(1)
                exponentials(2)
                attention_out(0)
                exponentials(3)
                act.wait_ge(*at(hyena_done, l, 2))
                for q in range(2):
                    last = fn(x_hi[:, 4 + q, :], conv[:, q, :], ACT.Copy, scale=par("gm", 4 + q))
                last.then_inc(mix_hi.sem, 1)
                fn(mixed_sq[:, 4:6, :], conv[:, 0:2, :], ACT.Square).then_inc(hyena_sq.sem, 1)
                probs_transposed(2)
                probs_transposed(3)
                attention_out(1)
                for n in range(O0 + 1, Q0):
                    upper(n, 0)
                    upper(n, 1)
                upper(Q0, 0)
                upper(Q0, 1)
                act.wait_ge(*at(half_used, l, 2 * Q0))
                for b in range(TB):
                    act.wait_ge(*at(out_added, l, 4 + b + 1))
                    fn(x_lo[:, b * 4:(b + 1) * 4, :], x[:, b, :].rearrange("p (k t) -> p k t", k=4), ACT.Square,
                       accum_out=ss[:, b:b + 1]).then_inc(sq_sum.sem, 1)
                upper(Q0 + 1, 0)
                upper(Q0 + 1, 1)
                transposed_upper("g2", 4)
                for n in range(Q0 + 2, U0):
                    upper(n, 0)
                    upper(n, 1)
                upper(U0, 0)
                upper(U0, 1)
                act.wait_ge(*at(half_used, l, 2 * U0))
                for g in range(4):
                    fn(query_t[:, 2 * g:2 * g + 2, :], ps[:, g, :].rearrange("p (k t) -> p k t", k=2),
                       ACT.Copy).then_inc(query_act.sem, 1)
                upper(U0 + 1, 0)
                upper(U0 + 1, 1)
                for g in range(4):
                    act.wait_ge(*at(scores_ready, l, 4 + g + 1))
                    fn(scores[:, 1, 4 * g:4 * g + 4, :], ps[:, 4 + g, :].rearrange("p (k n) -> p k n", k=4),
                       ACT.Copy).then_inc(scores_act.sem, 1)

                def u_upper(i, s):
                    for h in range(2):
                        act.wait_ge(*at(half_used, l, i * 8 + 2 * (U0 + s) + h - 3))
                        if h == 0:
                            act.wait_ge(*at(raw_in[s], l, i * 16 + 16 * (U0 // 4 + 1)))
                        fn(half(tab_hi, s, h), half(raw, s, h), ACT.Copy).then_inc(hi_done.sem, 1)

                def gelu(n, bank):
                    act.wait_ge(*at(half_used, l, n * 4 + 2 * U0 + 4))
                    fn(work[:, bass.ds(2 * n, 2), :], ps[:, bank, :].rearrange("p (k t) -> p k t", k=2),
                       ACT.Gelu).then_inc(gelu_done.sem, 1)

                def u_quad(i):
                    u_upper(i, 0)
                    u_upper(i, 1)
                    gelu(i * 2 - 1, 1)
                    u_upper(i, 2)
                    u_upper(i, 3)
                    gelu(i * 2, 0)

                u_upper(0, 2)
                u_upper(0, 3)
                gelu(0, 0)
                with act.Fori(1, 8) as i:
                    u_quad(i)
                act.wait_ge(*at(best_done, l, 1))
                fn(best.rearrange("p b h n -> p (b h n)"), best.rearrange("p b h n -> p (b h n)"),
                   ACT.Exp).then_inc(gate_exp.sem, 1)
                u_quad(8)
                with act.Fori(9, GUARD // 4) as i:
                    u_quad(i)
                act.wait_ge(*at(topk_done, l, 1))
                with act.Fori(GUARD // 4, 32) as i:
                    u_quad(i)
                gelu(63, 1)

                def absolute(i, s, first=False):
                    if not first:
                        act.wait_ge(*at(hot_j_act, l, i * 3 + s - 2))
                    for t in range(4):
                        last = fn(dist_abs[:, s, t, :], iota, ACT.Abs, bias=minus_j[:, bass.ds(i * 16 + 4 * s + t, 1)])
                    last.then_inc(abs_done.sem, 1)

                def one_hot_j(i, s, first=False):
                    if not first:
                        act.wait_ge(*at(gates_ready, l, i * 4 + s - 1))
                    act.wait_ge(*at(abs_done, l, i * 3 + s + 1))
                    fn(onehot[:, s % 2, 1, :, :], dist_abs[:, s, :, :].bitcast(F32), ACT.Relu, scale=-1.0, bias=1.0)\
                        .then_inc(hot_j_act.sem, 1)

                act.wait_ge(*at(picksT_done, l, 2))
                fn(minus_j, picks[:, 1, :], ACT.Copy, scale=-1.0).then_inc(minus_done.sem, 1)
                act.wait_ge(*at(minus_done, l, 1))
                for s in range(3):
                    absolute(0, s, True)
                    one_hot_j(0, s, s < 2)
                with act.Fori(1, 16) as i:
                    for s in range(3):
                        absolute(i, s)
                        one_hot_j(i, s)

                def v_quad(i):
                    for s in range(4):
                        for h in range(2):
                            act.wait_ge(*at(half_used, l, i * 8 + 2 * (V0 + s) + h - 3))
                            if h == 0:
                                act.wait_ge(*at(raw_in[s], l, i * 16 + 16 * (V0 // 4 + 1)))
                            else:
                                fn(w_hi[:, s % 2, :], work[:, i * 4 + s, :], ACT.Copy).then_inc(whi_done.sem, 1)
                            fn(half(tab_hi, s, h), half(raw, s, h), ACT.Copy).then_inc(hi_done.sem, 1)

                act.wait_ge(*at(weighted, l, 64))
                with act.Fori(0, 32) as i:
                    v_quad(i)
            act.wait_ge(layer_done.sem, DEPTH + 1)
            for b in range(TB):
                fn(x_lo[:, b * 4:(b + 1) * 4, :], x[:, b, :].rearrange("p (k t) -> p k t", k=4), ACT.Square,
                   accum_out=ss[:, b:b + 1]).then_inc(sq_sum.sem, 1)

        @block.gpsimd
        def _(pool):
            tt = nc.gpsimd.tensor_tensor
            pool.wait_ge(const_in.sem, 16)
            with pool.Fori(0, DEPTH) as l:
                def inverse_root(n, dst, src, width):
                    pool.wait_ge(*at(mean_sq, l, n))
                    tt(dst, src, neg_half.broadcast_to([P, width]), ALU.pow).then_inc(inv_root.sem, 1)

                def lower(n, h, width=512):
                    if n >= 2:
                        pool.wait_ge(*at(half_used, l, 2 * n + h - 3))
                    pool.wait_ge(*at(hi_done, l, 2 * n + h + 1))
                    tt(half(tab_lo, n, h, width), half(raw, n, h, width), half(tab_hi, n, h, width).bitcast(F32),
                       ALU.subtract).then_inc(lo_pool.sem, 1)

                pool.wait_ge(layer_done.sem, l + 1)
                inverse_root(1, rinv, ms, 2)
                for n in range(A0, B0):
                    lower(n, 0)
                    lower(n, 1)
                pool.wait_ge(*at(gqk_in, l, 16))
                g5 = gqk.rearrange("p (h a e d) -> p h a e d", h=10, a=2, e=2)
                for b in range(TB):
                    tt(cos_g[:, b, :].rearrange("p (h d) -> p h d", d=HEAD), gqk.rearrange("p (h d) -> p h d", d=HEAD),
                       cos_r[:, b:b + 1, :].broadcast_to([P, 10, HEAD]), ALU.mult)
                    sins = sin_r[:, b:b + 1, :].rearrange("p o (a e d) -> p o a e d", a=2, e=2)
                    sing = sin_g[:, b, :].rearrange("p (h a e d) -> p h a e d", h=10, a=2, e=2)
                    for e in range(2):
                        last = tt(sing[:, :, :, e, :], g5[:, :, :, 1 - e, :],
                                  sins[:, :, :, e, :].broadcast_to([P, 10, 2, 16]), ALU.mult)
                last.then_inc(rope_tab_done.sem, 1)
                for n in range(B0, O0):
                    lower(n, 0, 384)
                    lower(n, 1, 384)
                pool.wait_ge(*at(conv_taps, l, 1))
                tt(conv, conv, tap1, ALU.add).then_inc(pool_step.sem, 1)
                pool.wait_ge(*at(pool_step, l, 1))
                tt(conv, conv, tap2, ALU.add).then_inc(conv_done.sem, 1)
                inverse_root(2, r20, ms20, 20)
                pool.wait_ge(*at(qn_done, l, 1))
                pool.wait_ge(*at(rope_tab_done, l, 1))
                rot5 = rot.rearrange("p (b h a e d) -> p b h a e d", b=TB, h=10, a=2, e=2)
                qn5 = qn.rearrange("p (b h a e d) -> p b h a e d", b=TB, h=10, a=2, e=2)
                for b in range(TB):
                    sing = sin_g[:, b, :].rearrange("p (h a e d) -> p h a e d", h=10, a=2, e=2)
                    for e in range(2):
                        last = tt(rot5[:, b, :, :, e, :], qn5[:, b, :, :, 1 - e, :], sing[:, :, :, e, :], ALU.mult)
                last.then_inc(rot_done.sem, 1)
                for n in range(O0, O0 + 2):
                    lower(n, 0)
                    lower(n, 1)
                inverse_root(3, r6, ms6, 6)
                for n in range(O0 + 2, Q0):
                    lower(n, 0)
                    lower(n, 1)
                inverse_root(4, rinv, ms, 2)

                def u_lower(i):
                    for s in range(4):
                        for h in range(2):
                            pool.wait_ge(*at(half_used, l, i * 8 + 2 * (U0 + s) + h - 3))
                            pool.wait_ge(*at(hi_done, l, i * 8 + 2 * (U0 + s) + h + 1))
                            tt(half(tab_lo, s, h), half(raw, s, h), half(tab_hi, s, h).bitcast(F32),
                               ALU.subtract).then_inc(lo_pool.sem, 1)

                with pool.Fori(0, EARLY // 4) as i:
                    u_lower(i)

                def scale_hot(i, first=False):
                    for s in range(4):
                        n = i * 4 + s
                        if s >= 2 or not first:
                            pool.wait_ge(*at(gates_ready, l, n - 1))
                        pool.wait_ge(*at(hot_i, l, n + 1))
                        tt(onehot[:, s % 2, 0, :, :], hot_rows[:, s, :, :].bitcast(F32),
                           picks[:, 2, bass.ds(n * 4, 4)].rearrange("p (t a) -> p t a", a=1).broadcast_to([P, 4, P]),
                           ALU.mult).then_inc(hot_scaled.sem, 1)

                scale_hot(0, True)
                with pool.Fori(1, 16) as i:
                    scale_hot(i)
            pool.wait_ge(mean_sq.sem, DEPTH * 4 + 1)
            tt(rinv, ms, neg_half.broadcast_to([P, 2]), ALU.pow).then_inc(inv_root.sem, 1)

        @block.vector
        def _(dve):
            v = nc.vector
            dve.wait_ge(x_landed.sem, 16)
            v.memset(small[:, 127:128], 0.0).then_inc(layer_done.sem, 1)
            dve.wait_ge(const_in.sem, 16)
            with dve.Fori(0, DEPTH) as l:
                count = [0]

                def link(ins):
                    count[0] += 1
                    ins.then_inc(dve_step.sem, 1)
                    dve.wait_ge(*at(dve_step, l, count[0]))

                def norm_scale(n):
                    dve.wait_ge(*at(sq_sum, l, 2 * n + 2))
                    v.tensor_scalar(ms, ss, 1.0 / D, EPS, ALU.mult, ALU.add).then_inc(mean_sq.sem, 1)
                    dve.wait_ge(*at(inv_root, l, (1, 4)[n]))
                    for b in range(TB):
                        v.tensor_scalar(xn[:, b, :], x[:, b, :], rinv[:, b:b + 1], None, ALU.mult)\
                            .then_inc(xn_done.sem, 1)

                def transposed_lower(gain, done):
                    for k in range(DT):
                        if k % 2 == 0:
                            dve.wait_ge(*at(h_hi, l, done + k + 2))
                        v.scalar_tensor_tensor(x_lo[:, k, :], ps[:, 4 + k // 2, (k % 2) * 256:(k % 2) * 256 + 256],
                                               par(gain, k), x_hi[:, k, :].bitcast(F32), ALU.mult, ALU.subtract)\
                            .then_inc(h_lo.sem, 1)

                def sine_argument(n, bank):
                    dve.wait_ge(*at(mlp_ready, l, n + 1))
                    link(v.tensor_scalar(arg, ps[0:64, bank, 0:256], par(("b1", "b2")[n], rows=64),
                                         par(("f1", "f2")[n], rows=64), ALU.add, ALU.mult))
                    link(v.tensor_scalar(turns, arg, INV_2PI, ROUND, ALU.mult, ALU.add))
                    link(v.tensor_scalar(turns, turns, ROUND, None, ALU.subtract))
                    for part in TWO_PI:
                        link(v.scalar_tensor_tensor(arg, turns, -part, arg, ALU.mult, ALU.add))
                    v.tensor_scalar(arg, arg, SIN_MAX, -SIN_MAX, ALU.min, ALU.max).then_inc(sine_arg.sem, 1)

                norm_scale(0)
                dve.wait_ge(*at(params_in, l, 64))
                sine_argument(0, 0)
                transposed_lower("g1", 0)
                dve.wait_ge(*at(sine_done, l, 1))
                sine_argument(1, 4)
                dve.wait_ge(*at(sine_done, l, 2))
                for b in range(TB):
                    dve.wait_ge(*at(taps_ready, l, b + 1))
                    bank = (6, 4)[b]
                    v.tensor_tensor(filt[:, b, :, :, :].rearrange("p o e c -> p (o e) c"),
                                    ps[:, bank:bank + 2, :].rearrange("p k (e c) -> p (k e) c", c=256),
                                    decay[:, b:b + 1, :].broadcast_to([P, 4, 256]), ALU.mult)\
                        .then_inc(filt_done.sem, 1)
                dve.wait_ge(*at(filt_done, l, 2))
                for b in range(TB):
                    mask = kc[:, KC["not_first"]:KC["not_first"] + 1] if b == 0 else 1.0
                    v.scalar_tensor_tensor(f_sum[:, b, :, :], filt[:, b, :, 1, :], mask, filt[:, b, :, 0, :],
                                           ALU.mult, ALU.add)
                    last = v.tensor_tensor(f_dif[:, b, :, :], filt[:, b, :, 1, :], filt[:, b, :, 0, :], ALU.subtract)
                last.then_inc(sumdif_done.sem, 1)
                dve.wait_ge(*at(f_root_done, l, 1))
                link(v.reciprocal(f_rn, f_rn))
                for n, bank in enumerate((4, 5, 7, 6, 4)):
                    dve.wait_ge(*at(spec_ready, l, n + 1))
                    v.tensor_tensor(spec[:, n, :, :].rearrange("p o c -> p (o c)"), ps[:, bank, :], f_rn, ALU.mult)\
                        .then_inc(spec_done.sem, 1)
                v.memset(p_t[:, :, 0:1], 0.0)
                v.memset(p_t[:, :, 257:258], 0.0).then_inc(pad_done.sem, 1)
                dve.wait_ge(*at(fn_m_ready, l, 1))
                v.tensor_copy(fn_m.rearrange("p m q c -> p (m q c)"), ps[:, 5, :]).then_inc(fn_m_done.sem, 1)
                dve.wait_ge(*at(half_used, l, 2 * (B0 + DT)))
                for n in range(4):
                    v.tensor_copy(p_qkv[:, n // 2, (n % 2) * 384:(n % 2) * 384 + 384], ps[:, 4 + n, 0:384])\
                        .then_inc(qkv_done.sem, 1)
                dve.wait_ge(*at(qk_sq, l, 4))
                rope3 = rope.rearrange("p (b n) -> p b n", b=TB)
                qn3 = qn.rearrange("p (b n) -> p b n", b=TB)
                link(v.tensor_reduce(ss20, rope.rearrange("p (n d) -> p n d", d=HEAD), AX.X, ALU.add))
                v.tensor_scalar(ms20, ss20, 1.0 / HEAD, EPS, ALU.mult, ALU.add).then_inc(mean_sq.sem, 1)
                dve.wait_ge(*at(qkv_done, l, 4))
                dve.wait_ge(*at(inv_root, l, 2))
                for b in range(TB):
                    last = v.tensor_tensor(qn3[:, b, :].rearrange("p (h d) -> p h d", d=HEAD),
                                           p_qkv[:, b, 0:640].rearrange("p (h d) -> p h d", d=HEAD),
                                           r20[:, b * 10:(b + 1) * 10].rearrange("p (h a) -> p h a", a=1)
                                           .broadcast_to([P, 10, HEAD]), ALU.mult)
                last.then_inc(qn_done.sem, 1)
                dve.wait_ge(*at(qn_done, l, 1))
                dve.wait_ge(*at(rope_tab_done, l, 1))
                link(v.tensor_tensor(rope3, qn3, cos_g, ALU.mult))
                dve.wait_ge(*at(rot_done, l, 1))
                link(v.tensor_tensor(rope, rope, rot, ALU.add))
                for b in range(TB):
                    last = v.tensor_copy(k_twice[:, b, :, :, :],
                                         rope3[:, b, 512:640].rearrange("p (g a d) -> p g a d", g=2, a=1)
                                         .broadcast_to([P, 2, 2, HEAD]))
                last.then_inc(rope_done.sem, 1)

                def hyena_multiply(o):
                    dve.wait_ge(*at(u_spec_ready, l, o + 1))
                    re = ps[:, 1, :].rearrange("p (k c) -> p k c", k=2)
                    im = ps[:, 2, :].rearrange("p (k c) -> p k c", k=2)
                    v.tensor_tensor(prod[:, 0, :, :], re, spec[:, 0:2, o, :], ALU.mult)
                    v.tensor_tensor(prod[:, 1, :, :], im, spec[:, 2:4, o, :], ALU.mult)
                    v.tensor_tensor(prod[:, 2, :, :], re, spec[:, 2:4, o, :], ALU.mult)
                    v.tensor_tensor(prod[:, 3, 0, :], im[:, 0, :], spec[:, 4, o, :], ALU.mult)
                    link(v.tensor_tensor(prod[:, 3, 1, :], im[:, 1, :], spec[:, 1, o, :], ALU.mult))
                    v.tensor_tensor(y_spec[:, 0, :, :], prod[:, 0, :, :], prod[:, 1, :, :], ALU.subtract)
                    v.tensor_tensor(y_spec[:, 1, :, :], prod[:, 2, :, :], prod[:, 3, :, :], ALU.add)\
                        .then_inc(y_spec_done.sem, 1)

                def hyena_gate(o):
                    dve.wait_ge(*at(y_ready, l, o + 1))
                    dve.wait_ge(*at(y_spec_done, l, o + 1))
                    for c in range(2):
                        last = v.scalar_tensor_tensor(prod[:, 0, c, :], conv[:, c, :], par("hb", 2 * o + c),
                                                      ps[:, 0, c * 256:(c + 1) * 256], ALU.mult, ALU.add)
                    link(last)
                    v.tensor_tensor(conv[:, 0:2, :], prod[:, 0, :, :], conv[:, 2 + 2 * o:4 + 2 * o, :], ALU.mult)\
                        .then_inc(hyena_done.sem, 1)

                def softmax_max(u):
                    g = u % 2
                    dve.wait_ge(*at(att_ready, l, u + 1))
                    link(v.tensor_reduce(mx[:, 4 * g:4 * g + 4],
                                         ps[:, 4 + 2 * g:6 + 2 * g, :].rearrange("p k (s n) -> p (k s) n", n=256),
                                         AX.X, ALU.max))
                    v.tensor_scalar(nmx[:, 4 * g:4 * g + 4], mx[:, 4 * g:4 * g + 4], -HEAD ** -0.5, None, ALU.mult)\
                        .then_inc(max_done.sem, 1)

                def softmax_scale(u):
                    g = u % 2
                    dve.wait_ge(*at(exp_done, l, u + 1))
                    link(v.reciprocal(rrs[:, 4 * g:4 * g + 4], rs[:, 4 * g:4 * g + 4]))
                    v.tensor_tensor(probs[:, g, :, :], probs[:, g, :, :],
                                    rrs[:, 4 * g:4 * g + 4].rearrange("p (s a) -> p s a", a=1)
                                    .broadcast_to([P, 4, 256]), ALU.mult).then_inc(probs_done.sem, 1)

                def probs_transposed(u):
                    dve.wait_ge(*at(pT_ready, l, u + 1))
                    v.tensor_copy(probs_t[:, u, 1, :, :],
                                  ps[:, 5 + 2 * (u % 2), :].rearrange("p (s q) -> p s q", q=P))\
                        .then_inc(pT_dve.sem, 1)

                def mixed_lower(n, parts):
                    dve.wait_ge(*at(mix_hi, l, n))
                    for k, tok, src in parts:
                        last = v.scalar_tensor_tensor(x_lo[:, k, tok], src, par("gm", k),
                                                      x_hi[:, k, tok].bitcast(F32), ALU.mult, ALU.subtract)
                    last.then_inc(mix_lo.sem, 1)

                def attention_lower(n, b):
                    mixed_lower(n, [(k, slice(b * P, (b + 1) * P), ps[:, 3, k * P:(k + 1) * P]) for k in range(4)])

                hyena_multiply(0)
                softmax_max(0)
                mixed_lower(1, [(6 + q, slice(0, SEQ), fn_u[:, q, :]) for q in range(2)])
                hyena_gate(0)
                softmax_max(1)
                softmax_scale(0)
                probs_transposed(0)
                softmax_scale(1)
                hyena_multiply(1)
                softmax_max(2)
                probs_transposed(1)
                attention_lower(2, 0)
                softmax_max(3)
                softmax_scale(2)
                hyena_gate(1)
                probs_transposed(2)
                softmax_scale(3)
                mixed_lower(3, [(4 + q, slice(0, SEQ), conv[:, q, :]) for q in range(2)])
                probs_transposed(3)
                attention_lower(4, 1)
                dve.wait_ge(*at(group_ready, l, 1))
                v.tensor_scalar(ms6[:, 0:2], ps[:, 7, 0:2], 1.0 / A_W, EPS, ALU.mult, ALU.add)
                v.tensor_scalar(ms6[:, 2:6], ps[:, 7, 2:6], 1.0 / HY_W, EPS, ALU.mult, ALU.add)\
                    .then_inc(mean_sq.sem, 1)
                dve.wait_ge(*at(inv_root, l, 3))
                for n, g in enumerate((2, 1, 0)):
                    dve.wait_ge(*at(half_used, l, 2 * (O0 + (2, 4, 8)[n])))
                    for b in range(TB):
                        bank = (4 if g == 1 else 0) + 2 * b
                        v.scalar_tensor_tensor(x[:, b, :], ps[:, bank:bank + 2, :].rearrange("p k n -> p (k n)"),
                                               r6[:, 2 * g + b:2 * g + b + 1], x[:, b, :], ALU.mult, ALU.add)\
                            .then_inc(out_added.sem, 1)
                    dve.wait_ge(*at(out_added, l, 2 * n + 2))
                norm_scale(1)
                transposed_lower("g2", 8)

                def lower(n, h):
                    dve.wait_ge(*at(half_used, l, 2 * n + h - 3))
                    dve.wait_ge(*at(hi_done, l, 2 * n + h + 1))
                    v.tensor_tensor(half(tab_lo, n, h), half(raw, n, h), half(tab_hi, n, h).bitcast(F32),
                                    ALU.subtract).then_inc(lo_dve.sem, 1)

                for n in range(Q0, U0):
                    lower(n, 0)
                    lower(n, 1)
                dve.wait_ge(*at(half_used, l, 2 * U0))
                for g in range(4):
                    v.tensor_copy(query_t[:, 8 + 2 * g:10 + 2 * g, :],
                                  ps[:, 4 + g, :].rearrange("p (k t) -> p k t", k=2)).then_inc(query_dve.sem, 1)
                for g in range(4):
                    dve.wait_ge(*at(scores_ready, l, g + 1))
                    if g == 3:
                        dve.wait_ge(*at(scores_act, l, 4))
                    v.tensor_copy(scores[:, 0, 4 * g:4 * g + 4, :], ps[:, g, :].rearrange("p (k n) -> p k n", k=4))\
                        .then_inc(scores_dve.sem, 1)
                settled(dve)

                def top16(values, indices, row, rows):
                    steps = (lambda r: v.max(values(r)[:, 0:8], row(r)),
                             lambda r: v.max_index(indices(r)[:, 0:8], values(r)[:, 0:8], row(r)),
                             lambda r: v.match_replace(row(r), values(r)[:, 0:8], row(r), NEG),
                             lambda r: v.max(values(r)[:, 8:16], row(r)),
                             lambda r: v.max_index(indices(r)[:, 8:16], values(r)[:, 8:16], row(r)))
                    for step in steps:
                        for r in range(rows):
                            last = step(r)
                        settled(dve)

                for b in range(TB):
                    top16(lambda r: v_top[:, b, r, :], lambda r: i_top[:, b, r, :], lambda r: scores[:, b, r, :], HP)
                link(v.tensor_copy(i_topf, i_top))
                for b in range(TB):
                    side = v_top[:, b, :, :].rearrange("p (h s) n -> p h s n", s=2)
                    v.tensor_tensor(
                        cand, side[:, :, 0, :].rearrange("p h (n a) -> p h n a", a=1).broadcast_to([P, PH, 16, 16]),
                        side[:, :, 1:2, :].broadcast_to([P, PH, 16, 16]), ALU.add)
                    settled(dve)
                    top16(lambda r: best[:, b, r, :], lambda r: pos[:, b, r * 16:(r + 1) * 16],
                          lambda r: cand[:, r, :, :].rearrange("p a b -> p (a b)"), PH)
                bests = best.rearrange("p b h n -> p (b h) n")
                link(v.tensor_copy(ssg.rearrange("p (n a) -> p n a", a=1), bests[:, :, 0:1]))
                v.tensor_tensor(bests, bests, ssg.rearrange("p (n a) -> p n a", a=1).broadcast_to([P, 16, 16]),
                                ALU.subtract).then_inc(best_done.sem, 1)
                for b in range(TB):
                    link(v.tensor_single_scalar(place_u[:, 0, :], pos[:, b, :], 4, op=ALU.logical_shift_right))
                    link(v.tensor_single_scalar(place_u[:, 1, :], pos[:, b, :], 15, op=ALU.bitwise_and))
                    link(v.tensor_copy(place_f, place_u))
                    for s in range(2):
                        link(v.tensor_tensor(
                            eq, place_f[:, s, :].rearrange("p (n a) -> p n a", a=1).broadcast_to([P, PICKS, TOPK]),
                            iota16.rearrange("p (a n) -> p a n", a=1).broadcast_to([P, PICKS, TOPK]), ALU.is_equal))
                        side = i_topf[:, b, :, :].rearrange("p (h s) n -> p h s n", s=2)[:, :, s:s + 1, :]
                        eq4 = eq.rearrange("p (h k) r -> p h k r", h=PH)
                        link(v.tensor_tensor(eq4, eq4, side.broadcast_to([P, PH, TOPK, TOPK]), ALU.mult))
                        link(v.tensor_reduce(chosen[:, s, b, :], eq, AX.X, ALU.add))
                dve.wait_ge(*at(gate_exp, l, 1))
                link(v.tensor_reduce(ssg, bests, AX.X, ALU.add))
                link(v.reciprocal(ssg, ssg))
                v.tensor_tensor(chosen[:, 2, :, :].rearrange("p b (h n) -> p (b h) n", n=16), bests,
                                ssg.rearrange("p (n a) -> p n a", a=1).broadcast_to([P, 16, 16]), ALU.mult)\
                    .then_inc(topk_done.sem, 1)
                def u_lower(i):
                    for s in range(4):
                        for h in range(2):
                            dve.wait_ge(*at(half_used, l, i * 8 + 2 * (U0 + s) + h - 3))
                            dve.wait_ge(*at(hi_done, l, i * 8 + 2 * (U0 + s) + h + 1))
                            v.tensor_tensor(half(tab_lo, s, h), half(raw, s, h), half(tab_hi, s, h).bitcast(F32),
                                            ALU.subtract).then_inc(lo_dve.sem, 1)

                settled(dve)
                with dve.Fori(EARLY // 4, 32) as i:
                    u_lower(i)
                dve.wait_ge(*at(picksT_ready, l, 1))
                v.tensor_copy(picks[:, 0:2, :], ps[:, 4, :].rearrange("p (n t) -> p n t", n=2))\
                    .then_inc(picksT_done.sem, 1)
                v.tensor_copy(picks[:, 2, :], ps[:, 5, 0:256]).then_inc(picksT_done.sem, 1)
                dve.wait_ge(*at(picksT_done, l, 2))
                dve.wait_ge(*at(gelu_done, l, 64))

                def one_hot(rows, side, n, signal):
                    v.tensor_tensor(rows, iota.rearrange("p (a c) -> p a c", a=1).broadcast_to([P, 4, P]),
                                    picks[:, side, bass.ds(n * 4, 4)].rearrange("p (t a) -> p t a", a=1)
                                    .broadcast_to([P, 4, P]), ALU.is_equal).then_inc(signal.sem, 1)

                def one_hot_i(i, s, first=False):
                    if not first:
                        dve.wait_ge(*at(hot_scaled, l, i * 4 + s - 3))
                    one_hot(hot_rows[:, s, :, :], 0, i * 4 + s, hot_i)

                def gate_body(i, first=False, last=False):
                    for s in range(4):
                        if s < 2:
                            one_hot_i(i, s + 2, first)
                        elif not last:
                            one_hot_i(i + 1, s - 2)
                        n = i * 4 + s
                        if s == 2:
                            dve.wait_ge(*at(gates_ready, l, n))
                            one_hot(onehot[:, 1, 1, :, :], 1, n + 1, hot_j_dve)
                        dve.wait_ge(*at(gates_ready, l, n + 1))
                        cell = work[:, :, bass.ds(n * 4, 4)]
                        v.tensor_tensor(cell, ps[:, 2 + s % 2, :].rearrange("p (t j) -> p j t", t=4), cell, ALU.mult)\
                            .then_inc(weighted.sem, 1)

                one_hot_i(0, 0, True)
                one_hot_i(0, 1, True)
                gate_body(0, first=True)
                with dve.Fori(1, 15) as i:
                    gate_body(i)
                gate_body(15, last=True)
                settled(dve)

                with dve.Fori(0, 32) as i:
                    for s in range(4):
                        for h in range(2):
                            dve.wait_ge(*at(half_used, l, i * 8 + 2 * (V0 + s) + h - 3))
                            dve.wait_ge(*at(hi_done, l, i * 8 + 2 * (V0 + s) + h + 1))
                            v.tensor_tensor(half(tab_lo, s, h), half(raw, s, h), half(tab_hi, s, h).bitcast(F32),
                                            ALU.subtract).then_inc(lo_dve.sem, 1)
                            if h == 1:
                                dve.wait_ge(*at(whi_done, l, i * 4 + s + 1))
                                v.tensor_tensor(w_lo[:, s % 2, :], work[:, i * 4 + s, :],
                                                w_hi[:, s % 2, :].bitcast(F32), ALU.subtract).then_inc(wlo_done.sem, 1)
                dve.wait_ge(*at(half_used, l, 2 * TILES))
                v.tensor_tensor(x[:, :, :].rearrange("p b d -> p (b d)"), ps[:, 4:8, :].rearrange("p k n -> p (k n)"),
                                x[:, :, :].rearrange("p b d -> p (b d)"), ALU.add).then_inc(layer_done.sem, 1)
                assert count[0] == dve_step.per_layer, f"dve_step counts {count[0]} per layer"
                dve.wait_ge(*at(layer_done, l, 2))
            dve.wait_ge(sq_sum.sem, DEPTH * 4 + 2)
            v.tensor_scalar(ms, ss, 1.0 / D, EPS, ALU.mult, ALU.add).then_inc(mean_sq.sem, 1)
            dve.wait_ge(inv_root.sem, DEPTH * 4 + 1)
            dve.wait_ge(fg_in.sem, 16)
            for b in range(TB):
                last = v.scalar_tensor_tensor(xn[:, b, :], x[:, b, :], rinv[:, b:b + 1], area(8192, D), ALU.mult,
                                              ALU.mult)
            last.then_inc(fin.sem, 1)


def constants():
    import numpy as np
    f32 = np.float32
    kc = np.zeros((P, KC_N), f32)
    kc[:, KC["ident"]:KC["ident"] + P] = np.eye(P)
    kc[:, KC["iota"]:KC["iota"] + P] = np.arange(P)
    kc[:, KC["ones"]:KC["ones"] + P] = 1.0
    row = np.repeat(np.arange(SEQ // 64), 64).astype(f32)
    col = np.tile(np.arange(64), SEQ // 64).astype(f32)
    inv = (f32(10000.0) ** (-np.arange(16, dtype=f32) / f32(16))).astype(f32)
    ang = np.stack([row[:, None] * inv, col[:, None] * inv], axis=1)
    cos = np.stack([np.cos(ang), np.cos(ang)], axis=2).reshape(TB, P, 64)
    sin = np.stack([-np.sin(ang), np.sin(ang)], axis=2).reshape(TB, P, 64)
    kc[:, KC["cos"]:KC["cos"] + 128] = cos.transpose(1, 0, 2).reshape(P, 128)
    kc[:, KC["sin"]:KC["sin"] + 128] = sin.transpose(1, 0, 2).reshape(P, 128)
    kc[:, KC["neg_half"]] = -0.5
    kc[:, KC["not_first"]] = 1.0
    kc[0, KC["not_first"]] = 0.0
    kc[:, KC["iota16"]:KC["iota16"] + 16] = np.arange(16)

    def tiles(m):
        return m.reshape(TB, P, -1).transpose(1, 0, 2).reshape(P, -1)

    cf = np.zeros((P, CF_N), f32)
    t = np.linspace(0.0, 1.0, SEQ, dtype=f32)[:, None]
    bands = np.arange(1, 9, dtype=f32)
    a = (f32(2.0 * np.pi) * t * bands).astype(f32)
    z = np.concatenate([t, np.sin(a), np.cos(a)], axis=-1)
    cf[0:17, CF["z"]:CF["z"] + 256] = z.T
    rates = np.linspace(-np.log(1e-2) / 1.5, -np.log(1e-2) / 0.3, HY_W, dtype=f32)
    cf[:, CF["decay"]:CF["decay"] + 512] = tiles(np.exp(-t * rates))
    n = np.arange(SEQ)
    w = 2 * np.pi * ((n[:, None] * n[None, :]) % 512) / 512
    nyq = (-1.0) ** n
    c, s = np.cos(w), np.sin(w)
    cf[:, CF["sin0"]:CF["sin0"] + 512] = tiles(s)
    cn = c[:, 0:P].copy()
    cn[:, 0] = nyq
    cf[:, CF["cosn"]:CF["cosn"] + 256] = tiles(cn)
    k = np.arange(64)
    wk = 2 * np.pi * ((k[:, None] * k[None, :]) % 64) / 64
    for g in range(2):
        cf[g * 64:(g + 1) * 64, CF["bc"] + g * 64:CF["bc"] + (g + 1) * 64] = np.cos(wk) / 128.0
        cf[g * 64:(g + 1) * 64, CF["bs"] + g * 64:CF["bs"] + (g + 1) * 64] = -np.sin(wk) / 128.0
    cd = np.zeros((P, CD_N), f32)
    sp = -s.copy()
    sp[:, 0] = nyq
    ic = c * (2.0 / 512)
    ic[0, :] = 1.0 / 512
    isn = -s * (2.0 / 512)
    isn[0, :] = nyq / 512
    wl = 2 * np.pi * ((n[:, None] * n[None, :]) % SEQ) / SEQ
    for name, m in (("cos", c), ("sin", sp), ("icos", ic), ("isin", isn), ("fc", np.cos(wl)), ("fs", np.sin(wl))):
        cd[:, CD[name]:CD[name] + 512] = tiles(m)
    return kc, cf, cd


def layouts(i):
    import numpy as np
    f32 = np.float32
    a = {k: np.asarray(v) for k, v in i.items()}
    pvec = np.zeros((DEPTH, P, PV_N), f32)

    def cols(v, k):
        return v.reshape(DEPTH, k, P).transpose(0, 2, 1)

    pvec[:, :, 0:8] = cols(a["norm1_g"], 8)
    pvec[:, :, 8:16] = cols(a["norm2_g"], 8)
    pvec[:, :, 16:24] = cols(a["mix_norm_g"], 8)
    pvec[:, :, 24:42] = cols(a["hy_conv_w"], 18)
    pvec[:, :, 42:48] = cols(a["hy_conv_b"], 6)
    pvec[:, :, 48:52] = cols(a["hy_bias"], 4)
    pvec[:, :, 52:54] = cols(a["fn_b"], 2)
    for n, name in enumerate(("hy_b1", "hy_freq1", "hy_b2", "hy_freq2")):
        pvec[:, 0:64, 54 + n] = a[name]
    pmat = np.zeros((DEPTH, P, PM_N), f32)
    pmat[:, 0:17, 0:64] = a["hy_w1"]
    pmat[:, 0:64, 64:128] = a["hy_w2"]
    pmat[:, 0:64, 128:1152] = a["hy_w3"]
    for g in range(4):
        q, h = g // 2, g % 2
        pmat[:, h * 64:(h + 1) * 64, 1152 + q * P + h * 64:1152 + q * P + (h + 1) * 64] = a["fn_w"][:, g]
    gqk = np.concatenate([np.tile(a["q_norm_g"], (1, 8)), np.tile(a["k_norm_g"], (1, 2))], axis=1)
    gqk = np.ascontiguousarray(np.broadcast_to(gqk[:, None, :], (DEPTH, P, 640)))
    subk = np.ascontiguousarray(a["peer_sub_keys"].transpose(0, 4, 2, 1, 3).reshape(DEPTH, P, HP * KEYS))
    tu = np.ascontiguousarray(a["peer_u"].reshape(DEPTH, P, P, DT, P).transpose(0, 2, 4, 3, 1).reshape(DEPTH, P, P, D))
    tv = np.ascontiguousarray(a["peer_v"].reshape(DEPTH, P, P, D).transpose(0, 2, 1, 3))
    w_proj = np.concatenate([a["w_in"][:, :, QKV:], a["w_in"][:, :, :QKV], a["w_out"], a["peer_w_query"]], axis=2)
    kc, cf, cd = constants()
    return {
        "x_in": a["x"].reshape(SEQ, D), "w_proj": w_proj,
        "sub_keys": subk, "tab_u": tu, "tab_v": tv, "pvec": pvec, "pmat": pmat, "gain_qk": gqk, "kconst": kc,
        "cfilter": cf, "cdft": cd,
        "final_g": np.ascontiguousarray(np.broadcast_to(a["final_g"][None, :], (P, D))),
    }


def kernel(**inputs):
    import concourse.bacc as bacc
    from concourse.bass_utils import run_bass_kernel_spmd

    nc = bacc.Bacc("TRN2", target_bir_lowering=False, num_devices=1)
    arrays = layouts(inputs)
    args = [nc.dram_tensor(name, v.shape, mybir.dt.from_np(v.dtype), kind="ExternalInput").ap()
            for name, v in arrays.items()]
    out = nc.dram_tensor("out", (SEQ, D), F32, kind="ExternalOutput").ap()
    hybrid_encoder(nc, *args, out)
    r = run_bass_kernel_spmd(nc, [arrays], core_ids=[0])
    return r.results[0]["out"].reshape(1, SEQ, D)
```

```python
from contextlib import ExitStack

import concourse.bass as bass
from concourse import mybir

ALU = mybir.AluOpType
ACT = mybir.ActivationFunctionType
AX = mybir.AxisListType
F32 = mybir.dt.float32
F32R = mybir.dt.float32r
U32 = mybir.dt.uint32

P = 128
DEPTH = 2
SEQ = 256
D = 1024
TB = SEQ // P
DT = D // P
HEAD = 64
HEADS, KV_HEADS = 8, 2
A_W, KV_W, HY_W, FN_W = 512, 128, 256, 256
QKV = A_W + 2 * KV_W
CT = (3 * HY_W + FN_W) // P
IN_COLS = QKV + CT * P
PH, KEYS, TOPK = 8, 128, 16
HP = 2 * PH
PICKS = PH * TOPK
EPS = 1e-6
NEG = -3.0e38

INV_2PI = 0.15915494309189535
ROUND = 12582912.0
TWO_PI = (6.28125, 0.0019350051879882812, 3.019916050561733e-07)
SIN_MAX = 3.1415925

PV = {"g1": 0, "g2": 8, "gm": 16, "cw": 24, "cb": 42, "hb": 48, "fb": 52, "b1": 54, "f1": 55, "b2": 56, "f2": 57}
PV_N = 58
PM = {"w1": 0, "w2": 64, "w3": 128, "fw": 1152}
PM_N = 1408
KC = {"ident": 0, "iota": 128, "ones": 256, "cos": 384, "sin": 512, "neg_half": 640, "not_first": 641, "iota16": 642}
KC_N = 658
CF = {"z": 0, "decay": 256, "sin0": 768, "cosn": 1280, "bc": 1536, "bs": 1664}
CF_N = 1792
CD = {"cos": 0, "sin": 512, "icos": 1024, "isin": 1536, "fc": 2048, "fs": 2560}
CD_N = 3072

FILTER_C, FILTER_M = 0, 1792
DFT, GAIN_QK = 3200, 6272
LOADED_AHEAD = 6912
SINE, FILT, FILT_SQ, F_SUM, F_DIF, F_RN = 6912, 7936, 9984, 12032, 13056, 14080
PROBS_T, MIXED_SQ = 9984, 0
Y_SPEC, PROD = 8960, 19712
SPEC = 14592
ROPE_TAB = 17152
XN = 19712
PROBS = (6912, 7936, ROPE_TAB, ROPE_TAB + 1024)
P_QKV, P_T, FN_U = 21760, 23296, 24844
CONV, Z_T, ROPE, QN = 25356, 26892, 27404, 28684
Q_T, K_T, FN_P = 29964, 30988, 31500
QUERY_T = 0
SUBKEYS = SPEC
CAND, EQ, SCORES = 24576, 26624, 28672
GUARD = 96

A0, B0, O0, Q0, U0, V0, TILES = 0, 8, 16, 24, 40, 168, 296
OUT_ORDER = (6, 7, 4, 5, 0, 1, 2, 3)
EARLY = 40
LO_POOL = 2 * (O0 + 8) + 2 * EARLY
LO_DVE = 2 * TILES - LO_POOL
UNIT_BANKS = (4, 6, 1, 4)
FNET_BANKS, HYENA_BANKS, ATTN_BANKS = ((6, 7), (0, 2)), ((1, 4), (5, 3)), ((6, 7), (0, 2))
FNET_SUMS, HYENA_SUMS, ATTN_SUMS = 2, 4, 2
DVE_STEPS = 55


class Signal:

    def __init__(self, sem, per_layer):
        self.sem, self.per_layer = sem, per_layer


def at(signal, layer, count):
    return signal.sem, layer * signal.per_layer + count


def hybrid_encoder(nc, x_in, w_proj, sub_keys, tab_u, tab_v, pvec, pmat, gain_qk, kconst, cfilter,
                   cdft, final_g, out):
    with ExitStack() as ctx:
        def sb(name, shape, dt=F32):
            return ctx.enter_context(nc.sbuf_tensor(name, shape, dt))

        def sig(name, per_layer):
            return Signal(ctx.enter_context(nc.semaphore(name)), per_layer)

        work = sb("work", [P, P, SEQ])
        x = sb("x", [P, TB, D])
        x_hi = sb("x_hi", [P, DT, SEQ], F32R)
        x_lo = sb("x_lo", [P, DT, SEQ], F32R)
        raw = sb("raw", [P, 4, D])
        tab_hi = sb("tab_hi", [P, 2, D], F32R)
        tab_lo = sb("tab_lo", [P, 2, D], F32R)
        w_hi = sb("w_hi", [P, 2, SEQ], F32R)
        w_lo = sb("w_lo", [P, 2, SEQ], F32R)
        picks = sb("picks", [P, 3, SEQ])
        onehot = sb("onehot", [P, 2, 2, 4, P])
        kc = sb("kc", [P, KC_N])
        pv = sb("pv", [P, PV_N])
        chosen = sb("chosen", [P, 3, TB, PICKS])
        small = sb("small", [P, 192])
        ps = ctx.enter_context(nc.psum_tensor("ps", [P, 8, 512], F32))

        workf = work[:, :, :].rearrange("p j t -> p (j t)")
        onef = onehot[:, :, :, :, :].rearrange("p s a t c -> p (s a t c)")
        picksf = picks[:, :, :].rearrange("p n t -> p (n t)")
        chosenf = chosen[:, :, :, :].rearrange("p n b t -> p (n b t)")

        def area(start, n):
            return workf[:, start:start + n]

        ident = kc[:, KC["ident"]:KC["ident"] + P]
        iota = kc[:, KC["iota"]:KC["iota"] + P]
        ones = kc[:, KC["ones"]:KC["ones"] + P]
        cos_r = kc[:, KC["cos"]:KC["cos"] + TB * HEAD].rearrange("p (b d) -> p b d", b=TB)
        sin_r = kc[:, KC["sin"]:KC["sin"] + TB * HEAD].rearrange("p (b d) -> p b d", b=TB)
        neg_half = kc[:, KC["neg_half"]:KC["neg_half"] + 1]
        iota16 = kc[:, KC["iota16"]:KC["iota16"] + TOPK]

        def par(name, i=0, rows=P):
            return pv[0:rows, PV[name] + i:PV[name] + i + 1]

        ss = small[:, 0:2]
        rinv = small[:, 2:4]
        ss20 = small[:, 4:24]
        r20 = small[:, 24:44]
        mx, nmx, rs, rrs = (small[:, c:c + 16] for c in range(128, 192, 16))
        ms6 = small[:, 76:82]
        r6 = small[:, 82:88]
        ssg = small[:, 88:104]
        ms = small[:, 104:106]
        ms20 = small[:, 106:126]

        fc = area(FILTER_C, CF_N)
        fm = area(FILTER_M, PM_N)
        arg = workf[0:64, SINE:SINE + 256]
        turns = workf[0:64, SINE + 256:SINE + 512]
        f_h1 = workf[0:64, SINE + 512:SINE + 768]
        f_h2 = workf[0:64, SINE + 768:SINE + 1024]
        filt = area(FILT, 2048).rearrange("p (b o e c) -> p b o e c", b=TB, o=2, e=2)
        filt_sq = area(FILT_SQ, 2048).rearrange("p (b o e c) -> p b o e c", b=TB, o=2, e=2)
        f_sum = area(F_SUM, 1024).rearrange("p (b o c) -> p b o c", b=TB, o=2)
        f_dif = area(F_DIF, 1024).rearrange("p (b o c) -> p b o c", b=TB, o=2)
        f_rn = area(F_RN, 512)
        decay = fc[:, CF["decay"]:CF["decay"] + 512].rearrange("p (b c) -> p b c", b=TB)
        sin0 = fc[:, CF["sin0"]:CF["sin0"] + 512].rearrange("p (b f) -> p b f", b=TB)
        cosn = fc[:, CF["cosn"]:CF["cosn"] + 256].rearrange("p (b f) -> p b f", b=TB)
        spec = area(SPEC, 2560).rearrange("p (k o c) -> p k o c", k=5, o=2)
        dft = area(DFT, CD_N)

        def mat(name):
            return dft[:, CD[name]:CD[name] + 512].rearrange("p (b f) -> p b f", b=TB)

        xn = area(XN, 2048).rearrange("p (b d) -> p b d", b=TB)
        p_qkv = area(P_QKV, TB * QKV).rearrange("p (b n) -> p b n", b=TB)
        p_t = area(P_T, 6 * 258).rearrange("p (k t) -> p k t", k=6)
        fn_u = area(FN_U, 512).rearrange("p (k t) -> p k t", k=2)
        fn_m = chosenf[:, 0:512].rearrange("p (m q c) -> p m q c", m=2, q=2)
        conv = area(CONV, 1536).rearrange("p (k t) -> p k t", k=6)
        z_t = area(Z_T, 512).rearrange("p (b c) -> p b c", b=TB)
        prod = area(PROD, 2048).rearrange("p (m k c) -> p m k c", m=4, k=2)
        y_spec = area(Y_SPEC, 1024).rearrange("p (m k c) -> p m k c", m=2, k=2)
        qn = area(QN, 1280)
        rope = area(ROPE, 1280)
        rot = onef[:, 0:1280]
        gqk = area(GAIN_QK, 640)
        cos_g = area(ROPE_TAB, 1280).rearrange("p (b n) -> p b n", b=TB)
        sin_g = area(ROPE_TAB + 1280, 1280).rearrange("p (b n) -> p b n", b=TB)
        k_twice = picksf[:, 0:512].rearrange("p (b g e d) -> p b g e d", b=TB, g=2, e=2)
        q_t = area(Q_T, 1024).rearrange("p (k t) -> p k t", k=4)
        k_t = area(K_T, 512).rearrange("p (k t) -> p k t", k=2)
        probs = [area(start, 1024).rearrange("p (s k) -> p s k", s=4) for start in PROBS]
        probs_t = area(PROBS_T, 4096).rearrange("p (u b s q) -> p u b s q", u=4, b=TB, s=4)
        fn_p = area(FN_P, 1024).rearrange("p (b q m c) -> p b q m c", b=TB, q=2, m=2)
        mixed_sq = area(MIXED_SQ, 2048).rearrange("p (k t) -> p k t", k=8)
        query_t = area(QUERY_T, HP * SEQ).rearrange("p (k t) -> p k t", k=HP)
        subk = area(SUBKEYS, HP * KEYS).rearrange("p (k n) -> p k n", k=HP)
        scores = area(SCORES, TB * HP * KEYS).rearrange("p (b k n) -> p b k n", b=TB, k=HP)
        cand = area(CAND, PH * TOPK * TOPK).rearrange("p (h a b) -> p h a b", h=PH, a=TOPK)
        eq = area(EQ, PICKS * TOPK).rearrange("p (n r) -> p n r", r=TOPK)
        v_top = onef[:, 0:512].rearrange("p (b k n) -> p b k n", b=TB, k=HP)
        i_top = onef[:, 512:1024].bitcast(U32).rearrange("p (b k n) -> p b k n", b=TB, k=HP)
        i_topf = onef[:, 1024:1536].rearrange("p (b k n) -> p b k n", b=TB, k=HP)
        best = onef[:, 1536:1792].rearrange("p (b h n) -> p b h n", b=TB, h=PH)
        pos = onef[:, 1792:2048].bitcast(U32).rearrange("p (b n) -> p b n", b=TB)
        dist_abs, hot_rows = (h[:, :, :].rearrange("p (s a) t -> p s (a t)", s=4)
                              .rearrange("p s (t c) -> p s t c", t=4) for h in (x_hi, x_lo))
        minus_j = chosenf[:, 0:SEQ]
        place_u = onef[:, 0:256].bitcast(U32).rearrange("p (s n) -> p s n", s=2)
        place_f = onef[:, 256:512].rearrange("p (s n) -> p s n", s=2)

        const_in = sig("const_in", 0)
        x_landed = sig("x_landed", 0)
        pv_in = sig("pv_in", 16)
        mlp_in = sig("mlp_in", 32)
        params_in = sig("params_in", 48)
        dft_in = sig("dft_in", 16)
        gqk_in = sig("gqk_in", 16)
        subk_in = sig("subk_in", 16)
        raw_in = [sig(f"raw_in{s}", 16 * TILES // 4) for s in range(4)]
        hi_done = sig("hi_done", 2 * TILES)
        lo_pool = sig("lo_pool", LO_POOL)
        lo_dve = sig("lo_dve", LO_DVE)
        half_used = sig("half_used", 2 * TILES)
        dve_step = sig("dve_step", DVE_STEPS)
        mlp_ready = sig("mlp_ready", 2)
        sine_arg = sig("sine_arg", 2)
        sine_done = sig("sine_done", 2)
        taps_ready = sig("taps_ready", TB)
        filt_done = sig("filt_done", TB)
        filt_sq_done = sig("filt_sq_done", 1)
        sumdif_done = sig("sumdif_done", 1)
        f_norm_ready = sig("f_norm_ready", 1)
        f_root_done = sig("f_root_done", 1)
        spec_ready = sig("spec_ready", 5)
        spec_done = sig("spec_done", 5)
        rope_tab_done = sig("rope_tab_done", 1)
        sq_sum = sig("sq_sum", 4)
        mean_sq = sig("mean_sq", 5)
        inv_root = sig("inv_root", 5)
        xn_done = sig("xn_done", 2 * TB)
        xT_ready = sig("xT_ready", 8)
        h_hi = sig("h_hi", 16)
        h_lo = sig("h_lo", 16)
        fn_m_ready = sig("fn_m_ready", 1)
        fn_m_done = sig("fn_m_done", 1)
        chan_done = sig("chan_done", 4)
        qkv_done = sig("qkv_done", 4)
        qk_sq = sig("qk_sq", 4)
        conv_done = sig("conv_done", 1)
        zT_ready = sig("zT_ready", 2)
        zT_done = sig("zT_done", 2)
        u_spec_ready = sig("u_spec_ready", 2)
        y_spec_done = sig("y_spec_done", 2)
        y_ready = sig("y_ready", 2)
        hyena_done = sig("hyena_done", 2)
        fn1_ready = sig("fn1_ready", 2)
        fn1_done = sig("fn1_done", 2)
        fn2_ready = sig("fn2_ready", 1)
        fn2_done = sig("fn2_done", 1)
        qk_mean = sig("qk_mean", TB)
        qk_root = sig("qk_root", 1)
        qn_done = sig("qn_done", TB)
        rot_done = sig("rot_done", 1)
        rope_done = sig("rope_done", 1)
        k_twice_done = sig("k_twice_done", 1)
        qkT_ready = sig("qkT_ready", 3)
        qkT_done = sig("qkT_done", 3)
        att_ready = sig("att_ready", 4)
        max_done = sig("max_done", 4)
        exp_done = sig("exp_done", 4)
        probs_done = sig("probs_done", 4)
        pT_ready = sig("pT_ready", 4)
        pT_act = sig("pT_act", 4)
        pT_dve = sig("pT_dve", 4)
        attn_ready = sig("attn_ready", 4)
        attn_sq = sig("attn_sq", TB)
        mix_hi = sig("mix_hi", 4)
        mix_lo = sig("mix_lo", 4)
        fnet_sq = sig("fnet_sq", 1)
        hyena_sq = sig("hyena_sq", 1)
        group_ready = sig("group_ready", 3)
        out_first = sig("out_first", 1)
        out_added = sig("out_added", 12)
        query_act = sig("query_act", 4)
        query_dve = sig("query_dve", 4)
        scores_ready = sig("scores_ready", 8)
        scores_act = sig("scores_act", 4)
        scores_dve = sig("scores_dve", 4)
        best_done = sig("best_done", 1)
        gate_exp = sig("gate_exp", 1)
        topk_done = sig("topk_done", 1)
        picksT_ready = sig("picksT_ready", 1)
        picksT_done = sig("picksT_done", 1)
        gelu_done = sig("gelu_done", 64)
        hot_i = sig("hot_i", 64)
        hot_scaled = sig("hot_scaled", 64)
        abs_done = sig("abs_done", 48)
        hot_j_act = sig("hot_j_act", 48)
        hot_j_dve = sig("hot_j_dve", 16)
        gates_ready = sig("gates_ready", 64)
        weighted = sig("weighted", 64)
        whi_done = sig("whi_done", 128)
        wlo_done = sig("wlo_done", 128)
        first_block = sig("first_block", 1)
        layer_done = sig("layer_done", TB)
        fin = sig("fin", 0)
        fg_in = sig("fg_in", 0)
        out_written = sig("out_written", 0)

        block = ctx.enter_context(nc.Block())

        def settled(eng):
            eng.drain()

        def half(buf, n, h, width=512):
            return buf[:, n % buf.shape[1], h * width:(h + 1) * width]

        def lo_count(n, h):
            if n < Q0:
                return lo_pool, 2 * n + h + 1
            return lo_dve, 2 * (n - Q0) + h + 1

        LO_U = 2 * (U0 - Q0 - EARLY)
        LO_V = 2 * (V0 - Q0 - EARLY)
        LO_E = 2 * Q0

        def crossed(tensor_tensor, b):
            dst = rot[:, b * 640:(b + 1) * 640].rearrange("p (h a e d) -> p h a e d", h=10, a=2, e=2)
            src = qn[:, b * 640:(b + 1) * 640].rearrange("p (h a e d) -> p h a e d", h=10, a=2, e=2)
            sines = sin_g[:, b, :].rearrange("p (h a e d) -> p h a e d", h=10, a=2, e=2)
            for e in range(2):
                last = tensor_tensor(dst[:, :, :, e, :], src[:, :, :, 1 - e, :], sines[:, :, :, e, :], ALU.mult)
            return last

        @block.sync
        def _(sp):
            def load_filter_inputs(layer):
                sp.dma_start(fc[:, 0:256], cfilter[:, 0:256]).then_inc(mlp_in.sem, 16)
                sp.dma_start(fm[:, 0:192], pmat[layer, :, 0:192]).then_inc(mlp_in.sem, 16)

            def load_params(layer):
                sp.dma_start(fm[:, 192:704], pmat[layer, :, 192:704]).then_inc(params_in.sem, 16)
                sp.dma_start(fc[:, 256:CF_N], cfilter[:, 256:CF_N]).then_inc(params_in.sem, 16)
                sp.dma_start(fm[:, 704:1408], pmat[layer, :, 704:1408]).then_inc(params_in.sem, 16)

            def load_late_params(layer):
                sp.dma_start(dft, cdft[:, :]).then_inc(dft_in.sem, 16)
                sp.dma_start(gqk, gain_qk[layer, :, :]).then_inc(gqk_in.sem, 16)

            def load_channels(layer, k):
                sp.dma_start(raw[:, k % 4, :], w_proj[layer, k * P:(k + 1) * P, 0:D])\
                  .then_inc(raw_in[k % 4].sem, 16)

            sp.dma_start(x[:, :, :], x_in.rearrange("(b p) d -> p b d", p=P)).then_inc(x_landed.sem, 16)
            sp.dma_start(kc[:, :], kconst[:, :]).then_inc(const_in.sem, 16)
            sp.dma_start(pv[:, :], pvec[0, :, :]).then_inc(pv_in.sem, 16)
            load_filter_inputs(0)
            load_channels(0, 0)
            load_channels(0, 1)
            load_params(0)
            load_channels(0, 2)
            load_channels(0, 3)
            load_late_params(0)
            with sp.Fori(0, DEPTH) as l:
                following = (l + 1) % DEPTH

                def slot_free(n):
                    signal, count = lo_count(n - 4, 1)
                    sp.wait_ge(*at(signal, l, count))

                for k in range(4, DT):
                    slot_free(A0 + k)
                    load_channels(l, k)
                for k in range(DT):
                    slot_free(B0 + k)
                    sp.dma_start(raw[:, k % 4, 0:QKV], w_proj[l, k * P:(k + 1) * P, D:D + QKV])\
                      .then_inc(raw_in[k % 4].sem, 16)
                for n, c in enumerate(OUT_ORDER):
                    slot_free(O0 + n)
                    sp.dma_start(raw[:, n % 4, :], w_proj[l, c * P:(c + 1) * P, IN_COLS:IN_COLS + D])\
                      .then_inc(raw_in[n % 4].sem, 16)
                for n in range(16):
                    slot_free(Q0 + n)
                    if n == 4:
                        sp.wait_ge(*at(hyena_done, l, 2))
                        sp.dma_start(subk, sub_keys[l, :, :]).then_inc(subk_in.sem, 16)
                    c, k = n // 8, n % 8
                    sp.dma_start(raw[:, n % 4, :], w_proj[l, k * P:(k + 1) * P, IN_COLS + (c + 1) * D:IN_COLS + (c + 2) * D])\
                      .then_inc(raw_in[n % 4].sem, 16)
                for n in range(4):
                    slot_free(U0 + n)
                    sp.dma_start(raw[:, n, :], tab_u[l, n, :, :]).then_inc(raw_in[n].sem, 16)

                def stream(i, table, signal, offset):
                    for s in range(4):
                        j = i * 4 + s
                        sp.wait_ge(*at(signal, l, j * 2 + offset - 6))
                        sp.dma_start(raw[:, s, :], table[l, j, :, :]).then_inc(raw_in[s].sem, 16)

                with sp.Fori(1, EARLY // 4 + 1) as i:
                    stream(i, tab_u, lo_pool, LO_E)
                with sp.Fori(EARLY // 4 + 1, 32) as i:
                    stream(i, tab_u, lo_dve, LO_U)
                with sp.Fori(0, 12) as i:
                    stream(i, tab_v, lo_dve, LO_V)
                sp.wait_ge(*at(whi_done, l, LOADED_AHEAD // SEQ + 1))
                sp.wait_ge(*at(wlo_done, l, LOADED_AHEAD // SEQ + 1))
                load_filter_inputs(following)
                load_params(following)
                load_late_params(following)
                sp.dma_start(pv[:, :], pvec[following, :, :]).then_inc(pv_in.sem, 16)
                with sp.Fori(12, 32) as i:
                    stream(i, tab_v, lo_dve, LO_V)
                for k in range(4):
                    sp.wait_ge(*at(lo_dve, l, LO_DVE + 2 * (k - 3)))
                    load_channels(following, k)
            sp.wait_ge(*at(layer_done, DEPTH, TB))
            sp.dma_start(area(8192, D), final_g[:, :]).then_inc(fg_in.sem, 16)
            sp.wait_ge(fin.sem, 1)
            sp.dma_start(out.rearrange("(b p) d -> p b d", p=P), xn).then_inc(out_written.sem, 16)
            sp.wait_ge(out_written.sem, 16)
            sp.wait_ge(pv_in.sem, (DEPTH + 1) * 16)
            sp.wait_ge(mlp_in.sem, (DEPTH + 1) * 32)
            sp.wait_ge(params_in.sem, (DEPTH + 1) * 48)
            sp.wait_ge(dft_in.sem, (DEPTH + 1) * 16)
            sp.wait_ge(gqk_in.sem, (DEPTH + 1) * 16)
            for s in range(4):
                sp.wait_ge(raw_in[s].sem, DEPTH * raw_in[s].per_layer + 16)

        @block.tensor
        def _(pe):
            mm, tr = nc.tensor.matmul, nc.tensor.transpose
            pe.wait_ge(const_in.sem, 16)
            with pe.Fori(0, DEPTH) as l:
                def in_halves(n, h):
                    signal, count = lo_count(n, h)
                    pe.wait_ge(*at(signal, l, count))

                def keep_clock(n, bank):
                    for _ in range(n):
                        mm(ps[:, bank, 0:P], ident, ident, start=True, stop=True)

                pe.wait_ge(*at(layer_done, l, TB))
                pe.wait_ge(*at(mlp_in, l, 32))
                mm(ps[0:64, 0, 0:256], fm[0:17, PM["w1"]:PM["w1"] + 64], fc[0:17, CF["z"]:CF["z"] + 256],
                   start=True, stop=True).then_inc(mlp_ready.sem, 1)

                def transpose_x(done):
                    for b in range(TB):
                        pe.wait_ge(*at(xn_done, l, done + b + 1))
                        for k in range(DT):
                            last = tr(ps[:, 4 + k // 2, (k % 2) * 256 + b * P:(k % 2) * 256 + (b + 1) * P],
                                      xn[:, b, k * P:(k + 1) * P], ident)
                            if b == 1 and k % 2:
                                last.then_inc(xT_ready.sem, 1)

                def channels(k):
                    pe.wait_ge(*at(h_hi, l, k + 1))
                    pe.wait_ge(*at(h_lo, l, k + 1))
                    for h in range(2):
                        in_halves(A0 + k, h)
                        for c in range(4 * h, 4 * h + 4):
                            bank = ps[:, c // 2, (c % 2) * 256:(c % 2) * 256 + 256]
                            col = slice((c % 4) * P, (c % 4 + 1) * P)
                            hi, lo = half(tab_hi, A0 + k, h)[:, col], half(tab_lo, A0 + k, h)[:, col]
                            mm(bank, hi, x_lo[:, k, :], start=(k == 0 and c % 2 == 0), stop=False,
                               skip_group_check=True)
                            mm(bank, hi, x_hi[:, k, :], start=False, stop=False, skip_group_check=True)
                            last = mm(bank, lo, x_hi[:, k, :], start=False, stop=(k == DT - 1), skip_group_check=True)
                        last.then_inc(half_used.sem, 1)

                keep_clock(8, 1)
                transpose_x(0)
                pe.wait_ge(*at(sine_arg, l, 1))
                channels(0)
                channels(1)
                pe.wait_ge(*at(sine_done, l, 1))
                mm(ps[:, 4, 0:256], fm[0:64, PM["w2"]:PM["w2"] + P], f_h1,
                   start=True, stop=True).then_inc(mlp_ready.sem, 1)
                channels(2)
                channels(3)
                pe.wait_ge(*at(params_in, l, 48))
                pe.wait_ge(*at(h_lo, l, DT))
                pe.wait_ge(*at(sine_done, l, 2))
                for b in range(TB):
                    for n in range(2):
                        last = mm(ps[:, (6, 4)[b] + n, :], f_h2[:, b * P:(b + 1) * P],
                                  fm[0:64, PM["w3"] + n * 512:PM["w3"] + (n + 1) * 512], start=True, stop=True)
                    last.then_inc(taps_ready.sem, 1)
                channels(4)
                pe.wait_ge(*at(filt_sq_done, l, 1))
                for b in range(TB):
                    for e in range(2):
                        last = mm(ps[:, 6, :], ones, filt_sq[:, b, :, e, :], start=(b + e == 0), stop=(b + e == 2))
                last.then_inc(f_norm_ready.sem, 1)
                channels(5)
                pe.wait_ge(*at(sumdif_done, l, 1))
                pe.wait_ge(*at(dft_in, l, 16))
                for n, (m, c, src, bank) in enumerate((
                        (mat("cos"), 0, f_sum, 4), (mat("cos"), P, f_sum, 5), (sin0, 0, f_dif, 7),
                        (sin0, P, f_dif, 6), (cosn, 0, f_sum, 4))):
                    if n == 3:
                        pe.wait_ge(*at(f_root_done, l, 1))
                    if n == 4:
                        channels(6)
                        channels(7)
                        pe.wait_ge(*at(spec_done, l, 1))
                    for b in range(TB):
                        last = mm(ps[:, bank, :], m[:, b, c:c + P], src[:, b, :, :], start=(b == 0), stop=(b == 1))
                    last.then_inc(spec_ready.sem, 1)
                pe.wait_ge(*at(spec_done, l, 2))
                for n, name in enumerate(("bc", "bs")):
                    last = mm(ps[:, 5, n * 256:(n + 1) * 256], fc[:, CF[name]:CF[name] + P],
                              fm[:, PM["fw"]:PM["fw"] + 256], start=True, stop=True)
                last.then_inc(fn_m_ready.sem, 1)
                def hyena_transposes(o):
                    if o == 0:
                        pe.wait_ge(*at(conv_done, l, 1))
                        pe.wait_ge(*at(fn1_done, l, 2))
                    else:
                        pe.wait_ge(*at(hyena_done, l, 1))
                    for b in range(TB):
                        for c in range(2):
                            last = tr(ps[:, 0, b * 256 + c * P:b * 256 + (c + 1) * P],
                                      conv[:, c, b * P:(b + 1) * P], ident)
                    last.then_inc(zT_ready.sem, 1)

                def hyena_forward(o):
                    pe.wait_ge(*at(zT_done, l, o + 1))
                    for n, name in enumerate(("cos", "sin")):
                        for f in range(2):
                            for b in range(TB):
                                last = mm(ps[:, 1 + n, f * 256:(f + 1) * 256], mat(name)[:, b, f * P:(f + 1) * P],
                                          z_t[:, b, :], start=(b == 0), stop=(b == 1))
                    last.then_inc(u_spec_ready.sem, 1)

                def hyena_inverse(o):
                    pe.wait_ge(*at(y_spec_done, l, o + 1))
                    for c in range(2):
                        for n, name in enumerate(("icos", "isin")):
                            for f in range(2):
                                last = mm(ps[:, 0, c * 256:(c + 1) * 256], y_spec[:, n, f, c * P:(c + 1) * P],
                                          mat(name)[:, f, :], start=(n + f == 0), stop=(n + f == 2))
                    last.then_inc(y_ready.sem, 1)

                def fnet_channels():
                    pe.wait_ge(*at(chan_done, l, 4))
                    for b in range(TB):
                        for q in range(2):
                            last = mm(ps[:, (3, 0)[b], q * 256:(q + 1) * 256], fn_u[:, q, b * P:(b + 1) * P],
                                      fn_m[:, :, q, :], start=True, stop=True)
                        last.then_inc(fn1_ready.sem, 1)

                def fnet_positions():
                    pe.wait_ge(*at(fn1_done, l, 2))
                    for q in range(2):
                        for b in range(TB):
                            for n, name in enumerate(("fc", "fs")):
                                last = mm(ps[:, 3, q * 256:(q + 1) * 256], fn_p[:, b, q, n, :], mat(name)[:, b, :],
                                          start=(b + n == 0), stop=(b + n == 2))
                    last.then_inc(fn2_ready.sem, 1)

                pe.wait_ge(*at(spec_done, l, 5))
                pe.wait_ge(*at(fn_m_done, l, 1))
                for k in range(DT):
                    for h in range(2):
                        in_halves(B0 + k, h)
                        hi, lo = half(tab_hi, B0 + k, h, 384), half(tab_lo, B0 + k, h, 384)
                        for b in range(TB):
                            tok = slice(b * P, (b + 1) * P)
                            bank = ps[:, 4 + 2 * b + h, 0:384]
                            mm(bank, x_hi[:, k, tok], lo, start=(k == 0), stop=False)
                            mm(bank, x_hi[:, k, tok], hi, start=False, stop=False)
                            last = mm(bank, x_lo[:, k, tok], hi, start=False, stop=(k == DT - 1))
                        last.then_inc(half_used.sem, 1)
                    if k == 2:
                        fnet_channels()
                    if k == 3:
                        hyena_transposes(0)
                    if k == 4:
                        hyena_forward(0)
                    if k == 6:
                        hyena_inverse(0)
                hyena_transposes(1)
                hyena_forward(1)
                fnet_positions()
                keep_clock(8, 0)
                pe.wait_ge(*at(qkv_done, l, 4))
                pe.wait_ge(*at(qk_sq, l, 4))
                pe.wait_ge(*at(rope_done, l, 1))
                rope4 = rope.rearrange("p (b h d) -> p b h d", b=TB, h=10)
                for g in range(3):
                    if g == 2:
                        pe.wait_ge(*at(k_twice_done, l, 1))
                    for k in range(2):
                        for b in range(TB):
                            if g < 2:
                                src = rope4[:, b, 4 * g + 2 * k:4 * g + 2 * k + 2, :].rearrange("p h d -> p (h d)")
                            else:
                                src = k_twice[:, b, k, :, :].rearrange("p e d -> p (e d)")
                            last = tr(ps[:, 4 + g, k * 256 + b * P:k * 256 + (b + 1) * P], src, ident)
                    last.then_inc(qkT_ready.sem, 1)

                keep_clock(5, 0)

                def attention_scores(u):
                    if u == 0:
                        pe.wait_ge(*at(qkT_done, l, 3))
                    if u == 2:
                        pe.wait_ge(*at(y_spec_done, l, 2))
                    if u == 3:
                        pe.wait_ge(*at(pT_act, l, 1))
                        pe.wait_ge(*at(pT_dve, l, 1))
                    b, base = u // 2, 64 * (u % 2)
                    for s in range(4):
                        last = mm(ps[:, UNIT_BANKS[u] + s // 2, (s % 2) * 256:(s % 2) * 256 + 256],
                                  q_t[base:base + 64, s, b * P:(b + 1) * P], k_t[base:base + 64, s // 2, :],
                                  start=True, stop=True)
                    last.then_inc(att_ready.sem, 1)

                def attention_transposes(u):
                    pe.wait_ge(*at(probs_done, l, u + 1))
                    for kb in range(TB):
                        for s in range(4):
                            last = tr(ps[:, UNIT_BANKS[u] + kb, s * P:(s + 1) * P],
                                      probs[u][:, s, kb * P:(kb + 1) * P], ident)
                    last.then_inc(pT_ready.sem, 1)

                def attention_values(u):
                    pe.wait_ge(*at(pT_act, l, u + 1))
                    pe.wait_ge(*at(pT_dve, l, u + 1))
                    b, base = u // 2, 64 * (u % 2)
                    if u == 0:
                        pe.wait_ge(*at(fn2_done, l, 1))
                    if u == 2:
                        pe.wait_ge(*at(mix_lo, l, 2))
                        pe.wait_ge(*at(attn_sq, l, 1))
                    for s in range(4):
                        v_col = A_W + KV_W + (s // 2) * HEAD
                        for kb in range(TB):
                            last = mm(ps[base:base + 64, 3, s * P:(s + 1) * P],
                                      p_qkv[:, kb, v_col:v_col + HEAD], probs_t[:, u, kb, s, :],
                                      start=(kb == 0), stop=(kb == 1))
                    last.then_inc(attn_ready.sem, 1)

                def group_sums(c0, c1, bank):
                    for b in range(TB):
                        for c in range(c0, c1):
                            last = mm(ps[:, bank, b:b + 1], mixed_sq[:, c, b * P:(b + 1) * P], ones[:, 0:1],
                                      start=(c == c0), stop=(c == c1 - 1))
                    last.then_inc(group_ready.sem, 1)

                def output_tile(n, banks, before=None):
                    c, first, final = OUT_ORDER[n], n in (0, 2, 4), n in (1, 3, 7)
                    order = [(h, b) for h in range(2) for b in range(TB)]
                    if n == 7:
                        order = [(h, b) for b in range(TB) for h in range(2)]
                    for h, b in order:
                        if b == 0:
                            in_halves(O0 + n, h)
                        hi, lo = half(tab_hi, O0 + n, h), half(tab_lo, O0 + n, h)
                        for signal, value in (before or {}).get(banks[b][h], ()):
                            pe.wait_ge(*at(signal, l, value))
                        tok = slice(b * P, (b + 1) * P)
                        bank = ps[:, banks[b][h], :]
                        mm(bank, x_hi[:, c, tok], lo, start=first, stop=False, skip_group_check=True)
                        mm(bank, x_hi[:, c, tok], hi, start=False, stop=False, skip_group_check=True)
                        last = mm(bank, x_lo[:, c, tok], hi, start=False, stop=final, skip_group_check=True)
                        if b == 1:
                            last.then_inc(half_used.sem, 1)
                        elif n == 7 and h == 1:
                            last.then_inc(out_first.sem, 1)

                attention_scores(0)
                attention_scores(1)
                attention_scores(2)
                attention_transposes(0)
                hyena_inverse(1)
                attention_transposes(1)
                attention_values(0)
                attention_scores(3)
                attention_transposes(2)
                attention_values(1)
                keep_clock(10, 6)
                pe.wait_ge(*at(fnet_sq, l, 1))
                pe.wait_ge(*at(pT_act, l, 3))
                pe.wait_ge(*at(pT_dve, l, 3))
                group_sums(6, 8, FNET_SUMS)
                pe.wait_ge(*at(mix_lo, l, 1))
                output_tile(0, FNET_BANKS, {0: ((hyena_done, 2),), FNET_SUMS: ((mean_sq, 2),)})
                attention_transposes(3)
                attention_values(2)
                attention_values(3)
                output_tile(1, FNET_BANKS)
                pe.wait_ge(*at(hyena_sq, l, 1))
                group_sums(4, 6, HYENA_SUMS)
                pe.wait_ge(*at(mix_lo, l, 3))
                output_tile(2, HYENA_BANKS, {HYENA_SUMS: ((mean_sq, 3),),
                                             3: ((attn_sq, 2), (mix_hi, 4), (mix_lo, 4))})
                output_tile(3, HYENA_BANKS)
                pe.wait_ge(*at(out_added, l, 4))
                group_sums(0, 4, ATTN_SUMS)
                output_tile(4, ATTN_BANKS, {ATTN_SUMS: ((mean_sq, 4),)})
                for n in range(5, 8):
                    output_tile(n, ATTN_BANKS)
                pe.wait_ge(*at(out_added, l, 8))
                keep_clock(16, 1)
                transpose_x(2)
                for n in range(16):
                    part, k = n // 8, n % 8
                    pe.wait_ge(*at(h_hi, l, DT + k + 1))
                    pe.wait_ge(*at(h_lo, l, DT + (DT if part else k + 1)))
                    for h in range(2):
                        in_halves(Q0 + n, h)
                        for c in range(4):
                            tile = part * 8 + h * 4 + c
                            bank = ps[:, tile // 2, (tile % 2) * 256:(tile % 2) * 256 + 256]
                            col = slice(c * P, (c + 1) * P)
                            hi, lo = half(tab_hi, Q0 + n, h)[:, col], half(tab_lo, Q0 + n, h)[:, col]
                            mm(bank, hi, x_lo[:, k, :], start=(k == 0 and c % 2 == 0), stop=False,
                               skip_group_check=True)
                            mm(bank, hi, x_hi[:, k, :], start=False, stop=False, skip_group_check=True)
                            last = mm(bank, lo, x_hi[:, k, :], start=False, stop=(k == DT - 1), skip_group_check=True)
                        last.then_inc(half_used.sem, 1)
                pe.wait_ge(*at(subk_in, l, 16))
                pe.wait_ge(*at(query_act, l, 4))
                for b in range(TB):
                    for c in range(HP):
                        if b == 0 and c == 8:
                            pe.wait_ge(*at(query_dve, l, 4))
                        last = mm(ps[:, 4 * b + c // 4, (c % 4) * P:(c % 4 + 1) * P],
                                  query_t[:, c, b * P:(b + 1) * P], subk[:, c, :], start=True, stop=True)
                        if c % 4 == 3:
                            last.then_inc(scores_ready.sem, 1)
                pe.wait_ge(*at(scores_dve, l, 2))

                def u_product(i, first, signal, offset):
                    for s in range(4):
                        j = i * 4 + s
                        if s % 2 == 0 and not first:
                            pe.wait_ge(*at(gelu_done, l, i * 2 + s // 2 - 1))
                        bank = ps[:, s // 2, (s % 2) * 256:(s % 2) * 256 + 256]
                        for h in range(2):
                            pe.wait_ge(*at(signal, l, j * 2 + offset + h + 1))
                            for k in range(4):
                                col = slice(k * P, (k + 1) * P)
                                hi, lo = half(tab_hi, s, h)[:, col], half(tab_lo, s, h)[:, col]
                                mm(bank, hi, x_lo[:, 4 * h + k, :], start=(h + k == 0), stop=False)
                                mm(bank, hi, x_hi[:, 4 * h + k, :], start=False, stop=False)
                                last = mm(bank, lo, x_hi[:, 4 * h + k, :], start=False, stop=(h + k == 4))
                            last.then_inc(half_used.sem, 1)

                u_product(0, True, lo_pool, LO_E)
                with pe.Fori(1, EARLY // 4) as i:
                    u_product(i, False, lo_pool, LO_E)
                with pe.Fori(EARLY // 4, GUARD // 4) as i:
                    u_product(i, False, lo_dve, LO_U)
                pe.wait_ge(*at(topk_done, l, 1))
                for n in range(3):
                    for b in range(TB):
                        last = tr(ps[:, 4 + n // 2, (n % 2) * 256 + b * P:(n % 2) * 256 + (b + 1) * P],
                                  chosen[:, n, b, :], ident)
                last.then_inc(picksT_ready.sem, 1)
                with pe.Fori(GUARD // 4, 32) as i:
                    u_product(i, False, lo_dve, LO_U)
                def gates(i, first):
                    for s in range(4):
                        n = i * 4 + s
                        pe.wait_ge(*at(hot_scaled, l, n + 1))
                        if s < 3:
                            pe.wait_ge(*at(hot_j_act, l, i * 3 + s + 1))
                        else:
                            pe.wait_ge(*at(hot_j_dve, l, i + 1))
                        if not first:
                            pe.wait_ge(*at(weighted, l, n - 3))
                        for t in range(4):
                            last = mm(ps[:, 2 + s, t * P:(t + 1) * P], onehot[:, s % 2, 0, t, :],
                                      onehot[:, s % 2, 1, t, :], start=True, stop=True)
                        last.then_inc(gates_ready.sem, 1)

                gates(0, True)
                with pe.Fori(1, 16) as i:
                    gates(i, False)
                pe.wait_ge(*at(picksT_done, l, 1))

                def v_product(i, first, final):
                    for s in range(4):
                        j = i * 4 + s
                        pe.wait_ge(*at(wlo_done, l, j + 1))
                        last_tile = final and s == 3
                        order = [(h, b) for h in range(2) for b in range(TB)]
                        if last_tile:
                            order = [(h, b) for b in range(TB) for h in range(2)]
                        for h, b in order:
                            if b == 0:
                                pe.wait_ge(*at(lo_dve, l, j * 2 + LO_V + h + 1))
                            hi, lo = half(tab_hi, s, h), half(tab_lo, s, h)
                            tok = slice(b * P, (b + 1) * P)
                            bank = ps[:, 4 + 2 * b + h, :]
                            mm(bank, w_hi[:, s % 2, tok], lo, start=(first and s == 0), stop=False,
                               skip_group_check=True)
                            mm(bank, w_hi[:, s % 2, tok], hi, start=False, stop=False, skip_group_check=True)
                            last = mm(bank, w_lo[:, s % 2, tok], hi, start=False, stop=last_tile,
                                      skip_group_check=True)
                            if b == 1:
                                last.then_inc(half_used.sem, 1)
                            elif last_tile and h == 1:
                                last.then_inc(first_block.sem, 1)

                v_product(0, True, False)
                with pe.Fori(1, 31) as i:
                    v_product(i, False, False)
                v_product(31, False, True)

        @block.scalar
        def _(act):
            fn = nc.scalar.activation
            act.wait_ge(x_landed.sem, 16)
            with act.Fori(0, DEPTH) as l:
                def upper(n, h, width=512):
                    if n >= 2:
                        act.wait_ge(*at(half_used, l, 2 * n + h - 3))
                    if h == 0:
                        act.wait_ge(*at(raw_in[n % 4], l, 16 * (n // 4 + 1)))
                    fn(half(tab_hi, n, h, width), half(raw, n, h, width), ACT.Copy).then_inc(hi_done.sem, 1)

                def square_sums():
                    for b in range(TB):
                        act.wait_ge(*at(layer_done, l, b + 1))
                        fn(x_lo[:, b * 4:(b + 1) * 4, :], x[:, b, :].rearrange("p (k t) -> p k t", k=4), ACT.Square,
                           accum_out=ss[:, b:b + 1]).then_inc(sq_sum.sem, 1)

                def transposed_upper(gain, ready):
                    for k in range(DT):
                        if k % 2 == 0:
                            act.wait_ge(*at(xT_ready, l, ready + k // 2 + 1))
                        fn(x_hi[:, k, :], ps[:, 4 + k // 2, (k % 2) * 256:(k % 2) * 256 + 256], ACT.Copy,
                           scale=par(gain, k)).then_inc(h_hi.sem, 1)

                square_sums()
                upper(0, 0)
                upper(0, 1)
                upper(1, 0)
                upper(1, 1)
                act.wait_ge(*at(pv_in, l, 16))
                transposed_upper("g1", 0)
                act.wait_ge(*at(sine_arg, l, 1))
                fn(f_h1, arg, ACT.Sin).then_inc(sine_done.sem, 1)
                for n in (2, 3):
                    upper(n, 0)
                    upper(n, 1)
                act.wait_ge(*at(sine_arg, l, 2))
                fn(f_h2, arg, ACT.Sin).then_inc(sine_done.sem, 1)
                for n in (4, 5):
                    upper(n, 0)
                    upper(n, 1)
                act.wait_ge(*at(filt_done, l, 2))
                fn(filt_sq, filt, ACT.Square).then_inc(filt_sq_done.sem, 1)
                upper(6, 0)
                upper(6, 1)
                act.wait_ge(*at(f_norm_ready, l, 1))
                fn(f_rn, ps[:, 6, :], ACT.Sqrt, bias=EPS).then_inc(f_root_done.sem, 1)
                upper(7, 0)
                upper(7, 1)
                for n in (8, 9):
                    upper(n, 0, 384)
                    upper(n, 1, 384)
                act.wait_ge(*at(half_used, l, 2 * (A0 + DT)))
                for g in range(3):
                    fn(p_t[:, 2 * g:2 * g + 2, 1:257], ps[:, g, :].rearrange("p (k t) -> p k t", k=2),
                       ACT.Copy).then_inc(chan_done.sem, 1)
                fn(fn_u, ps[:, 3, :].rearrange("p (k t) -> p k t", k=2), ACT.Copy).then_inc(chan_done.sem, 1)
                def z_transposed(o):
                    act.wait_ge(*at(zT_ready, l, o + 1))
                    fn(z_t, ps[:, 0, :].rearrange("p (b c) -> p b c", b=TB), ACT.Copy).then_inc(zT_done.sem, 1)

                def exponentials(u):
                    act.wait_ge(*at(max_done, l, u + 1))
                    g = u % 2
                    for s in range(4):
                        last = fn(probs[u][:, s, :],
                                  ps[:, UNIT_BANKS[u] + s // 2, (s % 2) * 256:(s % 2) * 256 + 256], ACT.Exp,
                                  bias=nmx[:, 4 * u + s:4 * u + s + 1], scale=HEAD ** -0.5,
                                  accum_out=rs[:, 4 * u + s:4 * u + s + 1])
                    last.then_inc(exp_done.sem, 1)

                def probs_transposed(u):
                    act.wait_ge(*at(pT_ready, l, u + 1))
                    fn(probs_t[:, u, 0, :, :], ps[:, UNIT_BANKS[u], :].rearrange("p (s q) -> p s q", q=P),
                       ACT.Copy).then_inc(pT_act.sem, 1)

                def attention_out(b):
                    act.wait_ge(*at(attn_ready, l, 2 * b + 2))
                    fn(mixed_sq[:, 0:4, b * P:(b + 1) * P], ps[:, 3, :].rearrange("p (k q) -> p k q", k=4),
                       ACT.Square).then_inc(attn_sq.sem, 1)
                    for k in range(4):
                        last = fn(x_hi[:, k, b * P:(b + 1) * P], ps[:, 3, k * P:(k + 1) * P], ACT.Copy,
                                  scale=par("gm", k))
                    last.then_inc(mix_hi.sem, 1)

                def output_upper(n):
                    upper(O0 + n, 0)
                    upper(O0 + n, 1)

                for n in range(10, 16):
                    upper(n, 0, 384)
                    upper(n, 1, 384)
                    if n == 12:
                        for b in range(TB):
                            act.wait_ge(*at(fn1_ready, l, b + 1))
                            fn(fn_p[:, b, :, :, :], ps[:, (3, 0)[b], :].rearrange("p (q m c) -> p q m c", q=2, m=2),
                               ACT.Copy).then_inc(fn1_done.sem, 1)
                    if n == 13:
                        z_transposed(0)
                z_transposed(1)
                for n, cols in enumerate((384, 256, 384, 256)):
                    start = (n // 2) * 640 + (n % 2) * 384
                    act.wait_ge(*at(qkv_done, l, n + 1))
                    fn(rope[:, start:start + cols], p_qkv[:, n // 2, (n % 2) * 384:(n % 2) * 384 + cols],
                       ACT.Square).then_inc(qk_sq.sem, 1)

                act.wait_ge(*at(qk_mean, l, 2))
                fn(r20, ss20, ACT.Sqrt, scale=1.0 / HEAD, bias=EPS).then_inc(qk_root.sem, 1)
                output_upper(0)
                act.wait_ge(*at(fn2_ready, l, 1))
                for q in range(2):
                    last = fn(fn_u[:, q, :], ps[:, 3, q * 256:(q + 1) * 256], ACT.Identity, bias=par("fb", q))
                last.then_inc(fn2_done.sem, 1)
                act.wait_ge(*at(rope_done, l, 1))
                for b in range(TB):
                    last = fn(k_twice[:, b, :, :, :],
                              rope[:, b * 640 + 512:(b + 1) * 640].rearrange("p (g a d) -> p g a d", g=2, a=1)
                              .broadcast_to([P, 2, 2, HEAD]), ACT.Copy)
                last.then_inc(k_twice_done.sem, 1)
                act.wait_ge(*at(fn2_done, l, 1))
                for q in range(2):
                    last = fn(x_hi[:, 6 + q, :], fn_u[:, q, :], ACT.Copy, scale=par("gm", 6 + q))
                last.then_inc(mix_hi.sem, 1)
                fn(mixed_sq[:, 6:8, :], fn_u, ACT.Square).then_inc(fnet_sq.sem, 1)
                for g in range(3):
                    dst = (q_t[:, 0:2, :], q_t[:, 2:4, :], k_t)[g]
                    act.wait_ge(*at(qkT_ready, l, g + 1))
                    fn(dst, ps[:, 4 + g, :].rearrange("p (k t) -> p k t", k=2), ACT.Copy).then_inc(qkT_done.sem, 1)
                exponentials(0)
                exponentials(1)
                exponentials(2)
                probs_transposed(0)
                probs_transposed(1)
                output_upper(1)
                exponentials(3)
                probs_transposed(2)
                attention_out(0)
                act.wait_ge(*at(hyena_done, l, 2))
                fn(mixed_sq[:, 4:6, :], conv[:, 0:2, :], ACT.Square).then_inc(hyena_sq.sem, 1)
                for q in range(2):
                    last = fn(x_hi[:, 4 + q, :], conv[:, q, :], ACT.Copy, scale=par("gm", 4 + q))
                last.then_inc(mix_hi.sem, 1)
                probs_transposed(3)
                output_upper(2)
                attention_out(1)
                output_upper(3)
                output_upper(4)
                for n in range(5, 8):
                    output_upper(n)
                upper(Q0, 0)
                upper(Q0, 1)
                act.wait_ge(*at(half_used, l, 2 * Q0))
                for b in range(TB):
                    act.wait_ge(*at(out_added, l, 8 + 2 * b + 2))
                    fn(x_lo[:, b * 4:(b + 1) * 4, :], x[:, b, :].rearrange("p (k t) -> p k t", k=4), ACT.Square,
                       accum_out=ss[:, b:b + 1]).then_inc(sq_sum.sem, 1)
                    upper(Q0 + 1, b)
                transposed_upper("g2", 4)
                for n in range(Q0 + 2, Q0 + 10):
                    upper(n, 0)
                    upper(n, 1)
                for g in range(4):
                    fn(query_t[:, 2 * g:2 * g + 2, :], ps[:, g, :].rearrange("p (k t) -> p k t", k=2),
                       ACT.Copy).then_inc(query_act.sem, 1)
                for n in range(Q0 + 10, U0 + 1):
                    upper(n, 0)
                    upper(n, 1)
                upper(U0 + 1, 0)
                upper(U0 + 1, 1)
                for g in range(4):
                    act.wait_ge(*at(scores_ready, l, 4 + g + 1))
                    fn(scores[:, 1, 4 * g:4 * g + 4, :], ps[:, 4 + g, :].rearrange("p (k n) -> p k n", k=4),
                       ACT.Copy).then_inc(scores_act.sem, 1)

                def u_upper(i, s):
                    for h in range(2):
                        act.wait_ge(*at(half_used, l, i * 8 + 2 * (U0 + s) + h - 3))
                        if h == 0:
                            act.wait_ge(*at(raw_in[s], l, i * 16 + 16 * (U0 // 4 + 1)))
                        fn(half(tab_hi, s, h), half(raw, s, h), ACT.Copy).then_inc(hi_done.sem, 1)

                def gelu(n, bank):
                    act.wait_ge(*at(half_used, l, n * 4 + 2 * U0 + 4))
                    fn(work[:, bass.ds(2 * n, 2), :], ps[:, bank, :].rearrange("p (k t) -> p k t", k=2),
                       ACT.Gelu).then_inc(gelu_done.sem, 1)

                def u_quad(i):
                    u_upper(i, 0)
                    u_upper(i, 1)
                    gelu(i * 2 - 1, 1)
                    u_upper(i, 2)
                    u_upper(i, 3)
                    gelu(i * 2, 0)

                u_upper(0, 2)
                u_upper(0, 3)
                gelu(0, 0)
                with act.Fori(1, 8) as i:
                    u_quad(i)
                act.wait_ge(*at(best_done, l, 1))
                fn(best.rearrange("p b h n -> p (b h n)"), best.rearrange("p b h n -> p (b h n)"),
                   ACT.Exp).then_inc(gate_exp.sem, 1)
                u_quad(8)
                with act.Fori(9, GUARD // 4) as i:
                    u_quad(i)
                act.wait_ge(*at(topk_done, l, 1))
                with act.Fori(GUARD // 4, 32) as i:
                    u_quad(i)
                gelu(63, 1)

                def absolute(i, s, first=False):
                    if not first:
                        act.wait_ge(*at(hot_j_act, l, i * 3 + s - 2))
                    for t in range(4):
                        last = fn(dist_abs[:, s, t, :], iota, ACT.Abs, bias=minus_j[:, bass.ds(i * 16 + 4 * s + t, 1)])
                    last.then_inc(abs_done.sem, 1)

                def one_hot_j(i, s, first=False):
                    if not first:
                        act.wait_ge(*at(gates_ready, l, i * 4 + s - 1))
                    act.wait_ge(*at(abs_done, l, i * 3 + s + 1))
                    fn(onehot[:, s % 2, 1, :, :], dist_abs[:, s, :, :].bitcast(F32), ACT.Relu, scale=-1.0, bias=1.0)\
                        .then_inc(hot_j_act.sem, 1)

                act.wait_ge(*at(picksT_done, l, 1))

                def hot_body(i, first=False, last=False):
                    for s in range(3):
                        if s < 2:
                            absolute(i, s + 1, first)
                        elif not last:
                            absolute(i + 1, 0)
                        one_hot_j(i, s, first and s < 2)

                absolute(0, 0, True)
                hot_body(0, first=True)
                with act.Fori(1, 15) as i:
                    hot_body(i)
                hot_body(15, last=True)

                def weight_upper(i, s):
                    fn(w_hi[:, s % 2, :], work[:, i * 4 + s, :], ACT.Copy).then_inc(whi_done.sem, 1)

                def v_quad(i, first=False):
                    for s in range(4):
                        for h in range(2):
                            act.wait_ge(*at(half_used, l, i * 8 + 2 * (V0 + s) + h - 3))
                            if h == 0:
                                act.wait_ge(*at(raw_in[s], l, i * 16 + 16 * (V0 // 4 + 1)))
                            elif s >= 2 or not first:
                                weight_upper(i, s)
                            fn(half(tab_hi, s, h), half(raw, s, h), ACT.Copy).then_inc(hi_done.sem, 1)
                        if first and s == 1:
                            act.wait_ge(*at(weighted, l, 64))
                            weight_upper(i, 0)
                            weight_upper(i, 1)

                v_quad(0, True)
                with act.Fori(1, 32) as i:
                    v_quad(i)
            act.wait_ge(*at(layer_done, DEPTH, TB))
            for b in range(TB):
                fn(x_lo[:, b * 4:(b + 1) * 4, :], x[:, b, :].rearrange("p (k t) -> p k t", k=4), ACT.Square,
                   accum_out=ss[:, b:b + 1]).then_inc(sq_sum.sem, 1)

        @block.gpsimd
        def _(pool):
            tt = nc.gpsimd.tensor_tensor
            pool.wait_ge(const_in.sem, 16)
            with pool.Fori(0, DEPTH) as l:
                def inverse_root(n, dst, src, width):
                    pool.wait_ge(*at(mean_sq, l, n))
                    tt(dst, src, neg_half.broadcast_to([P, width]), ALU.pow).then_inc(inv_root.sem, 1)

                def lower(n, h, width=512):
                    if n >= 2:
                        pool.wait_ge(*at(half_used, l, 2 * n + h - 3))
                    pool.wait_ge(*at(hi_done, l, 2 * n + h + 1))
                    tt(half(tab_lo, n, h, width), half(raw, n, h, width), half(tab_hi, n, h, width).bitcast(F32),
                       ALU.subtract).then_inc(lo_pool.sem, 1)

                pool.wait_ge(*at(layer_done, l, TB))
                inverse_root(1, rinv, ms, 2)
                for n in range(A0, B0):
                    lower(n, 0)
                    lower(n, 1)
                pool.wait_ge(*at(gqk_in, l, 16))
                g5 = gqk.rearrange("p (h a e d) -> p h a e d", h=10, a=2, e=2)
                for b in range(TB):
                    tt(cos_g[:, b, :].rearrange("p (h d) -> p h d", d=HEAD), gqk.rearrange("p (h d) -> p h d", d=HEAD),
                       cos_r[:, b:b + 1, :].broadcast_to([P, 10, HEAD]), ALU.mult)
                    sins = sin_r[:, b:b + 1, :].rearrange("p o (a e d) -> p o a e d", a=2, e=2)
                    sing = sin_g[:, b, :].rearrange("p (h a e d) -> p h a e d", h=10, a=2, e=2)
                    for e in range(2):
                        last = tt(sing[:, :, :, e, :], g5[:, :, :, 1 - e, :],
                                  sins[:, :, :, e, :].broadcast_to([P, 10, 2, 16]), ALU.mult)
                last.then_inc(rope_tab_done.sem, 1)
                for n in range(B0, O0):
                    lower(n, 0, 384)
                    lower(n, 1, 384)
                pool.wait_ge(*at(qn_done, l, 1))
                pool.wait_ge(*at(rope_tab_done, l, 1))
                crossed(tt, 0).then_inc(rot_done.sem, 1)
                for n in range(O0, O0 + 2):
                    lower(n, 0)
                    lower(n, 1)
                inverse_root(2, r6[:, 4:6], ms6[:, 4:6], 2)
                for n in range(O0 + 2, Q0):
                    if n == O0 + 4:
                        inverse_root(3, r6[:, 2:4], ms6[:, 2:4], 2)
                    if n == O0 + 6:
                        inverse_root(4, r6[:, 0:2], ms6[:, 0:2], 2)
                    lower(n, 0)
                    lower(n, 1)
                inverse_root(5, rinv, ms, 2)

                def u_lower(i):
                    for s in range(4):
                        for h in range(2):
                            pool.wait_ge(*at(half_used, l, i * 8 + 2 * (U0 + s) + h - 3))
                            pool.wait_ge(*at(hi_done, l, i * 8 + 2 * (U0 + s) + h + 1))
                            tt(half(tab_lo, s, h), half(raw, s, h), half(tab_hi, s, h).bitcast(F32),
                               ALU.subtract).then_inc(lo_pool.sem, 1)

                with pool.Fori(0, EARLY // 4) as i:
                    u_lower(i)

                def scale_hot(i, first=False):
                    for s in range(4):
                        n = i * 4 + s
                        if s >= 2 or not first:
                            pool.wait_ge(*at(gates_ready, l, n - 1))
                        pool.wait_ge(*at(hot_i, l, n + 1))
                        tt(onehot[:, s % 2, 0, :, :], hot_rows[:, s, :, :].bitcast(F32),
                           picks[:, 2, bass.ds(n * 4, 4)].rearrange("p (t a) -> p t a", a=1).broadcast_to([P, 4, P]),
                           ALU.mult).then_inc(hot_scaled.sem, 1)

                scale_hot(0, True)
                with pool.Fori(1, 16) as i:
                    scale_hot(i)
            pool.wait_ge(mean_sq.sem, DEPTH * 5 + 1)
            tt(rinv, ms, neg_half.broadcast_to([P, 2]), ALU.pow).then_inc(inv_root.sem, 1)

        @block.vector
        def _(dve):
            v = nc.vector
            dve.wait_ge(x_landed.sem, 16)
            for b in range(TB):
                v.memset(small[:, 126 + b:127 + b], 0.0).then_inc(layer_done.sem, 1)
            dve.wait_ge(const_in.sem, 16)
            with dve.Fori(0, DEPTH) as l:
                count = [0]

                def link(ins):
                    count[0] += 1
                    ins.then_inc(dve_step.sem, 1)
                    dve.wait_ge(*at(dve_step, l, count[0]))

                def norm_scale(n):
                    dve.wait_ge(*at(sq_sum, l, 2 * n + 2))
                    v.tensor_scalar(ms, ss, 1.0 / D, EPS, ALU.mult, ALU.add).then_inc(mean_sq.sem, 1)
                    dve.wait_ge(*at(inv_root, l, (1, 5)[n]))
                    for b in range(TB):
                        v.tensor_scalar(xn[:, b, :], x[:, b, :], rinv[:, b:b + 1], None, ALU.mult)\
                            .then_inc(xn_done.sem, 1)

                def transposed_lower(gain, done):
                    for k in range(DT):
                        if k % 2 == 0:
                            dve.wait_ge(*at(h_hi, l, done + k + 2))
                        v.scalar_tensor_tensor(x_lo[:, k, :], ps[:, 4 + k // 2, (k % 2) * 256:(k % 2) * 256 + 256],
                                               par(gain, k), x_hi[:, k, :].bitcast(F32), ALU.mult, ALU.subtract)\
                            .then_inc(h_lo.sem, 1)

                def sine_argument(n, bank):
                    dve.wait_ge(*at(mlp_ready, l, n + 1))
                    link(v.tensor_scalar(arg, ps[0:64, bank, 0:256], par(("b1", "b2")[n], rows=64),
                                         par(("f1", "f2")[n], rows=64), ALU.add, ALU.mult))
                    link(v.tensor_scalar(turns, arg, INV_2PI, ROUND, ALU.mult, ALU.add))
                    link(v.tensor_scalar(turns, turns, ROUND, None, ALU.subtract))
                    for part in TWO_PI:
                        link(v.scalar_tensor_tensor(arg, turns, -part, arg, ALU.mult, ALU.add))
                    v.tensor_scalar(arg, arg, SIN_MAX, -SIN_MAX, ALU.min, ALU.max).then_inc(sine_arg.sem, 1)

                norm_scale(0)
                dve.wait_ge(*at(pv_in, l, 16))
                sine_argument(0, 0)
                transposed_lower("g1", 0)
                dve.wait_ge(*at(sine_done, l, 1))
                sine_argument(1, 4)
                dve.wait_ge(*at(sine_done, l, 2))
                dve.wait_ge(*at(params_in, l, 48))
                for b in range(TB):
                    dve.wait_ge(*at(taps_ready, l, b + 1))
                    bank = (6, 4)[b]
                    v.tensor_tensor(filt[:, b, :, :, :].rearrange("p o e c -> p (o e) c"),
                                    ps[:, bank:bank + 2, :].rearrange("p k (e c) -> p (k e) c", c=256),
                                    decay[:, b:b + 1, :].broadcast_to([P, 4, 256]), ALU.mult)\
                        .then_inc(filt_done.sem, 1)
                dve.wait_ge(*at(filt_done, l, 2))
                for b in range(TB):
                    mask = kc[:, KC["not_first"]:KC["not_first"] + 1] if b == 0 else 1.0
                    v.scalar_tensor_tensor(f_sum[:, b, :, :], filt[:, b, :, 1, :], mask, filt[:, b, :, 0, :],
                                           ALU.mult, ALU.add)
                    last = v.tensor_tensor(f_dif[:, b, :, :], filt[:, b, :, 1, :], filt[:, b, :, 0, :], ALU.subtract)
                last.then_inc(sumdif_done.sem, 1)
                dve.wait_ge(*at(f_root_done, l, 1))
                link(v.reciprocal(f_rn, f_rn))
                for n, bank in enumerate((4, 5, 7, 6, 4)):
                    dve.wait_ge(*at(spec_ready, l, n + 1))
                    v.tensor_tensor(spec[:, n, :, :].rearrange("p o c -> p (o c)"), ps[:, bank, :], f_rn, ALU.mult)\
                        .then_inc(spec_done.sem, 1)
                dve.wait_ge(*at(fn_m_ready, l, 1))
                v.tensor_copy(fn_m.rearrange("p m q c -> p (m q c)"), ps[:, 5, :]).then_inc(fn_m_done.sem, 1)
                v.memset(p_t[:, :, 0:1], 0.0)
                link(v.memset(p_t[:, :, 257:258], 0.0))
                dve.wait_ge(*at(chan_done, l, 3))
                for c in range(6):
                    last = v.tensor_scalar(conv[:, c, :], p_t[:, c, 0:256], par("cw", c), par("cb", c), ALU.mult, ALU.add)
                link(last)
                for tap in (1, 2):
                    for c in range(6):
                        last = v.scalar_tensor_tensor(conv[:, c, :], p_t[:, c, tap:tap + 256], par("cw", 6 * tap + c),
                                                      conv[:, c, :], ALU.mult, ALU.add)
                    if tap == 1:
                        link(last)
                last.then_inc(conv_done.sem, 1)
                def hyena_multiply(o):
                    dve.wait_ge(*at(u_spec_ready, l, o + 1))
                    re = ps[:, 1, :].rearrange("p (k c) -> p k c", k=2)
                    im = ps[:, 2, :].rearrange("p (k c) -> p k c", k=2)
                    v.tensor_tensor(prod[:, 0, :, :], re, spec[:, 0:2, o, :], ALU.mult)
                    v.tensor_tensor(prod[:, 1, :, :], im, spec[:, 2:4, o, :], ALU.mult)
                    v.tensor_tensor(prod[:, 2, :, :], re, spec[:, 2:4, o, :], ALU.mult)
                    v.tensor_tensor(prod[:, 3, 0, :], im[:, 0, :], spec[:, 4, o, :], ALU.mult)
                    link(v.tensor_tensor(prod[:, 3, 1, :], im[:, 1, :], spec[:, 1, o, :], ALU.mult))
                    v.tensor_tensor(y_spec[:, 0, :, :], prod[:, 0, :, :], prod[:, 1, :, :], ALU.subtract)
                    v.tensor_tensor(y_spec[:, 1, :, :], prod[:, 2, :, :], prod[:, 3, :, :], ALU.add)\
                        .then_inc(y_spec_done.sem, 1)

                def hyena_gate(o):
                    dve.wait_ge(*at(y_ready, l, o + 1))
                    dve.wait_ge(*at(y_spec_done, l, o + 1))
                    for c in range(2):
                        last = v.scalar_tensor_tensor(prod[:, 0, c, :], conv[:, c, :], par("hb", 2 * o + c),
                                                      ps[:, 0, c * 256:(c + 1) * 256], ALU.mult, ALU.add)
                    link(last)
                    v.tensor_tensor(conv[:, 0:2, :], prod[:, 0, :, :], conv[:, 2 + 2 * o:4 + 2 * o, :], ALU.mult)\
                        .then_inc(hyena_done.sem, 1)

                def softmax_max(u):
                    g = u % 2
                    dve.wait_ge(*at(att_ready, l, u + 1))
                    link(v.tensor_reduce(mx[:, 4 * u:4 * u + 4],
                                         ps[:, UNIT_BANKS[u]:UNIT_BANKS[u] + 2, :]
                                         .rearrange("p k (s n) -> p (k s) n", n=256),
                                         AX.X, ALU.max))
                    v.tensor_scalar(nmx[:, 4 * u:4 * u + 4], mx[:, 4 * u:4 * u + 4], -HEAD ** -0.5, None, ALU.mult)\
                        .then_inc(max_done.sem, 1)

                def softmax_scale(u):
                    g = u % 2
                    dve.wait_ge(*at(exp_done, l, u + 1))
                    link(v.reciprocal(rrs[:, 4 * u:4 * u + 4], rs[:, 4 * u:4 * u + 4]))
                    v.tensor_tensor(probs[u], probs[u],
                                    rrs[:, 4 * u:4 * u + 4].rearrange("p (s a) -> p s a", a=1)
                                    .broadcast_to([P, 4, 256]), ALU.mult).then_inc(probs_done.sem, 1)

                def probs_transposed(u):
                    dve.wait_ge(*at(pT_ready, l, u + 1))
                    v.tensor_copy(probs_t[:, u, 1, :, :],
                                  ps[:, UNIT_BANKS[u] + 1, :].rearrange("p (s q) -> p s q", q=P))\
                        .then_inc(pT_dve.sem, 1)

                def mixed_lower(n, parts):
                    dve.wait_ge(*at(mix_hi, l, n))
                    for k, tok, src in parts:
                        last = v.scalar_tensor_tensor(x_lo[:, k, tok], src, par("gm", k),
                                                      x_hi[:, k, tok].bitcast(F32), ALU.mult, ALU.subtract)
                    last.then_inc(mix_lo.sem, 1)

                def attention_lower(n, b):
                    mixed_lower(n, [(k, slice(b * P, (b + 1) * P), ps[:, 3, k * P:(k + 1) * P]) for k in range(4)])

                def lower(n, h):
                    dve.wait_ge(*at(half_used, l, 2 * n + h - 3))
                    dve.wait_ge(*at(hi_done, l, 2 * n + h + 1))
                    v.tensor_tensor(half(tab_lo, n, h), half(raw, n, h), half(tab_hi, n, h).bitcast(F32),
                                    ALU.subtract).then_inc(lo_dve.sem, 1)

                def group_mean(n, g, width, bank):
                    dve.wait_ge(*at(group_ready, l, n))
                    v.tensor_scalar(ms6[:, 2 * g:2 * g + 2], ps[:, bank, 0:2], 1.0 / width, EPS, ALU.mult,
                                    ALU.add).then_inc(mean_sq.sem, 1)

                def add_group(n, g, banks):
                    dve.wait_ge(*(at(out_first, l, 1) if n == 2 else at(half_used, l, 2 * (O0 + 2 * n + 2))))
                    dve.wait_ge(*at(inv_root, l, 2 + n))
                    if n:
                        dve.wait_ge(*at(out_added, l, 4 * n))
                    for b in range(TB):
                        if n == 2 and b == 1:
                            dve.wait_ge(*at(half_used, l, 2 * Q0))
                        for h in range(2):
                            v.scalar_tensor_tensor(x[:, b, h * 512:(h + 1) * 512], ps[:, banks[b][h], :],
                                                   r6[:, 2 * g + b:2 * g + b + 1], x[:, b, h * 512:(h + 1) * 512],
                                                   ALU.mult, ALU.add).then_inc(out_added.sem, 1)

                hyena_multiply(0)
                hyena_gate(0)
                dve.wait_ge(*at(half_used, l, 2 * (B0 + DT)))
                for n in range(4):
                    v.tensor_copy(p_qkv[:, n // 2, (n % 2) * 384:(n % 2) * 384 + 384], ps[:, 4 + n, 0:384])\
                        .then_inc(qkv_done.sem, 1)
                rope3 = rope.rearrange("p (b n) -> p b n", b=TB)
                qn3 = qn.rearrange("p (b n) -> p b n", b=TB)
                for b in range(TB):
                    dve.wait_ge(*at(qk_sq, l, 2 * b + 2))
                    v.tensor_reduce(ss20[:, 10 * b:10 * b + 10], rope3[:, b, :].rearrange("p (n d) -> p n d", d=HEAD),
                                    AX.X, ALU.add).then_inc(qk_mean.sem, 1)
                dve.wait_ge(*at(qkv_done, l, 4))
                dve.wait_ge(*at(qk_mean, l, 2))
                v.tensor_scalar(ms20, ss20, 1.0 / HEAD, EPS, ALU.mult, ALU.add)
                dve.wait_ge(*at(qk_root, l, 1))
                link(v.reciprocal(r20, r20))
                link(v.tensor_tensor(ss20, r20, r20, ALU.mult))
                link(v.scalar_tensor_tensor(ss20, ss20, -0.5, ms20, ALU.mult, ALU.mult))
                link(v.scalar_tensor_tensor(r20, ss20, 1.5, r20, ALU.add, ALU.mult))
                for b in range(TB):
                    v.tensor_tensor(qn3[:, b, :].rearrange("p (h d) -> p h d", d=HEAD),
                                    p_qkv[:, b, 0:640].rearrange("p (h d) -> p h d", d=HEAD),
                                    r20[:, b * 10:(b + 1) * 10].rearrange("p (h a) -> p h a", a=1)
                                    .broadcast_to([P, 10, HEAD]), ALU.mult).then_inc(qn_done.sem, 1)
                dve.wait_ge(*at(qn_done, l, 2))
                dve.wait_ge(*at(rope_tab_done, l, 1))
                v.tensor_tensor(rope3, qn3, cos_g, ALU.mult)
                link(crossed(v.tensor_tensor, 1))
                dve.wait_ge(*at(rot_done, l, 1))
                v.tensor_tensor(rope, rope, rot, ALU.add).then_inc(rope_done.sem, 1)
                mixed_lower(1, [(6 + q, slice(0, SEQ), fn_u[:, q, :]) for q in range(2)])
                hyena_multiply(1)
                softmax_max(0)
                softmax_max(1)
                softmax_scale(0)
                softmax_max(2)
                softmax_scale(1)
                probs_transposed(0)
                probs_transposed(1)
                softmax_scale(2)
                hyena_gate(1)
                softmax_max(3)
                probs_transposed(2)
                softmax_scale(3)
                attention_lower(2, 0)
                group_mean(1, 2, FN_W, FNET_SUMS)
                mixed_lower(3, [(4 + q, slice(0, SEQ), conv[:, q, :]) for q in range(2)])
                probs_transposed(3)
                add_group(0, 2, FNET_BANKS)
                attention_lower(4, 1)
                group_mean(2, 1, HY_W, HYENA_SUMS)
                add_group(1, 1, HYENA_BANKS)
                group_mean(3, 0, A_W, ATTN_SUMS)
                lower(Q0, 0)
                lower(Q0, 1)
                add_group(2, 0, ATTN_BANKS)
                dve.wait_ge(*at(out_added, l, 12))
                norm_scale(1)
                lower(Q0 + 1, 0)
                lower(Q0 + 1, 1)
                transposed_lower("g2", 8)

                for n in range(Q0 + 2, U0):
                    lower(n, 0)
                    lower(n, 1)
                dve.wait_ge(*at(half_used, l, 2 * U0))
                for g in range(4):
                    v.tensor_copy(query_t[:, 8 + 2 * g:10 + 2 * g, :],
                                  ps[:, 4 + g, :].rearrange("p (k t) -> p k t", k=2)).then_inc(query_dve.sem, 1)
                for g in range(4):
                    dve.wait_ge(*at(scores_ready, l, g + 1))
                    if g == 3:
                        dve.wait_ge(*at(scores_act, l, 4))
                    v.tensor_copy(scores[:, 0, 4 * g:4 * g + 4, :], ps[:, g, :].rearrange("p (k n) -> p k n", k=4))\
                        .then_inc(scores_dve.sem, 1)
                settled(dve)

                def top16(values, indices, row, rows):
                    steps = (lambda r: v.max(values(r)[:, 0:8], row(r)),
                             lambda r: v.max_index(indices(r)[:, 0:8], values(r)[:, 0:8], row(r)),
                             lambda r: v.match_replace(row(r), values(r)[:, 0:8], row(r), NEG),
                             lambda r: v.max(values(r)[:, 8:16], row(r)),
                             lambda r: v.max_index(indices(r)[:, 8:16], values(r)[:, 8:16], row(r)))
                    for step in steps:
                        for r in range(rows):
                            last = step(r)
                        settled(dve)

                for b in range(TB):
                    top16(lambda r: v_top[:, b, r, :], lambda r: i_top[:, b, r, :], lambda r: scores[:, b, r, :], HP)
                link(v.tensor_copy(i_topf, i_top))
                for b in range(TB):
                    side = v_top[:, b, :, :].rearrange("p (h s) n -> p h s n", s=2)
                    v.tensor_tensor(
                        cand, side[:, :, 0, :].rearrange("p h (n a) -> p h n a", a=1).broadcast_to([P, PH, 16, 16]),
                        side[:, :, 1:2, :].broadcast_to([P, PH, 16, 16]), ALU.add)
                    settled(dve)
                    top16(lambda r: best[:, b, r, :], lambda r: pos[:, b, r * 16:(r + 1) * 16],
                          lambda r: cand[:, r, :, :].rearrange("p a b -> p (a b)"), PH)
                bests = best.rearrange("p b h n -> p (b h) n")
                link(v.tensor_copy(ssg.rearrange("p (n a) -> p n a", a=1), bests[:, :, 0:1]))
                v.tensor_tensor(bests, bests, ssg.rearrange("p (n a) -> p n a", a=1).broadcast_to([P, 16, 16]),
                                ALU.subtract).then_inc(best_done.sem, 1)
                for b in range(TB):
                    link(v.tensor_single_scalar(place_u[:, 0, :], pos[:, b, :], 4, op=ALU.logical_shift_right))
                    link(v.tensor_single_scalar(place_u[:, 1, :], pos[:, b, :], 15, op=ALU.bitwise_and))
                    link(v.tensor_copy(place_f, place_u))
                    for s in range(2):
                        link(v.tensor_tensor(
                            eq, place_f[:, s, :].rearrange("p (n a) -> p n a", a=1).broadcast_to([P, PICKS, TOPK]),
                            iota16.rearrange("p (a n) -> p a n", a=1).broadcast_to([P, PICKS, TOPK]), ALU.is_equal))
                        side = i_topf[:, b, :, :].rearrange("p (h s) n -> p h s n", s=2)[:, :, s:s + 1, :]
                        eq4 = eq.rearrange("p (h k) r -> p h k r", h=PH)
                        link(v.tensor_tensor(eq4, eq4, side.broadcast_to([P, PH, TOPK, TOPK]), ALU.mult))
                        link(v.tensor_reduce(chosen[:, s, b, :], eq, AX.X, ALU.add))
                dve.wait_ge(*at(gate_exp, l, 1))
                link(v.tensor_reduce(ssg, bests, AX.X, ALU.add))
                link(v.reciprocal(ssg, ssg))
                v.tensor_tensor(chosen[:, 2, :, :].rearrange("p b (h n) -> p (b h) n", n=16), bests,
                                ssg.rearrange("p (n a) -> p n a", a=1).broadcast_to([P, 16, 16]), ALU.mult)\
                    .then_inc(topk_done.sem, 1)
                def u_lower(i):
                    for s in range(4):
                        for h in range(2):
                            dve.wait_ge(*at(half_used, l, i * 8 + 2 * (U0 + s) + h - 3))
                            dve.wait_ge(*at(hi_done, l, i * 8 + 2 * (U0 + s) + h + 1))
                            v.tensor_tensor(half(tab_lo, s, h), half(raw, s, h), half(tab_hi, s, h).bitcast(F32),
                                            ALU.subtract).then_inc(lo_dve.sem, 1)

                settled(dve)
                with dve.Fori(EARLY // 4, GUARD // 4 + 1) as i:
                    u_lower(i)
                dve.wait_ge(*at(picksT_ready, l, 1))
                v.tensor_copy(picks[:, 0:2, :], ps[:, 4, :].rearrange("p (n t) -> p n t", n=2))
                v.tensor_single_scalar(minus_j, ps[:, 4, SEQ:2 * SEQ], -1.0, op=ALU.mult)
                v.tensor_copy(picks[:, 2, :], ps[:, 5, 0:256]).then_inc(picksT_done.sem, 1)
                settled(dve)
                with dve.Fori(GUARD // 4 + 1, 32) as i:
                    u_lower(i)
                dve.wait_ge(*at(half_used, l, 2 * V0))

                def one_hot(rows, side, n, signal):
                    v.tensor_tensor(rows, iota.rearrange("p (a c) -> p a c", a=1).broadcast_to([P, 4, P]),
                                    picks[:, side, bass.ds(n * 4, 4)].rearrange("p (t a) -> p t a", a=1)
                                    .broadcast_to([P, 4, P]), ALU.is_equal).then_inc(signal.sem, 1)

                def one_hot_i(i, s, first=False):
                    if not first:
                        dve.wait_ge(*at(hot_scaled, l, i * 4 + s - 3))
                    one_hot(hot_rows[:, s, :, :], 0, i * 4 + s, hot_i)

                def v_lower(i, s, h):
                    dve.wait_ge(*at(half_used, l, i * 8 + 2 * (V0 + s) + h - 3))
                    dve.wait_ge(*at(hi_done, l, i * 8 + 2 * (V0 + s) + h + 1))
                    v.tensor_tensor(half(tab_lo, s, h), half(raw, s, h), half(tab_hi, s, h).bitcast(F32),
                                    ALU.subtract).then_inc(lo_dve.sem, 1)

                def gate_body(i, first=False, last=False):
                    for s in range(4):
                        n = i * 4 + s
                        if s == 0:
                            one_hot_i(i, 3, first)
                        elif not last:
                            one_hot_i(i + 1, s - 1)
                        if last and s == 3:
                            v_lower(0, 0, 0)
                        dve.wait_ge(*at(gates_ready, l, n + 1))
                        if s == 1:
                            one_hot(onehot[:, 1, 1, :, :], 1, n + 2, hot_j_dve)
                        cell = work[:, :, bass.ds(n * 4, 4)]
                        v.tensor_tensor(cell, ps[:, 2 + s, :].rearrange("p (t j) -> p j t", t=4), cell, ALU.mult)\
                            .then_inc(weighted.sem, 1)

                one_hot_i(0, 0, True)
                one_hot_i(0, 1, True)
                one_hot_i(0, 2, True)
                dve.wait_ge(*at(gelu_done, l, 64))
                gate_body(0, first=True)
                with dve.Fori(1, 15) as i:
                    gate_body(i)
                gate_body(15, last=True)
                settled(dve)

                def v_quad(i, first=False):
                    for s in range(4):
                        if s or not first:
                            v_lower(i, s, 0)
                        v_lower(i, s, 1)
                        dve.wait_ge(*at(whi_done, l, i * 4 + s + 1))
                        v.tensor_tensor(w_lo[:, s % 2, :], work[:, i * 4 + s, :], w_hi[:, s % 2, :].bitcast(F32),
                                        ALU.subtract).then_inc(wlo_done.sem, 1)

                v_quad(0, True)
                settled(dve)
                with dve.Fori(1, 32) as i:
                    v_quad(i)
                dve.wait_ge(*at(first_block, l, 1))
                for b in range(TB):
                    if b == 1:
                        dve.wait_ge(*at(half_used, l, 2 * TILES))
                    v.tensor_tensor(x[:, b, :], ps[:, 4 + 2 * b:6 + 2 * b, :].rearrange("p k n -> p (k n)"), x[:, b, :],
                                    ALU.add).then_inc(layer_done.sem, 1)
                assert count[0] == dve_step.per_layer, f"dve_step counts {count[0]} per layer"
                dve.wait_ge(*at(layer_done, l, 2 * TB))
            dve.wait_ge(sq_sum.sem, DEPTH * 4 + 2)
            v.tensor_scalar(ms, ss, 1.0 / D, EPS, ALU.mult, ALU.add).then_inc(mean_sq.sem, 1)
            dve.wait_ge(inv_root.sem, DEPTH * 5 + 1)
            dve.wait_ge(fg_in.sem, 16)
            for b in range(TB):
                last = v.scalar_tensor_tensor(xn[:, b, :], x[:, b, :], rinv[:, b:b + 1], area(8192, D), ALU.mult,
                                              ALU.mult)
            last.then_inc(fin.sem, 1)


def constants():
    import numpy as np
    f32 = np.float32
    kc = np.zeros((P, KC_N), f32)
    kc[:, KC["ident"]:KC["ident"] + P] = np.eye(P)
    kc[:, KC["iota"]:KC["iota"] + P] = np.arange(P)
    kc[:, KC["ones"]:KC["ones"] + P] = 1.0
    row = np.repeat(np.arange(SEQ // 64), 64).astype(f32)
    col = np.tile(np.arange(64), SEQ // 64).astype(f32)
    inv = (f32(10000.0) ** (-np.arange(16, dtype=f32) / f32(16))).astype(f32)
    ang = np.stack([row[:, None] * inv, col[:, None] * inv], axis=1)
    cos = np.stack([np.cos(ang), np.cos(ang)], axis=2).reshape(TB, P, 64)
    sin = np.stack([-np.sin(ang), np.sin(ang)], axis=2).reshape(TB, P, 64)
    kc[:, KC["cos"]:KC["cos"] + 128] = cos.transpose(1, 0, 2).reshape(P, 128)
    kc[:, KC["sin"]:KC["sin"] + 128] = sin.transpose(1, 0, 2).reshape(P, 128)
    kc[:, KC["neg_half"]] = -0.5
    kc[:, KC["not_first"]] = 1.0
    kc[0, KC["not_first"]] = 0.0
    kc[:, KC["iota16"]:KC["iota16"] + 16] = np.arange(16)

    def tiles(m):
        return m.reshape(TB, P, -1).transpose(1, 0, 2).reshape(P, -1)

    cf = np.zeros((P, CF_N), f32)
    t = np.linspace(0.0, 1.0, SEQ, dtype=f32)[:, None]
    bands = np.arange(1, 9, dtype=f32)
    a = (f32(2.0 * np.pi) * t * bands).astype(f32)
    z = np.concatenate([t, np.sin(a), np.cos(a)], axis=-1)
    cf[0:17, CF["z"]:CF["z"] + 256] = z.T
    rates = np.linspace(-np.log(1e-2) / 1.5, -np.log(1e-2) / 0.3, HY_W, dtype=f32)
    cf[:, CF["decay"]:CF["decay"] + 512] = tiles(np.exp(-t * rates))
    n = np.arange(SEQ)
    w = 2 * np.pi * ((n[:, None] * n[None, :]) % 512) / 512
    nyq = (-1.0) ** n
    c, s = np.cos(w), np.sin(w)
    cf[:, CF["sin0"]:CF["sin0"] + 512] = tiles(s)
    cn = c[:, 0:P].copy()
    cn[:, 0] = nyq
    cf[:, CF["cosn"]:CF["cosn"] + 256] = tiles(cn)
    k = np.arange(64)
    wk = 2 * np.pi * ((k[:, None] * k[None, :]) % 64) / 64
    for g in range(2):
        cf[g * 64:(g + 1) * 64, CF["bc"] + g * 64:CF["bc"] + (g + 1) * 64] = np.cos(wk) / 128.0
        cf[g * 64:(g + 1) * 64, CF["bs"] + g * 64:CF["bs"] + (g + 1) * 64] = -np.sin(wk) / 128.0
    cd = np.zeros((P, CD_N), f32)
    sp = -s.copy()
    sp[:, 0] = nyq
    ic = c * (2.0 / 512)
    ic[0, :] = 1.0 / 512
    isn = -s * (2.0 / 512)
    isn[0, :] = nyq / 512
    wl = 2 * np.pi * ((n[:, None] * n[None, :]) % SEQ) / SEQ
    for name, m in (("cos", c), ("sin", sp), ("icos", ic), ("isin", isn), ("fc", np.cos(wl)), ("fs", np.sin(wl))):
        cd[:, CD[name]:CD[name] + 512] = tiles(m)
    return kc, cf, cd


def layouts(i):
    import numpy as np
    f32 = np.float32
    a = {k: np.asarray(v) for k, v in i.items()}
    pvec = np.zeros((DEPTH, P, PV_N), f32)

    def cols(v, k):
        return v.reshape(DEPTH, k, P).transpose(0, 2, 1)

    pvec[:, :, 0:8] = cols(a["norm1_g"], 8)
    pvec[:, :, 8:16] = cols(a["norm2_g"], 8)
    pvec[:, :, 16:24] = cols(a["mix_norm_g"], 8)
    pvec[:, :, 24:42] = cols(a["hy_conv_w"], 18)
    pvec[:, :, 42:48] = cols(a["hy_conv_b"], 6)
    pvec[:, :, 48:52] = cols(a["hy_bias"], 4)
    pvec[:, :, 52:54] = cols(a["fn_b"], 2)
    for n, name in enumerate(("hy_b1", "hy_freq1", "hy_b2", "hy_freq2")):
        pvec[:, 0:64, 54 + n] = a[name]
    pmat = np.zeros((DEPTH, P, PM_N), f32)
    pmat[:, 0:17, 0:64] = a["hy_w1"]
    pmat[:, 0:64, 64:128] = a["hy_w2"]
    pmat[:, 0:64, 128:1152] = a["hy_w3"]
    for g in range(4):
        q, h = g // 2, g % 2
        pmat[:, h * 64:(h + 1) * 64, 1152 + q * P + h * 64:1152 + q * P + (h + 1) * 64] = a["fn_w"][:, g]
    gqk = np.concatenate([np.tile(a["q_norm_g"], (1, 8)), np.tile(a["k_norm_g"], (1, 2))], axis=1)
    gqk = np.ascontiguousarray(np.broadcast_to(gqk[:, None, :], (DEPTH, P, 640)))
    subk = np.ascontiguousarray(a["peer_sub_keys"].transpose(0, 4, 2, 1, 3).reshape(DEPTH, P, HP * KEYS))
    tu = np.ascontiguousarray(a["peer_u"].reshape(DEPTH, P, P, DT, P).transpose(0, 2, 4, 3, 1).reshape(DEPTH, P, P, D))
    tv = np.ascontiguousarray(a["peer_v"].reshape(DEPTH, P, P, D).transpose(0, 2, 1, 3))
    w_proj = np.concatenate([a["w_in"][:, :, QKV:], a["w_in"][:, :, :QKV], a["w_out"], a["peer_w_query"]], axis=2)
    kc, cf, cd = constants()
    return {
        "x_in": a["x"].reshape(SEQ, D), "w_proj": w_proj,
        "sub_keys": subk, "tab_u": tu, "tab_v": tv, "pvec": pvec, "pmat": pmat, "gain_qk": gqk, "kconst": kc,
        "cfilter": cf, "cdft": cd,
        "final_g": np.ascontiguousarray(np.broadcast_to(a["final_g"][None, :], (P, D))),
    }


def kernel(**inputs):
    import concourse.bacc as bacc
    from concourse.bass_utils import run_bass_kernel_spmd

    nc = bacc.Bacc("TRN2", target_bir_lowering=False, num_devices=1)
    arrays = layouts(inputs)
    args = [nc.dram_tensor(name, v.shape, mybir.dt.from_np(v.dtype), kind="ExternalInput").ap()
            for name, v in arrays.items()]
    out = nc.dram_tensor("out", (SEQ, D), F32, kind="ExternalOutput").ap()
    hybrid_encoder(nc, *args, out)
    r = run_bass_kernel_spmd(nc, [arrays], core_ids=[0])
    return r.results[0]["out"].reshape(1, SEQ, D)
```
